# Optimizing a Trainium2 kernel written in Bass

```python
import math
import jax, jax.numpy as jnp
from jax import lax
import numpy as np

D_MODEL = 1024
BATCH = 1
SEQ = 512
DEPTH = 1

N_META = 16
BLOCK_Q = 128
RMS_EPS = 1e-6

FOX_HEADS = 8
FOX_HEAD_DIM = 64
FOX_WIDTH = FOX_HEADS * FOX_HEAD_DIM
FORGET_BIAS_INIT = 3.0

MLA_HEADS = 8
MLA_Q_RANK = 384
MLA_KV_RANK = 256
MLA_NOPE_DIM = 64
MLA_ROPE_DIM = 32
MLA_QK_DIM = MLA_NOPE_DIM + MLA_ROPE_DIM
MLA_V_DIM = 64
MLA_WIDTH = MLA_HEADS * MLA_V_DIM
ROPE_THETA = 10000.0

MIX_WIDTH = FOX_WIDTH + MLA_WIDTH

IN_SPLITS = [FOX_WIDTH, FOX_WIDTH, FOX_WIDTH, FOX_HEADS, MLA_Q_RANK, MLA_KV_RANK, MLA_ROPE_DIM]
IN_OFFSETS = [sum(IN_SPLITS[:i + 1]) for i in range(len(IN_SPLITS) - 1)]
IN_COLS = sum(IN_SPLITS)

N_GROUPS = 4
EXPERTS_PER_GROUP = 8
N_EXPERTS = N_GROUPS * EXPERTS_PER_GROUP
TOP_K = 2
D_EXPERT = 256

kernel_name = "hymba_fox_mla_hier_moe"

def rmsnorm(x, g):
    xf = x.astype(jnp.float32)
    y = xf * lax.rsqrt(jnp.mean(xf * xf, axis=-1, keepdims=True) + RMS_EPS)
    return (y * g.astype(jnp.float32)).astype(x.dtype)

def rope(x, pos):
    half = x.shape[-1] // 2
    inv_freq = jnp.exp(-math.log(ROPE_THETA) * jnp.arange(half, dtype=jnp.float32) / half)
    ang = pos[:, None] * inv_freq[None, :]
    cos = jnp.cos(ang)[None, :, None, :]
    sin = jnp.sin(ang)[None, :, None, :]
    xf = x.astype(jnp.float32)
    x1, x2 = xf[..., :half], xf[..., half:]
    return jnp.concatenate([x1 * cos - x2 * sin, x1 * sin + x2 * cos], axis=-1).astype(x.dtype)

def blocked_causal_attention(q, k, v, cum=None):
    L = q.shape[2]
    scale = 1.0 / math.sqrt(q.shape[-1])
    bounds = [0] + list(range(N_META, L + 1, BLOCK_Q))
    outs = []
    for s0, s1 in zip(bounds[:-1], bounds[1:]):
        qb = q[:, :, s0:s1]
        kb = k[:, :, :s1]
        vb = v[:, :, :s1]
        logits = jnp.einsum('bhqd,bhkd->bhqk', qb, kb).astype(jnp.float32) * scale
        if cum is not None:
            logits = logits + cum[:, :, s0:s1, None] - cum[:, :, None, :s1]
        causal = jnp.arange(s0, s1)[:, None] >= jnp.arange(s1)[None, :]
        logits = jnp.where(causal[None, None], logits, -jnp.inf)
        probs = jax.nn.softmax(logits, axis=-1).astype(v.dtype)
        outs.append(jnp.einsum('bhqk,bhkd->bhqd', probs, vb))
    return jnp.concatenate(outs, axis=2)

def to_heads(x, n_heads):
    B, L, W = x.shape
    return x.reshape(B, L, n_heads, W // n_heads).transpose(0, 2, 1, 3)

def from_heads(x):
    B, H, L, d = x.shape
    return x.transpose(0, 2, 1, 3).reshape(B, L, H * d)

def mixer_block(h, pos, g_attn, w_in, b_f, g_fox_q, g_fox_k, g_q_lat, w_uq, g_kv_lat, w_ukv,
                g_mla_q, g_mla_k, g_fox_out, g_mla_out, w_o):
    B, L, _ = h.shape
    u = rmsnorm(h, g_attn)
    proj = u @ w_in
    fq, fk, fv, ff, cq, ckv, kr = jnp.split(proj, IN_OFFSETS, axis=-1)

    fq = rmsnorm(to_heads(fq, FOX_HEADS), g_fox_q)
    fk = rmsnorm(to_heads(fk, FOX_HEADS), g_fox_k)
    fv = to_heads(fv, FOX_HEADS)
    log_f = jax.nn.log_sigmoid((ff + b_f).astype(jnp.float32))
    cum = jnp.cumsum(log_f.transpose(0, 2, 1), axis=-1)
    o_fox = from_heads(blocked_causal_attention(fq, fk, fv, cum))

    q = (rmsnorm(cq, g_q_lat) @ w_uq).reshape(B, L, MLA_HEADS, MLA_QK_DIM)
    kv = (rmsnorm(ckv, g_kv_lat) @ w_ukv).reshape(B, L, MLA_HEADS, MLA_NOPE_DIM + MLA_V_DIM)
    k_nope, mv = kv[..., :MLA_NOPE_DIM], kv[..., MLA_NOPE_DIM:]
    k_rope = jnp.broadcast_to(kr[:, :, None, :], (B, L, MLA_HEADS, MLA_ROPE_DIM))
    k = jnp.concatenate([k_nope, k_rope], axis=-1)
    q = rmsnorm(q, g_mla_q)
    k = rmsnorm(k, g_mla_k)
    q = jnp.concatenate([q[..., :MLA_NOPE_DIM], rope(q[..., MLA_NOPE_DIM:], pos)], axis=-1)
    k = jnp.concatenate([k[..., :MLA_NOPE_DIM], rope(k[..., MLA_NOPE_DIM:], pos)], axis=-1)
    o_mla = from_heads(blocked_causal_attention(q.transpose(0, 2, 1, 3), k.transpose(0, 2, 1, 3),
                                                mv.transpose(0, 2, 1, 3)))

    mix = jnp.concatenate([rmsnorm(o_fox, g_fox_out), rmsnorm(o_mla, g_mla_out)], axis=-1)
    return h + mix @ w_o

def hier_moe_block(h, g_ffn, w_group, b_group, w_expert, b_expert, w1, w3, w2):
    B, L, D = h.shape
    u = rmsnorm(h, g_ffn).reshape(B * L, D)
    group_logits = (u @ w_group + b_group).astype(jnp.float32)
    p_group = jax.nn.softmax(group_logits, axis=-1)
    g_idx = jnp.argmax(group_logits, axis=-1)
    p_sel = jnp.max(p_group, axis=-1, keepdims=True)
    exp_logits = (u @ w_expert + b_expert).astype(jnp.float32).reshape(-1, N_GROUPS, EXPERTS_PER_GROUP)
    within = jnp.einsum('tg,tge->te', jax.nn.one_hot(g_idx, N_GROUPS, dtype=jnp.float32), exp_logits)
    top_v, top_i = lax.top_k(within, TOP_K)
    w_sel = jax.nn.softmax(top_v, axis=-1) * p_sel
    e_idx = g_idx[:, None] * EXPERTS_PER_GROUP + top_i
    combine = jnp.sum(jax.nn.one_hot(e_idx, N_EXPERTS, dtype=jnp.float32) * w_sel[..., None], axis=1)
    combine = combine.astype(u.dtype)
    y = jnp.zeros_like(u)
    for e in range(N_EXPERTS):
        hid = jax.nn.silu(u @ w1[e]) * (u @ w3[e])
        y = y + combine[:, e:e + 1] * (hid @ w2[e])
    return h + y.reshape(B, L, D)

def setup_inputs(seed: int = 0) -> dict:
    key = jax.random.key(seed)
    ks = jax.random.split(key, 24)
    f32 = jnp.float32

    def nrm(k, shape, scale):
        return jax.random.normal(k, shape, f32) * scale

    def gain(k, shape):
        return 1.0 + 0.02 * jax.random.normal(k, shape, f32)

    return {
        "x": nrm(ks[0], (BATCH, SEQ, D_MODEL), 1.0),
        "meta_tokens": nrm(ks[1], (N_META, D_MODEL), 1.0),
        "g_attn": gain(ks[2], (DEPTH, D_MODEL)),
        "w_in": nrm(ks[3], (DEPTH, D_MODEL, IN_COLS), D_MODEL ** -0.5),
        "b_f": FORGET_BIAS_INIT + 0.1 * jax.random.normal(ks[4], (DEPTH, FOX_HEADS), f32),
        "g_fox_q": gain(ks[5], (DEPTH, FOX_HEAD_DIM)),
        "g_fox_k": gain(ks[6], (DEPTH, FOX_HEAD_DIM)),
        "g_q_lat": gain(ks[7], (DEPTH, MLA_Q_RANK)),
        "w_uq": nrm(ks[8], (DEPTH, MLA_Q_RANK, MLA_HEADS * MLA_QK_DIM), MLA_Q_RANK ** -0.5),
        "g_kv_lat": gain(ks[9], (DEPTH, MLA_KV_RANK)),
        "w_ukv": nrm(ks[10], (DEPTH, MLA_KV_RANK, MLA_HEADS * (MLA_NOPE_DIM + MLA_V_DIM)), MLA_KV_RANK ** -0.5),
        "g_mla_q": gain(ks[11], (DEPTH, MLA_QK_DIM)),
        "g_mla_k": gain(ks[12], (DEPTH, MLA_QK_DIM)),
        "g_fox_out": gain(ks[13], (DEPTH, FOX_WIDTH)),
        "g_mla_out": gain(ks[14], (DEPTH, MLA_WIDTH)),
        "w_o": nrm(ks[15], (DEPTH, MIX_WIDTH, D_MODEL), MIX_WIDTH ** -0.5),
        "g_ffn": gain(ks[16], (DEPTH, D_MODEL)),
        "w_group": nrm(ks[17], (DEPTH, D_MODEL, N_GROUPS), D_MODEL ** -0.5),
        "b_group": nrm(ks[18], (DEPTH, N_GROUPS), 0.01),
        "w_expert": nrm(ks[19], (DEPTH, D_MODEL, N_EXPERTS), D_MODEL ** -0.5),
        "b_expert": nrm(ks[20], (DEPTH, N_EXPERTS), 0.01),
        "w1": nrm(ks[21], (DEPTH, N_EXPERTS, D_MODEL, D_EXPERT), D_MODEL ** -0.5),
        "w3": nrm(ks[22], (DEPTH, N_EXPERTS, D_MODEL, D_EXPERT), D_MODEL ** -0.5),
        "w2": nrm(ks[23], (DEPTH, N_EXPERTS, D_EXPERT, D_MODEL), D_EXPERT ** -0.5),
    }

def reference(x, meta_tokens, g_attn, w_in, b_f, g_fox_q, g_fox_k, g_q_lat, w_uq, g_kv_lat, w_ukv,
              g_mla_q, g_mla_k, g_fox_out, g_mla_out, w_o, g_ffn, w_group, b_group, w_expert,
              b_expert, w1, w3, w2):
    B = x.shape[0]
    meta = jnp.broadcast_to(meta_tokens[None].astype(x.dtype), (B, N_META, x.shape[-1]))
    h = jnp.concatenate([meta, x], axis=1)
    pos = jnp.arange(h.shape[1], dtype=jnp.float32)
    for i in range(DEPTH):
        h = mixer_block(h, pos, g_attn[i], w_in[i], b_f[i], g_fox_q[i], g_fox_k[i], g_q_lat[i], w_uq[i],
                        g_kv_lat[i], w_ukv[i], g_mla_q[i], g_mla_k[i], g_fox_out[i], g_mla_out[i], w_o[i])
        h = hier_moe_block(h, g_ffn[i], w_group[i], b_group[i], w_expert[i], b_expert[i],
                           w1[i], w3[i], w2[i])
    return h[:, N_META:]


_drawn_inputs = setup_inputs


def setup_inputs(seed=0):
    import zlib

    import numpy as np

    out = dict(_drawn_inputs(seed))
    spreads = {}
    factors = {'g_fox_q': 2.904,
     'g_fox_k': 3.538,
     'g_q_lat': 3.333,
     'g_kv_lat': 2.785,
     'g_mla_q': 3.109,
     'g_mla_k': 3.626,
     'g_fox_out': 2.803,
     'g_mla_out': 3.446,
     'g_ffn': 3.317,
     'b_group': 6.445,
     'b_expert': 4.269}
    for name, (base, spread) in spreads.items():
        noise = np.random.default_rng([zlib.crc32(name.encode()), seed]).standard_normal(out[name].shape)
        drawn = base * np.exp(spread * noise) if base else spread * noise
        out[name] = __import__('jax').numpy.asarray(drawn.astype(out[name].dtype))
    for name, factor in factors.items():
        out[name] = (out[name] * factor).astype(out[name].dtype)
    return out
```

```python
from contextlib import ExitStack

import concourse.bass as bass
from concourse import mybir

F32 = mybir.dt.float32
BF16 = mybir.dt.bfloat16
I32 = mybir.dt.int32
U32 = mybir.dt.uint32
ALU = mybir.AluOpType
ACT = mybir.ActivationFunctionType
X = mybir.AxisListType.X

P = 128
EPS = 1e-6
NEG = -1e30
ARENA = 16512

D = 1024
SEQ = 512
META = 16
L = SEQ + META
NT = SEQ // P
MT = NT
TOKEN_TILES = [MT] + list(range(NT))
DK = D // P

H = 8
HD = 64
FOX = H * HD
FOX_AUG = HD + 2
QR = 384
KVR = 256
ROPE = 32
HALF = ROPE // 2
NOPE = 64
MQK = NOPE + ROPE
MLA = H * HD
QRK = QR // P
KVRK = KVR // P
QUP = H * MQK
KVUP = H * (NOPE + HD)
IN_COLS = 3 * FOX + H + QR + KVR + ROPE

NG = 4
EPG = 8
NE = NG * EPG
F = 256
FK = F // P
SLOTS = 64
RING = 4
ROUTE = NG + NE

BLOCKS = {
    "ffcq": (3 * FOX, H + QR),
    "v": (2 * FOX, FOX),
    "k": (FOX, FOX),
    "q": (0, FOX),
    "ckv": (3 * FOX + H + QR, KVR + ROPE),
}
BLOCK_ORDER = ["ffcq", "v", "k", "q", "ckv"]


def rows(t):
    return META if t == MT else P


def cols(t):
    return slice(t * P, t * P + rows(t))


def projection_plan():
    units = [(b, t) for b in BLOCK_ORDER for t in TOKEN_TILES if not (b == "q" and t == MT)]
    turned = lambda u: u[0] in ("k", "q", "ckv") or (u[0] == "ffcq" and u[1] != MT)
    steps = [("turn", ("x", t)) for t in TOKEN_TILES]
    for n, u in enumerate(units):
        steps.append(("project", u))
        if n >= 1 and turned(units[n - 1]):
            steps.append(("turn", units[n - 1]))
        if u == ("v", NT - 1):
            steps.append(("turn", ("cum", 0)))
    steps.append(("turn", units[-1]))
    turns = [u for what, u in steps if what == "turn"]
    return units, steps, turns


def build(nc, a, out, slots=SLOTS):
    units, steps, turns = projection_plan()
    unit_no = {u: n for n, u in enumerate(units)}
    turn_no = {u: n for n, u in enumerate(turns)}
    by_act = lambda u: u[0] in ("k", "q")
    staged = [u for u in turns if u[0] not in ("x", "cum")]
    stage_no = {u: n for n, u in enumerate(staged)}
    headed = [u for u in units if u[0] in ("k", "q")]
    head_no = {u: n for n, u in enumerate(headed)}
    rooted = [("x", t) for t in TOKEN_TILES] + [u for u in units if u in headed or u in staged]
    root_no = {u: n for n, u in enumerate(rooted)}

    up_units = [("kv", t) for t in TOKEN_TILES] + [("uq", t) for t in range(NT)]
    NU = len(up_units)
    UNITS = H * NT
    heads = [(ph, h, i) for ph in range(2) for h in range(H) for i in range(NT)]

    with ExitStack() as ctx:
        sem_names = {}

        def sem(name):
            sem_names[name] = ctx.enter_context(nc.semaphore(name))
            return sem_names[name]

        end = [ARENA]

        def place(name, shape, dt, offset):
            return nc.alloc_sbuf_tensor_at(name, shape, dt, offset=offset)

        def region(size):
            start = end[0]
            end[0] = start + (size + 31) // 32 * 32
            return start

        def new(name, shape, dt=F32):
            n = 1
            for s in shape[1:]:
                n *= s
            return place(name, shape, dt, region(n * (2 if dt == BF16 else 4)))

        SLOT = (2 * DK * F + FK * D) * 4
        ring = region(RING * SLOT)
        w13 = [place(f"w13_{s}", [P, 2, DK, F], F32, ring + s * SLOT) for s in range(RING)]
        w2s = [place(f"w2_{s}", [P, FK, D], F32, ring + s * SLOT + 2 * DK * F * 4) for s in range(RING)]
        w_in = place("w_in", [P, DK, IN_COLS], F32, ring)
        w_uq = place("w_uq", [P, QRK, QUP], F32, ring + 3 * SLOT)
        w_ukv = place("w_ukv", [P, KVRK, KVUP], F32, ring + 3 * SLOT + QRK * QUP * 4)
        WO_A = 6
        w_oa = place("w_oa", [P, WO_A, D], F32, ring + 2 * SLOT)

        x = new("x", [P, NT, D])
        r_qk = region((NT * P + L) * H * 4)
        xm = place("xm", [META, D], F32, r_qk)
        qT = place("qT", [MQK, H, SEQ], F32, r_qk)
        kT = place("kT", [MQK, H, L], F32, r_qk + H * SEQ * 4)
        mixn = place("mixn", [P, DK, P], F32, r_qk)
        mixT = place("mixT", [P, DK, P], F32, r_qk + 4096)
        u2n = [place(f"u2n{b}", [P, DK, P], F32, r_qk + 8192 + 4096 * b) for b in range(2)]
        u2T = place("u2T", [P, DK, P], F32, r_qk + 16384)
        xg = [place(f"xg{b}", [slots, DK, P], F32, r_qk + 20480 + 4096 * b) for b in range(2)]
        yg = [place(f"yg{b}", [P, D], F32, r_qk + 4096 * b) for b in range(4)]

        r_v = region((NT + 1) * FOX * 4)
        vals = place("vals", [P, NT + 1, FOX], F32, r_v)
        xt = [place(f"xt{b}", [P, DK, slots], F32, r_v + 2048 * b) for b in range(2)]
        sil = [place(f"sil{b}", [P, FK, slots], F32, r_v + 4096 + 512 * b) for b in range(2)]
        hT = [place(f"hT{b}", [P, FK, slots], F32, r_v + 5120 + 512 * b) for b in range(2)]

        r_u = region(DK * L * 4)
        uT = place("uT", [P, DK, L], F32, r_u)
        o_all = place("o_all", [P, NT, D], F32, r_u)
        ysb = [place(f"ysb{b}", [slots, D], F32, r_u + 4096 * b) for b in range(2)]

        r_l = region((QRK * SEQ + KVRK * L) * 4)
        cqT = place("cqT", [P, QRK, SEQ], F32, r_l)
        ckvT = place("ckvT", [P, KVRK, L], F32, r_l + QRK * SEQ * 4)
        w_ob = place("w_ob", [P, DK - WO_A, D], F32, r_l)

        r_p = region(9344)
        xs = [place(f"xs{b}", [P, DK, P], F32, r_p + 4096 * b) for b in range(2)]
        sq = [place(f"sq{b}", [P, QUP], F32, r_p + 3072 * b) for b in range(2)]
        rope_g = place("rope_g", [P, H, ROPE], F32, r_p + 6144)
        rope_t = place("rope_t", [P, 4, H, HALF], F32, r_p + 7168)
        probs = [place(f"probs{b}", [P, L], F32, r_p + L * 4 * b) for b in range(2)]
        pT = [place(f"pT{b}", [P, NT + 1, P], F32, r_p + 2 * L * 4 + (NT + 1) * P * 4 * b) for b in range(2)]

        r_s = region(2 * QUP * 4)
        st_fox = [place(f"st_fox{b}", [P, H, FOX_AUG], F32, r_s + QUP * 4 * b) for b in range(2)]
        st_lat = [place(f"st_lat{b}", [P, QRK, P], F32, r_s + QUP * 4 * b) for b in range(2)]
        st_mla = [place(f"st_mla{b}", [P, H, MQK], F32, r_s + QUP * 4 * b) for b in range(2)]

        krg = place("krg", [P, NT + 1, ROPE], F32, r_s)
        krt = place("krt", [P, 4, NT + 1, HALF], F32, r_s + (NT + 1) * ROPE * 4)

        ident = new("ident", [P, P])
        tri = new("tri", [P, P])
        ones = new("ones", [P, P])
        causal = new("causal", [P, P], BF16)
        identb = new("identb", [P, P], BF16)
        before = new("before", [P, P], BF16)
        onesb = new("onesb", [P, P], BF16)
        rope_cs = new("rope_cs", [P, NT + 1, ROPE])
        g_attn = new("g_attn_c", [P, DK])
        g_ffn = new("g_ffn_c", [P, DK])
        g_mix = new("g_mix_c", [P, DK])
        g_ql = new("g_ql_c", [P, QRK])
        g_kvl = new("g_kvl_c", [P, KVRK])
        gc_fox = [new("gc_foxq", [FOX_AUG, 1]), new("gc_foxk", [FOX_AUG, 1])]
        gc_mla = [new("gc_mlaq", [MQK, 1]), new("gc_mlak", [MQK, 1])]
        gr_q = new("gr_q", [P, ROPE])
        gr_k = new("gr_k", [P, ROPE])
        bf_b = new("bf_b", [P, H])
        ff = new("ff", [P, NT + 1, H])
        ff_e = new("ff_e", [P, NT + 1, H])
        logf = new("logf", [P, NT + 1, H])
        cum = new("cum", [P, NT + 1, H])
        kr = new("kr", [P, NT + 1, ROPE])
        krr = new("krr", [P, NT + 1, ROPE])
        kr_ss = new("kr_ss", [P, NT + 1])
        ss = [new(f"ss{b}", [P, H]) for b in range(2)]
        root = [new(f"root{b}", [P, H]) for b in range(2)]
        rinv = [new(f"rinv{b}", [P, H]) for b in range(2)]
        nmax = [new(f"nmax{b}", [P, 1]) for b in range(2)]
        psums = [new(f"psums{b}", [P, 1]) for b in range(2)]
        prinv = [new(f"prinv{b}", [P, 1]) for b in range(2)]
        junk = new("junk", [P, ROPE])
        w_route = new("w_route", [P, DK, ROUTE])
        b_route = new("b_route", [P, ROUTE])
        lg = new("lg", [P, NG + 4 + NE])
        gtop = new("gtop", [P, 8])
        gidx = new("gidx", [P, 8], U32)
        gf = new("gf", [P, 2])
        ghot = new("ghot", [P, NG])
        gprod = new("gprod", [P, EPG, NG])
        within = new("within", [P, EPG])
        etop = new("etop", [P, 8])
        eidx = new("eidx", [P, 8], U32)
        esel = new("esel", [P, 2])
        ehot = new("ehot", [P, 2, NE])
        ehots = new("ehots", [P, NT, 2, NE])
        picks = new("picks", [P, NT, NE], BF16)
        rprod = new("rprod", [P, 2, NE])
        ranks_all = new("ranks_all", [P, NT, 2])
        late = new("late", [P, 2, NT, 2])
        esels = new("esels", [P, NT, 2])
        wt = new("wt", [P, 8])
        gexp = new("gexp", [P, NG])
        coef = new("coef", [P, NT, 2])
        pos_t = new("pos_t", [P, NT, 2], I32)
        pos_y = new("pos_y", [P, NT, 2], I32)
        tok = new("tok", [P, NT], I32)
        iota_i = new("iota_i", [P, NE], I32)
        iota_f = new("iota_f", [P, NE])
        zero_i = new("zero_i", [P, P], I32)
        idx = new("idx", [slots, NE], I32)
        fb_idx = new("fb_idx", [slots, 1], I32)
        most = new("most", [P, 1])
        eps_c = new("eps_c", [P, 1])
        over = new("over", [P, 1], I32)
        assert end[0] <= 229344, end[0]

        ps = ctx.enter_context(nc.psum_tensor("ps", [P, 8, 512], F32))

        def pair(b, n):
            return ps[:, b:b + 2, :].rearrange("p a n -> p (a n)")[:, 0:n]

        u2_rows = nc.dram_tensor("u2_rows", [SEQ, D], F32).ap()
        table = nc.dram_tensor("table", [SEQ * NE, 1], I32).ap()
        MAIN = NE * slots
        REST = SEQ - slots
        y_rows = nc.dram_tensor("y_rows", [MAIN + NE * REST, D], F32).ap()

        consts_in, masks_made, vecs_made = sem("consts_in"), sem("masks_made"), sem("vecs_made")
        eps_made, dve_gf = sem("eps_made"), sem("dve_gf")
        x_in = [sem(f"x_in{t}") for t in range(NT + 1)]
        win_in = {b: sem(f"win_in_{b}") for b in BLOCK_ORDER}
        wup_in, wo_in, route_in = sem("wup_in"), sem("wo_in"), sem("route_in")
        act_step, dve_step, pool_step = sem("act_step"), sem("dve_step"), sem("pool_step")
        roots_made, xs_made = sem("roots_made"), sem("xs_made")
        projected, v_copied, unit_freed = sem("projected"), sem("v_copied"), sem("unit_freed")
        squares_made, sums_made, staged_done = sem("squares_made"), sem("sums_made"), sem("staged_done")
        turned, turn_act, turn_dve = sem("turned"), sem("turn_act"), sem("turn_dve")
        ff_in, ff_abs, ff_log, ff_exp, logf_made = (sem("ff_in"), sem("ff_abs"), sem("ff_log"), sem("ff_exp"),
                                                    sem("logf_made"))
        up_done, up_squares, up_sums, up_roots = sem("up_done"), sem("up_squares"), sem("up_sums"), sem("up_roots")
        up_vals, up_staged, up_turned, up_out = sem("up_vals"), sem("up_staged"), sem("up_turned"), sem("up_out")
        scored, maxed, exped = sem("scored"), sem("maxed"), sem("exped")
        pm_turned, p_turned, pm_copied, p_copied = (sem("pm_turned"), sem("p_turned"), sem("pm_copied"),
                                                    sem("p_copied"))
        pv_done, sums_inv, o_done = sem("pv_done"), sem("sums_inv"), sem("o_done")
        mix_roots, mix_inv, mix_made, mix_turned, mix_out = (sem("mix_roots"), sem("mix_inv"), sem("mix_made"),
                                                    sem("mix_turned"), sem("mix_out"))
        wo_done, h_made, h_roots, h_inv, u2_made = (sem("wo_done"), sem("h_made"), sem("h_roots"), sem("h_inv"),
                                                    sem("u2_made"))
        u2_stored = [sem(f"u2_stored{b}") for b in range(2)]
        u2_turned, u2_out, logits_done = sem("u2_turned"), sem("u2_out"), sem("logits_done")
        gmax_made, gexp_made, gap_made, gap_exp = (sem("gmax_made"), sem("gexp_made"), sem("gap_made"),
                                                   sem("gap_exp"))
        picks_made, ranked, pos_made, counted, over_made = (sem("picks_made"), sem("ranked"), sem("pos_made"),
                                                            sem("counted"), sem("over_made"))
        table_zeroed, table_filled, idx_in = sem("table_zeroed"), sem("table_filled"), sem("idx_in")
        w13_in = [sem(f"w13_in{s}") for s in range(RING)]
        w2_in = [sem(f"w2_in{s}") for s in range(RING)]
        xg_in = [sem(f"xg_in{b}") for b in range(2)]
        waits_ended = sem("waits_ended")
        xt_done, xt_out, h13_done, silu_done, hT_made = (sem("xt_done"), sem("xt_out"), sem("h13_done"),
                                                         sem("silu_done"), sem("hT_made"))
        y_done, y_copied = sem("y_done"), sem("y_copied")
        y_stored = [sem(f"y_stored{b}") for b in range(2)]
        fb_w, fb_idx_in, fb_xg, fb_xt, fb_xt_out, fb_h13, fb_silu, fb_hT, fb_y, fb_y_out, fb_stored = (
            sem(n) for n in ("fb_w", "fb_idx_in", "fb_xg", "fb_xt", "fb_xt_out", "fb_h13", "fb_silu", "fb_hT",
                             "fb_y", "fb_y_out", "fb_stored"))
        fb_pos, fb_blank, fb_zeroed = sem("fb_pos"), sem("fb_blank"), sem("fb_zeroed")
        yg_in = [sem(f"yg_in{b}") for b in range(4)]
        yg_used, out_made, out_stored = sem("yg_used"), sem("out_made"), sem("out_stored")

        x_tiles = a["x"][0].rearrange("(t p) d -> t p d", p=P)
        w_in_v = a["w_in"][0].rearrange("(p k) n -> p k n", k=DK)
        w_o_v = a["w_o"][0].rearrange("(g p k) n -> g p k n", g=2, k=DK // 2)
        w1_v = a["w1"][0].rearrange("e (p k) f -> e p k f", k=DK)
        w3_v = a["w3"][0].rearrange("e (p k) f -> e p k f", k=DK)
        w2_v = a["w2"][0].rearrange("e (m p) n -> e p m n", p=P)
        y_main = y_rows[0:MAIN, :].rearrange("(e r) d -> e r d", r=slots)
        y_over = y_rows[MAIN:, :].rearrange("(e r) d -> e r d", r=REST)
        y_over_tiles = y_rows[MAIN:, :].rearrange("(n p) d -> n p d", p=P)
        table_by_rank = table.rearrange("(r e) o -> r (e o)", e=NE)
        out_tiles = out[0].rearrange("(t p) d -> t p d", p=P)

        def wo_chunk(c):
            return w_oa[:, c, :] if c < WO_A else w_ob[:, c - WO_A, :]

        def unit_cols(i):
            n = P * (i + 1)
            return SEQ - n, SEQ, L

        def stepper(eng, signal):
            count = [0]

            def step(instruction):
                count[0] += 1
                instruction.then_inc(signal, 1)
                eng.wait_ge(signal, count[0])

            return step

        def turn_freed(eng, n):
            if n < 2:
                return
            u = turns[n - 2]
            if by_act(u):
                eng.wait_ge(turn_act, sum(by_act(v) for v in turns[:n - 1]))
            else:
                eng.wait_ge(turn_dve, sum(not by_act(v) for v in turns[:n - 1]))

        def unit_emptied(eng, n):
            of_act = lambda u: u[0] == "v"
            if of_act(units[n]):
                eng.wait_ge(v_copied, sum(of_act(u) for u in units[:n + 1]))
            else:
                eng.wait_ge(unit_freed, sum(not of_act(u) for u in units[:n + 1]))

        block = ctx.enter_context(nc.Block())

        CONSTS = 16

        @block.sync
        def _(sp):
            sp.dma_start(xm[:, :], a["meta_tokens"]).then_inc(x_in[MT], 16)
            for t in range(NT):
                sp.dma_start(x[:, t, :], x_tiles[t]).then_inc(x_in[t], 16)
            for b in BLOCK_ORDER:
                c0, n = BLOCKS[b]
                sp.dma_start(w_in[:, :, c0:c0 + n], w_in_v[:, :, c0:c0 + n]).then_inc(win_in[b], 16)
            sp.dma_start(w_uq[:, :, :], a["w_uq"][0].rearrange("(p k) n -> p k n", k=QRK)).then_inc(wup_in, 16)
            sp.dma_start(w_ukv[:, :, :], a["w_ukv"][0].rearrange("(p k) n -> p k n", k=KVRK)).then_inc(wup_in, 16)
            with nc.allow_non_contiguous_dma("router weights, 36 columns"):
                sp.dma_start(w_route[:, :, 0:NG], a["w_group"][0].rearrange("(p k) n -> p k n", k=DK)
                             ).then_inc(route_in, 16)
                sp.dma_start(w_route[:, :, NG:], a["w_expert"][0].rearrange("(p k) n -> p k n", k=DK)
                             ).then_inc(route_in, 16)

            def load_expert(s, e):
                sp.dma_start(w13[s][:, 0, :, :], w1_v[e]).then_inc(w13_in[s], 16)
                sp.dma_start(w13[s][:, 1, :, :], w3_v[e]).then_inc(w13_in[s], 16)
                sp.dma_start(w2s[s][:, :, :], w2_v[e]).then_inc(w2_in[s], 16)

            sp.wait_ge(projected, len(units))
            load_expert(0, 0)
            load_expert(1, 1)
            sp.dma_start(w_oa[:, 0:4, :], w_o_v[0]).then_inc(wo_in, 16)
            sp.dma_start(w_oa[:, 4:6, :], w_o_v[1][:, 0:2, :]).then_inc(wo_in, 16)
            sp.wait_ge(up_done, NU)
            sp.dma_start(w_ob[:, :, :], w_o_v[1][:, 2:4, :]).then_inc(wo_in, 16)
            load_expert(3, 3)
            sp.wait_ge(wo_done, NT)
            load_expert(2, 2)

            with sp.Fori(1, NE // RING) as it:
                for s in range(RING):
                    sp.wait_ge(y_done, it * RING + (s - RING + 1))
                    load_expert(s, it * RING + s)

            sp.wait_ge(over_made, 1)
            tripped = sp.value_load(over[0:1, 0:1], min_val=0, max_val=1)
            with sp.If(tripped > 0):
                sp.wait_ge(y_done, NE)
                with sp.Fori(0, NE) as e:
                    with sp.Fori(1, SEQ // slots) as c:
                        n = e * (SEQ // slots - 1) + c
                        sp.dma_start(w13[0][:, 0, :, :], w1_v[e]).then_inc(fb_w, 16)
                        sp.dma_start(w13[0][:, 1, :, :], w3_v[e]).then_inc(fb_w, 16)
                        sp.dma_start(w2s[0][:, :, :], w2_v[e]).then_inc(fb_w, 16)
                        sp.wait_ge(fb_stored, n * 16)
                        sp.sem_inc(waits_ended, 1)

            for t in range(NT):
                sp.wait_ge(out_made, t + 1)
                sp.dma_start(out_tiles[t], x[:, t, :]).then_inc(out_stored, 16)
            sp.wait_ge(out_stored, NT * 16)

        @block.gpsimd
        def _(pool):
            step = stepper(pool, pool_step)
            step(pool.memset(ident[:, :], 0.0))
            pool.affine_select(out=ident[:, :], in_=ident[:, :], compare_op=ALU.not_equal, fill=1.0, base=0,
                               pattern=[[-1, P]], channel_multiplier=1).then_inc(masks_made, 1)
            step(pool.memset(identb[:, :], 0.0))
            pool.affine_select(out=identb[:, :], in_=identb[:, :], compare_op=ALU.not_equal, fill=1.0, base=0,
                               pattern=[[-1, P]], channel_multiplier=1).then_inc(masks_made, 1)
            step(pool.memset(causal[:, :], 0.0))
            pool.affine_select(out=causal[:, :], in_=causal[:, :], compare_op=ALU.is_ge, fill=NEG, base=0,
                               pattern=[[-1, P]], channel_multiplier=1).then_inc(masks_made, 1)
            step(pool.memset(tri[:, :], 1.0))
            pool.affine_select(out=tri[:, :], in_=tri[:, :], compare_op=ALU.is_ge, fill=0.0, base=0,
                               pattern=[[1, P]], channel_multiplier=-1).then_inc(masks_made, 1)
            step(pool.memset(before[:, :], 1.0))
            pool.affine_select(out=before[:, :], in_=before[:, :], compare_op=ALU.is_ge, fill=0.0, base=-1,
                               pattern=[[1, P]], channel_multiplier=-1).then_inc(masks_made, 1)
            pool.memset(ones[:, :], 1.0).then_inc(masks_made, 1)
            pool.memset(onesb[:, :], 1.0).then_inc(masks_made, 1)
            pool.iota(tok[:, :], pattern=[[P, NT]], base=0, channel_multiplier=1).then_inc(masks_made, 1)
            step(pool.iota(iota_i[:, :], pattern=[[1, NE]], base=0, channel_multiplier=0))
            pool.tensor_copy(iota_f[:, :], iota_i[:, :]).then_inc(masks_made, 1)
            step(pool.memset(zero_i[:, :], 0))
            pool.dma_start(table.rearrange("(p n) o -> p (n o)", p=P), zero_i[:, :]).then_inc(table_zeroed, 16)

            pool.wait_ge(table_zeroed, 16)
            for t in range(NT):
                pool.wait_ge(pos_made, t + 1)
                for k in range(2):
                    pool.indirect_dma_start(
                        out=table, out_offset=bass.IndirectOffsetOnAxis(ap=pos_t[:, t, k:k + 1].bitcast(U32), axis=0),
                        in_=tok[:, t:t + 1], in_offset=None).then_inc(table_filled, 16)
            pool.wait_ge(table_filled, 2 * NT * 16)
            pool.dma_start(idx[:, :], table_by_rank[0:slots, :]).then_inc(idx_in, 16)
            pool.wait_ge(idx_in, 16)
            for b in range(2):
                pool.wait_ge(u2_stored[b], 16 * NT // 2)

            for e in range(NE):
                if e >= 2:
                    pool.wait_ge(xt_done, e - 1)
                pool.indirect_dma_start(
                    out=xg[e % 2][:, :, :].rearrange("p k n -> p (k n)"), out_offset=None, in_=u2_rows,
                    in_offset=bass.IndirectOffsetOnAxis(ap=idx[:, e:e + 1].bitcast(U32), axis=0)
                ).then_inc(xg_in[e % 2], 16)

            def fetch_outputs(source):
                for b in range(2):
                    pool.wait_ge(y_stored[b], 16 * NE // 2)
                for t in range(NT):
                    for k in range(2):
                        n = 2 * t + k
                        if n >= 4:
                            pool.wait_ge(yg_used, n - 3)
                        pool.indirect_dma_start(
                            out=yg[n % 4][:, :], out_offset=None, in_=source,
                            in_offset=bass.IndirectOffsetOnAxis(ap=pos_y[:, t, k:k + 1].bitcast(U32), axis=0)
                        ).then_inc(yg_in[n % 4], 16)

            pool.wait_ge(over_made, 1)
            tripped = pool.value_load(over[0:1, 0:1], min_val=0, max_val=1)
            with pool.If(tripped > 0):
                pool.wait_ge(xt_done, NE)
                pool.memset(yg[0][:, :], 0.0).then_inc(fb_blank, 1)
                pool.wait_ge(fb_blank, 1)
                with pool.Fori(0, NE * REST // P) as n:
                    pool.dma_start(y_over_tiles[n, :, :], yg[0][:, :]).then_inc(fb_zeroed, 16)
                    pool.wait_ge(fb_zeroed, n * 16 + 16)
                with pool.Fori(0, NE) as e:
                    with pool.Fori(1, SEQ // slots) as c:
                        n = e * (SEQ // slots - 1) + c
                        with nc.allow_non_contiguous_dma("one expert's tokens"):
                            pool.dma_start(fb_idx[:, :], table_by_rank[bass.ds(c * slots, slots), bass.ds(e, 1)]
                                           ).then_inc(fb_idx_in, 16)
                        pool.wait_ge(fb_idx_in, n * 16)
                        pool.sem_inc(waits_ended, 1)
                        pool.indirect_dma_start(
                            out=xg[0][:, :, :].rearrange("p k n -> p (k n)"), out_offset=None, in_=u2_rows,
                            in_offset=bass.IndirectOffsetOnAxis(ap=fb_idx[:, :].bitcast(U32), axis=0)
                        ).then_inc(fb_xg, 16)
                        pool.wait_ge(fb_stored, n * 16)
                pool.wait_ge(fb_pos, 1)
                fetch_outputs(y_rows)
            with pool.Else():
                fetch_outputs(y_rows[0:MAIN, :])

        @block.scalar
        def _(act):
            step = stepper(act, act_step)
            with nc.allow_non_contiguous_dma("small vectors"):
                def const(dst, src):
                    act.dma_start(dst, src).then_inc(consts_in, 16)
                const(g_attn[:, :], a["g_attn"][0].rearrange("(p k) -> p k", k=DK))
                const(g_ql[:, :], a["g_q_lat"][0].rearrange("(p k) -> p k", k=QRK))
                const(g_kvl[:, :], a["g_kv_lat"][0].rearrange("(p k) -> p k", k=KVRK))
                const(bf_b[:, :], a["b_f"][0].partition_broadcast(P))
                const(gc_fox[0][0:HD, :], a["g_fox_q"][0].rearrange("(p o) -> p o", o=1))
                const(gc_fox[1][0:HD, :], a["g_fox_k"][0].rearrange("(p o) -> p o", o=1))
                const(gc_mla[0][0:NOPE, :], a["g_mla_q"][0][0:NOPE].rearrange("(p o) -> p o", o=1))
                const(gc_mla[1][0:NOPE, :], a["g_mla_k"][0][0:NOPE].rearrange("(p o) -> p o", o=1))
                const(gr_q[:, :], a["g_mla_q"][0][NOPE:MQK].partition_broadcast(P))
                const(gr_k[:, :], a["g_mla_k"][0][NOPE:MQK].partition_broadcast(P))
                const(g_mix[:, 0:DK // 2], a["g_fox_out"][0].rearrange("(p k) -> p k", k=DK // 2))
                const(g_mix[:, DK // 2:], a["g_mla_out"][0].rearrange("(p k) -> p k", k=DK // 2))
                const(g_ffn[:, :], a["g_ffn"][0].rearrange("(p k) -> p k", k=DK))
                const(b_route[:, 0:NG], a["b_group"][0].partition_broadcast(P))
                const(b_route[:, NG:], a["b_expert"][0].partition_broadcast(P))
                const(rope_cs[:, :, :], a["rope"].rearrange("(t p) c -> p t c", p=P))
            act.wait_ge(eps_made, 1)
            for j, t in enumerate(TOKEN_TILES):
                r = rows(t)
                src = xm[:, :] if t == MT else x[:, t, :]
                act.wait_ge(x_in[t], 16)
                if j >= 2:
                    act.wait_ge(turned, j - 1)
                step(act.activation(xs[j % 2][0:r, :, :].rearrange("p k n -> p (k n)"), src, ACT.Square,
                                    accum_out=ss[j % 2][0:r, 0:1]))
                act.activation(root[j % 2][0:r, 0:1], ss[j % 2][0:r, 0:1], ACT.Sqrt, scale=1.0 / D,
                               bias=eps_c[0:r, :]).then_inc(roots_made, 1)

            def empty_turn(u):
                n = turn_no[u]
                t = u[1]
                r = rows(t)
                act.wait_ge(turned, n + 1)
                src = pair(4 + 2 * (n % 2), H * r)[0:FOX_AUG, :].rearrange("p (h c) -> p h c", h=H)
                if u == ("k", MT):
                    act.wait_ge(vecs_made, 1)
                which = 0 if u[0] == "q" else 1
                dst = (qT if u[0] == "q" else kT)[0:FOX_AUG, :, cols(t)]
                act.activation(dst, src, ACT.Copy, scale=gc_fox[which][:, :]).then_inc(turn_act, 1)

            for n, u in enumerate(units):
                b, t = u
                r = rows(t)
                bank = ps[0:r, n % 4, :]
                act.wait_ge(projected, n + 1)
                if b == "v":
                    act.activation(vals[0:r, t, :], bank, ACT.Copy).then_inc(v_copied, 1)
                elif b in ("k", "q"):
                    m = head_no[u]
                    if m >= 2:
                        act.wait_ge(sums_made, m - 1)
                    act.activation(sq[m % 2][0:r, 0:FOX], bank, ACT.Square).then_inc(squares_made, 1)
                    act.wait_ge(sums_made, m + 1)
                    k = root_no[u]
                    act.activation(root[k % 2][0:r, :], ss[k % 2][0:r, :], ACT.Sqrt, scale=1.0 / HD,
                                   bias=eps_c[0:r, :]).then_inc(roots_made, 1)
                elif b == "ckv" or t != MT:
                    k = root_no[u]
                    w, c0 = (KVR, 0) if b == "ckv" else (QR, H)
                    if b == "ckv":
                        step(act.activation(junk[0:r, :], bank[:, KVR:KVR + ROPE], ACT.Square,
                                            accum_out=kr_ss[0:r, t:t + 1]))
                    step(act.activation(sq[k % 2][0:r, 0:w], bank[:, c0:c0 + w], ACT.Square,
                                        accum_out=ss[k % 2][0:r, 0:1]))
                    act.activation(root[k % 2][0:r, 0:1], ss[k % 2][0:r, 0:1], ACT.Sqrt, scale=1.0 / w,
                                   bias=eps_c[0:r, :]).then_inc(roots_made, 1)
                if u == ("ffcq", NT - 1):
                    act.wait_ge(ff_in, 1)
                    act.activation(ff_e[:, :, :], ff[:, :, :], ACT.Abs).then_inc(ff_abs, 1)
                    act.wait_ge(ff_abs, 1)
                    act.activation(ff_e[:, :, :], ff_e[:, :, :], ACT.Exp, scale=-1.0).then_inc(ff_exp, 1)
                    act.wait_ge(ff_exp, 1)
                    act.activation(ff_e[:, :, :], ff_e[:, :, :], ACT.Ln, bias=1.0).then_inc(ff_log, 1)
                if n >= 2 and by_act(units[n - 2]):
                    empty_turn(units[n - 2])
            for u in units[-2:]:
                if by_act(u):
                    empty_turn(u)

            def attend(ph):
                g0 = ph * UNITS

                def exp(g):
                    i = g % NT
                    c0, _, c2 = unit_cols(i)
                    act.wait_ge(maxed, g + 1)
                    act.activation(probs[g % 2][:, c0:c2], pair(2 * (g % 2), L)[:, c0:c2], ACT.Exp,
                                   bias=nmax[g % 2][:, :], accum_out=psums[g % 2][:, :]).then_inc(exped, 1)

                exp(g0)
                exp(g0 + 1)
                for g in range(g0, g0 + UNITS):
                    h, i = g % UNITS // NT, g % NT
                    act.wait_ge(pm_turned, g + 1)
                    if g >= 2:
                        act.wait_ge(pv_done, g - 1)
                    act.activation(pT[g % 2][0:META, NT, :], ps[0:META, 6 + g % 2, 0:P], ACT.Copy
                                   ).then_inc(pm_copied, 1)
                    act.wait_ge(pv_done, g + 1)
                    act.wait_ge(sums_inv, g + 1)
                    c = ph * FOX + h * HD
                    act.activation(o_all[:, i, c:c + HD], ps[:, 6 + g % 2, P:P + HD], ACT.Copy,
                                   scale=prinv[g % 2][:, :]).then_inc(o_done, 1)
                    if g + 2 < g0 + UNITS:
                        exp(g + 2)

            attend(0)

            def empty_up(n):
                kind, t = up_units[n]
                r = rows(t)
                act.wait_ge(up_turned, n + 1)
                src = pair(4 + 2 * (n % 2), H * r)[0:MQK, :].rearrange("p (h c) -> p h c", h=H)
                which = 0 if kind == "uq" else 1
                dst = (qT if kind == "uq" else kT)[:, :, cols(t)]
                act.activation(dst, src, ACT.Copy, scale=gc_mla[which][:, :]).then_inc(up_out, 1)

            for n, (kind, t) in enumerate(up_units):
                r = rows(t)
                b0 = 2 * (n % 2)
                act.wait_ge(up_done, n + 1)
                if n >= 2:
                    act.wait_ge(up_sums, n - 1)
                if kind == "kv":
                    kv = pair(b0, KVUP)[0:r, :].rearrange("p (h c) -> p h c", h=H)
                    act.activation(sq[n % 2][0:r, 0:H * NOPE].rearrange("p (h c) -> p h c", h=H),
                                   kv[:, :, 0:NOPE], ACT.Square).then_inc(up_squares, 1)
                    act.activation(vals[0:r, t, :].rearrange("p (h c) -> p h c", h=H), kv[:, :, NOPE:],
                                   ACT.Copy).then_inc(up_vals, 1)
                else:
                    act.activation(sq[n % 2][0:r, :].rearrange("p (j c) -> p j c", j=2),
                                   ps[0:r, b0:b0 + 2, 0:QUP // 2], ACT.Square).then_inc(up_squares, 1)
                act.wait_ge(up_sums, n + 1)
                act.activation(root[n % 2][0:r, :], ss[n % 2][0:r, :], ACT.Sqrt, scale=1.0 / MQK,
                               bias=eps_c[0:r, :]).then_inc(up_roots, 1)
                if n >= 1:
                    empty_up(n - 1)
            empty_up(NU - 1)

            attend(1)

            def mix_norm(i):
                r2 = ss[i % 2]
                if i >= 1:
                    act.wait_ge(mix_turned, i)
                for gr in range(2):
                    ins = act.activation(mixn[:, gr * DK // 2:(gr + 1) * DK // 2, :].rearrange("p k n -> p (k n)"),
                                         o_all[:, i, gr * FOX:(gr + 1) * FOX], ACT.Square,
                                         accum_out=r2[:, gr:gr + 1])
                step(ins)
                act.activation(root[i % 2][:, 0:2], r2[:, 0:2], ACT.Sqrt, scale=1.0 / FOX,
                               bias=eps_c[:, :]).then_inc(mix_roots, 1)
                act.wait_ge(mix_inv, i + 1)
                for gr in range(2):
                    ins = act.activation(
                        mixn[:, gr * DK // 2:(gr + 1) * DK // 2, :],
                        o_all[:, i, gr * FOX:(gr + 1) * FOX].rearrange("p (n k) -> p k n", k=DK // 2),
                        ACT.Copy, scale=rinv[i % 2][:, gr:gr + 1])
                ins.then_inc(mix_made, 1)

            def h_norm(i):
                act.wait_ge(h_made, i + 1)
                if i >= 2:
                    act.wait_ge(u2_stored[i % 2], 16 * (i // 2))
                    act.wait_ge(u2_turned, i - 1)
                u = u2n[i % 2]
                step(act.activation(u[:, :, :].rearrange("p k n -> p (k n)"), x[:, i, :], ACT.Square,
                                    accum_out=ss[i % 2][:, 2:3]))
                act.activation(root[i % 2][:, 2:3], ss[i % 2][:, 2:3], ACT.Sqrt, scale=1.0 / D,
                               bias=eps_c[:, :]).then_inc(h_roots, 1)
                act.wait_ge(h_inv, i + 1)
                act.activation(u[:, :, :], x[:, i, :].rearrange("p (n k) -> p k n", k=DK), ACT.Copy,
                               scale=rinv[i % 2][:, 2:3]).then_inc(u2_made, 1)
                act.wait_ge(u2_made, i + 1)
                act.dma_start(u2_rows[i * P:(i + 1) * P, :], u[:, :, :].rearrange("p k n -> p (k n)")
                              ).then_inc(u2_stored[i % 2], 16)

            def route_exps(i):
                act.wait_ge(gmax_made, i + 1)
                act.activation(gexp[:, :], lg[:, 0:NG], ACT.Exp, bias=wt[:, 0:1],
                               accum_out=wt[:, 1:2]).then_inc(gexp_made, 1)
                act.wait_ge(gap_made, i + 1)
                act.activation(wt[:, 4:5], wt[:, 3:4], ACT.Exp).then_inc(gap_exp, 1)

            mix_norm(0)
            for i in range(NT):
                if i + 1 < NT:
                    mix_norm(i + 1)
                h_norm(i)
                if i >= 1:
                    route_exps(i - 1)
            route_exps(NT - 1)

            def act_expert(it, s, first):
                e = it * RING + s
                b = s % 2
                act.wait_ge(h13_done, e + 1)
                act.activation(sil[b][:, :, :], ps[:, 2 + b, 0:FK * slots].rearrange("p (m n) -> p m n", m=FK),
                               ACT.Silu).then_inc(silu_done, 1)
                act.wait_ge(y_done, e + 1)
                if not first or s >= 2:
                    act.wait_ge(y_stored[b], 16 * (RING // 2 * it + s // 2))
                act.activation(ysb[b][:, :], pair(4 + 2 * b, D)[0:slots, :], ACT.Copy).then_inc(y_copied, 1)
                act.wait_ge(y_copied, e + 1)
                act.dma_start(y_main[e, :, :], ysb[b][:, :]).then_inc(y_stored[b], 16)

            for s in range(RING):
                act_expert(0, s, True)
            with act.Fori(1, NE // RING) as it:
                for s in range(RING):
                    act_expert(it, s, False)

            act.wait_ge(over_made, 1)
            tripped = act.value_load(over[0:1, 0:1], min_val=0, max_val=1)
            with act.If(tripped > 0):
                for b in range(2):
                    act.wait_ge(y_stored[b], 16 * NE // 2)
                with act.Fori(0, NE) as e:
                    with act.Fori(1, SEQ // slots) as c:
                        n = e * (SEQ // slots - 1) + c
                        act.wait_ge(fb_h13, n)
                        act.activation(sil[0][:, :, :],
                                       ps[:, 2, 0:FK * slots].rearrange("p (m n) -> p m n", m=FK),
                                       ACT.Silu).then_inc(fb_silu, 1)
                        act.wait_ge(fb_y, n)
                        act.activation(ysb[0][:, :], pair(4, D)[0:slots, :], ACT.Copy).then_inc(fb_y_out, 1)
                        act.wait_ge(fb_y_out, n)
                        act.dma_start(y_over[e, bass.ds((c - 1) * slots, slots), :], ysb[0][:, :]
                                      ).then_inc(fb_stored, 16)

        @block.vector
        def _(dve):
            step = stepper(dve, dve_step)
            dve.memset(eps_c[:, :], EPS).then_inc(eps_made, 1)
            dve.memset(ff[:, :, :], 0.0)
            dve.memset(kr[:, :, :], 0.0)
            step(dve.memset(lg[:, :], -3e38))
            for j, t in enumerate(TOKEN_TILES):
                r = rows(t)
                src = (xm[:, :] if t == MT else x[:, t, :]).rearrange("p (n k) -> p k n", k=DK)
                dve.wait_ge(roots_made, j + 1)
                step(dve.reciprocal(rinv[j % 2][0:r, 0:1], root[j % 2][0:r, 0:1]))
                dve.tensor_scalar(xs[j % 2][0:r, :, :], src, rinv[j % 2][0:r, 0:1], None, ALU.mult
                                  ).then_inc(xs_made, 1)
                if j == 0:
                    dve.wait_ge(consts_in, CONSTS * 16)
                dve.wait_ge(turned, j + 1)
                for q in range(2):
                    k0 = q * DK // 2
                    ins = dve.tensor_tensor(
                        uT[:, k0:k0 + DK // 2, cols(t)],
                        ps[:, 4 + 2 * (j % 2) + q, 0:DK // 2 * r].rearrange("p (k n) -> p k n", k=DK // 2),
                        g_attn[:, k0:k0 + DK // 2].unsqueeze(2).to_broadcast([P, DK // 2, r]), ALU.mult)
                ins.then_inc(turn_dve, 1)
            dve.tensor_scalar(gc_fox[0][0:HD, :], gc_fox[0][0:HD, :], HD ** -0.5, None, ALU.mult)
            dve.tensor_scalar(gc_mla[0][0:NOPE, :], gc_mla[0][0:NOPE, :], MQK ** -0.5, None, ALU.mult)
            dve.memset(gc_mla[0][NOPE:MQK, :], MQK ** -0.5)
            dve.memset(gc_mla[1][NOPE:MQK, :], 1.0)
            dve.memset(gc_fox[0][HD:FOX_AUG, :], 1.0)
            dve.memset(gc_fox[1][HD:FOX_AUG, :], 1.0).then_inc(vecs_made, 1)

            def empty_turn(u):
                n = turn_no[u]
                b, t = u
                r = rows(t)
                dve.wait_ge(turned, n + 1)
                bank = ps[:, 4 + 2 * (n % 2), :]
                if b == "cum":
                    dve.tensor_copy(cum[:, :, :], bank[:, 0:(NT + 1) * H].rearrange("p (t h) -> p t h", h=H)
                                    ).then_inc(turn_dve, 1)
                    dve.wait_ge(turn_dve, sum(not by_act(v) for v in turns[:n + 1]))
                else:
                    dst, g, kk = (cqT, g_ql, QRK) if b == "ffcq" else (ckvT, g_kvl, KVRK)
                    dve.tensor_tensor(dst[:, :, cols(t)], bank[:, 0:kk * r].rearrange("p (k n) -> p k n", k=kk),
                                      g[:, :].unsqueeze(2).to_broadcast([P, kk, r]), ALU.mult
                                      ).then_inc(turn_dve, 1)

            for n, u in enumerate(units):
                b, t = u
                r = rows(t)
                bank = ps[0:r, n % 4, :]
                if b == "ffcq":
                    dve.wait_ge(projected, n + 1)
                    if t != MT:
                        dve.wait_ge(roots_made, root_no[u] + 1)
                    ins = dve.tensor_tensor(ff[0:r, t, :], bank[:, 0:H], bf_b[0:r, :], ALU.add)
                    if t == MT:
                        ins.then_inc(unit_freed, 1)
                    elif t == NT - 1:
                        ins.then_inc(ff_in, 1)
                if u in stage_no:
                    m = stage_no[u]
                    k = root_no[u]
                    if u in head_no:
                        hn = head_no[u]
                        dve.wait_ge(squares_made, hn + 1)
                        dve.tensor_reduce(ss[k % 2][0:r, :],
                                          sq[hn % 2][0:r, 0:FOX].rearrange("p (h c) -> p h c", h=H), X,
                                          ALU.add).then_inc(sums_made, 1)
                    dve.wait_ge(roots_made, k + 1)
                    w = H if u in head_no else 1
                    step(dve.reciprocal(rinv[k % 2][0:r, 0:w], root[k % 2][0:r, 0:w]))
                    if m >= 2:
                        dve.wait_ge(turned, turn_no[staged[m - 2]] + 1)
                    if u in head_no:
                        st = st_fox[m % 2]
                        dve.tensor_tensor(st[0:r, :, 0:HD], bank.rearrange("p (h c) -> p h c", h=H),
                                          rinv[k % 2][0:r, :].unsqueeze(2).to_broadcast([r, H, HD]), ALU.mult
                                          ).then_inc(unit_freed, 1)
                        one, c = (HD, HD + 1) if b == "k" else (HD + 1, HD)
                        dve.memset(st[0:r, :, one:one + 1], 1.0)
                        dve.tensor_scalar(st[0:r, :, c:c + 1], cum[0:r, t, :].unsqueeze(2),
                                          -1.0 if b == "k" else 1.0, None, ALU.mult).then_inc(staged_done, 1)
                    else:
                        kk, c0, w = (KVRK, 0, KVR) if b == "ckv" else (QRK, H, QR)
                        if b == "ckv":
                            dve.tensor_copy(kr[0:r, t, :], bank[:, KVR:KVR + ROPE])
                        dve.tensor_scalar(st_lat[m % 2][0:r, 0:kk, :],
                                          bank[:, c0:c0 + w].rearrange("p (n k) -> p k n", k=kk),
                                          rinv[k % 2][0:r, 0:1], None, ALU.mult).then_inc(staged_done, 1)
                        dve.wait_ge(staged_done, m + 1)
                        dve.sem_inc(unit_freed, 1)
                if u == ("ffcq", NT - 1):
                    dve.wait_ge(ff_log, 1)
                    dve.scalar_tensor_tensor(out=logf[:, :, :], in0=ff[:, :, :], scalar=0.0, in1=ff_e[:, :, :],
                                             op0=ALU.min, op1=ALU.subtract).then_inc(logf_made, 1)
                if u == ("v", NT - 1):
                    empty_turn(("cum", 0))
                if n >= 1 and units[n - 1] in stage_no and not by_act(units[n - 1]):
                    empty_turn(units[n - 1])
            empty_turn(units[-1])

            def attend(ph):
                g0 = ph * UNITS

                def row_max(g):
                    c0, _, c2 = unit_cols(g % NT)
                    dve.wait_ge(scored, g + 1)
                    dve.tensor_reduce(nmax[g % 2][:, :], pair(2 * (g % 2), L)[:, c0:c2], X, ALU.max, negate=True
                                      ).then_inc(maxed, 1)

                row_max(g0)
                row_max(g0 + 1)
                for g in range(g0, g0 + UNITS):
                    n = P * (g % NT + 1)
                    dve.wait_ge(p_turned, g + 1)
                    if g >= 2:
                        dve.wait_ge(pv_done, g - 1)
                    dve.tensor_copy(pT[g % 2][:, 0:g % NT + 1, :].rearrange("p c n -> p (c n)"),
                                    ps[:, 4 + g % 2, 0:n]).then_inc(p_copied, 1)
                    if g >= 2:
                        dve.wait_ge(o_done, g - 1)
                    dve.reciprocal(prinv[g % 2][:, :], psums[g % 2][:, :]).then_inc(sums_inv, 1)
                    if g + 2 < g0 + UNITS:
                        row_max(g + 2)

            attend(0)

            def rotate(dst1, dst2, a1, a2, cos, sin, tmp):
                dve.tensor_tensor(tmp[0], a1, cos, ALU.mult)
                dve.tensor_tensor(tmp[1], a2, sin, ALU.mult)
                dve.tensor_tensor(tmp[2], a1, sin, ALU.mult)
                step(dve.tensor_tensor(tmp[3], a2, cos, ALU.mult))
                dve.tensor_tensor(dst1, tmp[0], tmp[1], ALU.subtract)
                return dve.tensor_tensor(dst2, tmp[2], tmp[3], ALU.add)

            step(dve.tensor_tensor(krg[:, :, :], kr[:, :, :], gr_k[:, :].unsqueeze(1).to_broadcast([P, NT + 1, ROPE]),
                                   ALU.mult))
            step(rotate(krr[:, :, 0:HALF], krr[:, :, HALF:], krg[:, :, 0:HALF], krg[:, :, HALF:],
                        rope_cs[:, :, 0:HALF], rope_cs[:, :, HALF:], [krt[:, j, :, :] for j in range(4)]))
            for n, (kind, t) in enumerate(up_units):
                r = rows(t)
                b0 = 2 * (n % 2)
                st = st_mla[n % 2]
                dve.wait_ge(up_squares, n + 1)
                if kind == "kv":
                    step(dve.tensor_reduce(ss[n % 2][0:r, :],
                                           sq[n % 2][0:r, 0:H * NOPE].rearrange("p (h c) -> p h c", h=H), X, ALU.add))
                    dve.tensor_scalar(ss[n % 2][0:r, :], ss[n % 2][0:r, :], kr_ss[0:r, t:t + 1], None, ALU.add
                                      ).then_inc(up_sums, 1)
                else:
                    dve.tensor_reduce(ss[n % 2][0:r, :], sq[n % 2][0:r, :].rearrange("p (h c) -> p h c", h=H), X,
                                      ALU.add).then_inc(up_sums, 1)
                dve.wait_ge(up_roots, n + 1)
                step(dve.reciprocal(rinv[n % 2][0:r, :], root[n % 2][0:r, :]))
                if n >= 2:
                    dve.wait_ge(up_turned, n - 1)
                if kind == "kv":
                    kv = pair(b0, KVUP)[0:r, :].rearrange("p (h c) -> p h c", h=H)
                    dve.tensor_tensor(st[0:r, :, NOPE:], krr[0:r, t, :].unsqueeze(1).to_broadcast([r, H, ROPE]),
                                      rinv[n % 2][0:r, :].unsqueeze(2).to_broadcast([r, H, ROPE]), ALU.mult)
                    dve.tensor_tensor(st[0:r, :, 0:NOPE], kv[:, :, 0:NOPE],
                                      rinv[n % 2][0:r, :].unsqueeze(2).to_broadcast([r, H, NOPE]), ALU.mult
                                      ).then_inc(up_staged, 1)
                else:
                    hh = H // 2
                    step(dve.tensor_tensor(
                        st[:, :, :].rearrange("p (j h) c -> p j h c", j=2),
                        ps[:, b0:b0 + 2, 0:QUP // 2].rearrange("p j (h c) -> p j h c", h=hh),
                        rinv[n % 2][:, :].rearrange("p (j h) -> p j h", j=2).unsqueeze(3)
                        .to_broadcast([P, 2, hh, MQK]), ALU.mult))
                    step(dve.tensor_tensor(rope_g[:, :, :], st[:, :, NOPE:],
                                           gr_q[:, :].unsqueeze(1).to_broadcast([P, H, ROPE]), ALU.mult))
                    rotate(st[:, :, NOPE:NOPE + HALF], st[:, :, NOPE + HALF:], rope_g[:, :, 0:HALF],
                           rope_g[:, :, HALF:], rope_cs[:, t, 0:HALF].unsqueeze(1).to_broadcast([P, H, HALF]),
                           rope_cs[:, t, HALF:].unsqueeze(1).to_broadcast([P, H, HALF]),
                           [rope_t[:, j, :, :] for j in range(4)]).then_inc(up_staged, 1)

            attend(1)

            def mix_inverse(i):
                dve.wait_ge(mix_roots, i + 1)
                dve.reciprocal(rinv[i % 2][:, 0:2], root[i % 2][:, 0:2]).then_inc(mix_inv, 1)

            def gained(dst, bank0, gain, signal):
                for q in range(2):
                    k0 = q * DK // 2
                    ins = dve.tensor_tensor(
                        dst[:, k0:k0 + DK // 2, :],
                        ps[:, bank0 + q, :].rearrange("p (k n) -> p k n", k=DK // 2),
                        gain[:, k0:k0 + DK // 2].unsqueeze(2).to_broadcast([P, DK // 2, P]), ALU.mult)
                ins.then_inc(signal, 1)

            def mix_empty(i):
                dve.wait_ge(mix_turned, i + 1)
                if i >= 1:
                    dve.wait_ge(wo_done, i)
                gained(mixT, 4, g_mix, mix_out)

            def residual(i):
                dve.wait_ge(wo_done, i + 1)
                dve.tensor_tensor(x[:, i, :], x[:, i, :], pair(0, D), ALU.add).then_inc(h_made, 1)
                dve.wait_ge(h_roots, i + 1)
                dve.reciprocal(rinv[i % 2][:, 2:3], root[i % 2][:, 2:3]).then_inc(h_inv, 1)

            def route(i):
                dve.wait_ge(u2_turned, i + 1)
                if i >= 1:
                    dve.wait_ge(logits_done, i)
                gained(u2T, 6, g_ffn, u2_out)
                dve.wait_ge(logits_done, i + 1)
                dve.tensor_tensor(lg[:, 0:NG], ps[:, 2, 0:NG], b_route[:, 0:NG], ALU.add)
                step(dve.tensor_tensor(lg[:, 8:8 + NE], ps[:, 2, NG:ROUTE], b_route[:, NG:], ALU.add))
                step(dve.max(gtop[:, :], lg[:, 0:8]))
                dve.tensor_scalar(wt[:, 0:1], gtop[:, 0:1], -1.0, None, ALU.mult).then_inc(gmax_made, 1)
                step(dve.max_index(gidx[:, :], gtop[:, :], lg[:, 0:8]))
                step(dve.tensor_copy(gf[:, 0:1], gidx[:, 0:1]))
                step(dve.tensor_scalar(ghot[:, :], iota_f[:, 0:NG], gf[:, 0:1], None, ALU.is_equal))
                step(dve.tensor_tensor(gprod[:, :, :], lg[:, 8:8 + NE].rearrange("p (g e) -> p e g", g=NG),
                                       ghot[:, :].unsqueeze(1).to_broadcast([P, EPG, NG]), ALU.mult))
                step(dve.tensor_reduce(within[:, :], gprod[:, :, :], X, ALU.add))
                step(dve.max(etop[:, :], within[:, :]))
                dve.tensor_tensor(wt[:, 3:4], etop[:, 1:2], etop[:, 0:1], ALU.subtract).then_inc(gap_made, 1)
                step(dve.max_index(eidx[:, :], etop[:, :], within[:, :]))
                step(dve.tensor_copy(esel[:, :], eidx[:, 0:2]))
                dve.tensor_scalar(gf[:, 1:2], gf[:, 0:1], float(EPG), None, ALU.mult).then_inc(dve_gf, 1)
                dve.wait_ge(dve_gf, i + 1)
                step(dve.tensor_scalar(esels[:, i, :], esel[:, :], gf[:, 1:2], None, ALU.add))
                for k in range(2):
                    ins = dve.tensor_scalar(ehots[:, i, k, :], iota_f[:, :], esels[:, i, k:k + 1], None,
                                            ALU.is_equal)
                step(ins)
                dve.tensor_tensor(picks[:, i, :], ehots[:, i, 0, :], ehots[:, i, 1, :], ALU.add
                                  ).then_inc(picks_made, 1)
                dve.wait_ge(gexp_made, i + 1)
                dve.wait_ge(gap_exp, i + 1)
                step(dve.tensor_scalar(wt[:, 5:6], wt[:, 4:5], 1.0, None, ALU.add))
                step(dve.tensor_tensor(wt[:, 6:7], wt[:, 5:6], wt[:, 1:2], ALU.mult))
                step(dve.reciprocal(coef[:, i, 0:1], wt[:, 6:7]))
                step(dve.tensor_tensor(coef[:, i, 1:2], coef[:, i, 0:1], wt[:, 4:5], ALU.mult))

            def positions(i):
                dve.wait_ge(ranked, i + 1)
                step(dve.tensor_tensor(rprod[:, :, :], ehots[:, i, :, :],
                                       ps[:, 3, 0:NE].unsqueeze(1).to_broadcast([P, 2, NE]), ALU.mult))
                step(dve.tensor_reduce(ranks_all[:, i, :], rprod[:, :, :], X, ALU.add))
                dve.scalar_tensor_tensor(out=pos_t[:, i, :], in0=ranks_all[:, i, :], scalar=float(NE),
                                         in1=esels[:, i, :], op0=ALU.mult, op1=ALU.add)
                dve.scalar_tensor_tensor(out=pos_y[:, i, :], in0=esels[:, i, :], scalar=float(slots),
                                         in1=ranks_all[:, i, :], op0=ALU.mult, op1=ALU.add).then_inc(pos_made, 1)

            mix_inverse(0)
            mix_empty(0)
            for i in range(NT):
                if i + 1 < NT:
                    mix_inverse(i + 1)
                residual(i)
                if i + 1 < NT:
                    mix_empty(i + 1)
                if i >= 1:
                    route(i - 1)
                if i >= 2:
                    positions(i - 2)
            positions(NT - 2)
            route(NT - 1)
            positions(NT - 1)
            dve.wait_ge(counted, 1)
            step(dve.tensor_reduce(most[:, :], ps[:, 3, 0:NE], X, ALU.max))
            dve.tensor_scalar(over[:, :], most[:, :], float(slots), None, ALU.is_gt).then_inc(over_made, 1)

            def dve_turned(it, s, first):
                e = it * RING + s
                b = s % 2
                dve.wait_ge(xt_done, e + 1)
                if not first or s >= 2:
                    dve.wait_ge(h13_done, e - 1)
                dve.tensor_tensor(xt[b][:, :, :], ps[:, b, 0:DK * slots].rearrange("p (k n) -> p k n", k=DK),
                                  g_ffn[:, :].unsqueeze(2).to_broadcast([P, DK, slots]), ALU.mult
                                  ).then_inc(xt_out, 1)

            def dve_gate(it, s, first):
                e = it * RING + s
                b = s % 2
                dve.wait_ge(silu_done, e + 1)
                if not first or s >= 2:
                    dve.wait_ge(y_done, e - 1)
                dve.tensor_tensor(hT[b][:, :, :], sil[b][:, :, :],
                                  ps[:, 2 + b, FK * slots:2 * FK * slots].rearrange("p (m n) -> p m n", m=FK),
                                  ALU.mult).then_inc(hT_made, 1)

            def dve_expert(it, s, first=False, last=False):
                if not (last and s == RING - 1):
                    if s == RING - 1:
                        dve_turned(it + 1, 0, False)
                    else:
                        dve_turned(it, s + 1, first)
                dve_gate(it, s, first)

            dve_turned(0, 0, True)
            for s in range(RING):
                dve_expert(0, s, first=True)
            with dve.Fori(1, NE // RING - 1) as it:
                for s in range(RING):
                    dve_expert(it, s)
            for s in range(RING):
                dve_expert(NE // RING - 1, s, last=True)

            tripped = dve.value_load(over[0:1, 0:1], min_val=0, max_val=1)
            with dve.If(tripped > 0):
                dve.tensor_scalar(late[:, 0, :, :], ranks_all[:, :, :], float(slots), None, ALU.is_ge)
                step(dve.tensor_scalar(late[:, 1, :, :], esels[:, :, :], float(REST - slots), float(MAIN - slots),
                                       ALU.mult, ALU.add))
                step(dve.tensor_tensor(late[:, 0, :, :], late[:, 0, :, :], late[:, 1, :, :], ALU.mult))
                step(dve.scalar_tensor_tensor(out=late[:, 1, :, :], in0=esels[:, :, :], scalar=float(slots),
                                              in1=ranks_all[:, :, :], op0=ALU.mult, op1=ALU.add))
                dve.tensor_tensor(pos_y[:, :, :], late[:, 0, :, :], late[:, 1, :, :], ALU.add).then_inc(fb_pos, 1)
                dve.wait_ge(y_done, NE)
                with dve.Fori(0, NE) as e:
                    with dve.Fori(1, SEQ // slots) as c:
                        n = e * (SEQ // slots - 1) + c
                        dve.wait_ge(fb_xt, n)
                        dve.tensor_tensor(xt[0][:, :, :],
                                          ps[:, 0, 0:DK * slots].rearrange("p (k n) -> p k n", k=DK),
                                          g_ffn[:, :].unsqueeze(2).to_broadcast([P, DK, slots]), ALU.mult
                                          ).then_inc(fb_xt_out, 1)
                        dve.wait_ge(fb_silu, n)
                        dve.tensor_tensor(hT[0][:, :, :], sil[0][:, :, :],
                                          ps[:, 2, FK * slots:2 * FK * slots].rearrange("p (m n) -> p m n", m=FK),
                                          ALU.mult).then_inc(fb_hT, 1)

            for t in range(NT):
                for k in range(2):
                    n = 2 * t + k
                    dve.wait_ge(yg_in[n % 4], 16 * (n // 4 + 1))
                    if k == 1:
                        dve.wait_ge(yg_used, n)
                    ins = dve.scalar_tensor_tensor(out=x[:, t, :], in0=yg[n % 4][:, :],
                                                   scalar=coef[:, t, k:k + 1], in1=x[:, t, :], op0=ALU.mult,
                                                   op1=ALU.add)
                    ins.then_inc(out_made if k == 1 else yg_used, 1)
                    if k == 1:
                        dve.wait_ge(out_made, t + 1)
                        dve.sem_inc(yg_used, 1)

        @block.tensor
        def _(pe):
            pe.wait_ge(masks_made, 9)

            def turn(u):
                n = turn_no[u]
                b, t = u
                r = rows(t)
                b0 = 4 + 2 * (n % 2)
                turn_freed(pe, n)
                if b == "cum":
                    pe.wait_ge(logf_made, 1)
                    for t in TOKEN_TILES:
                        dst = ps[:, b0, t * H:(t + 1) * H]
                        earlier = [] if t == MT else [MT] + list(range(t))
                        for s in earlier:
                            pe.matmul(dst, ones[0:rows(s), :], logf[0:rows(s), s, :], start=(s == MT), stop=False)
                        ins = pe.matmul(dst, tri[:, :], logf[:, t, :], start=not earlier, stop=True)
                    ins.then_inc(turned, 1)
                    return
                if b == "x":
                    j = TOKEN_TILES.index(t)
                    pe.wait_ge(xs_made, j + 1)
                    for k in range(DK):
                        q, kk = divmod(k, DK // 2)
                        ins = pe.transpose(ps[:, b0 + q, kk * r:(kk + 1) * r], xs[j % 2][0:r, k, :],
                                           ident[0:r, 0:r])
                    ins.then_inc(turned, 1)
                    return
                m = stage_no[u]
                pe.wait_ge(staged_done, m + 1)
                if b in ("k", "q"):
                    for h in range(H):
                        ins = pe.transpose(pair(b0, H * r)[0:FOX_AUG, h * r:(h + 1) * r], st_fox[m % 2][0:r, h, :],
                                           ident[0:r, 0:r])
                else:
                    for k in range(KVRK if b == "ckv" else QRK):
                        ins = pe.transpose(ps[:, b0, k * r:(k + 1) * r], st_lat[m % 2][0:r, k, :],
                                           ident[0:r, 0:r])
                ins.then_inc(turned, 1)

            def project(u):
                n = unit_no[u]
                b, t = u
                c0, w = BLOCKS[b]
                if u == ("ffcq", MT):
                    w = H
                    pe.wait_ge(turn_dve, len(TOKEN_TILES))
                pe.wait_ge(win_in[b], 16)
                if n >= 4:
                    unit_emptied(pe, n - 4)
                for k in range(DK):
                    ins = pe.matmul(ps[0:rows(t), n % 4, 0:w], uT[:, k, cols(t)], w_in[:, k, c0:c0 + w],
                                    start=(k == 0), stop=(k == DK - 1))
                ins.then_inc(projected, 1)

            for what, u in steps:
                turn(u) if what == "turn" else project(u)

            def attend(ph):
                g0 = ph * UNITS
                depth = FOX_AUG if ph == 0 else MQK

                def score(g):
                    h, i = g % UNITS // NT, g % NT
                    c0, c1, c2 = unit_cols(i)
                    b0 = 2 * (g % 2)
                    q = qT[0:depth, h, i * P:(i + 1) * P]
                    if g >= 2:
                        pe.wait_ge(exped, g - 1)
                    pe.matmul(ps[:, b0, c0:c1], q, kT[0:depth, h, 0:c1 - c0], start=True, stop=False)
                    pe.matmul(ps[:, b0, c1 - P:c1], identb[:, :], causal[:, :], start=False, stop=True)
                    pe.matmul(ps[:, b0 + 1, 0:META], q, kT[0:depth, h, SEQ:L], start=True, stop=True
                              ).then_inc(scored, 1)

                score(g0)
                score(g0 + 1)
                for g in range(g0, g0 + UNITS):
                    h, i = g % UNITS // NT, g % NT
                    c0, c1, c2 = unit_cols(i)
                    pe.wait_ge(exped, g + 1)
                    if g >= 2:
                        pe.wait_ge(o_done, g - 1)
                        pe.wait_ge(p_copied, g - 1)
                    pe.transpose(ps[0:META, 6 + g % 2, 0:P], probs[g % 2][:, c1:c2], ident[:, :]
                                 ).then_inc(pm_turned, 1)
                    for c in range(i + 1):
                        ins = pe.transpose(ps[:, 4 + g % 2, c * P:(c + 1) * P],
                                           probs[g % 2][:, c0 + c * P:c0 + (c + 1) * P], ident[:, :])
                    ins.then_inc(p_turned, 1)
                    if g + 2 < g0 + UNITS:
                        score(g + 2)
                    dst = ps[:, 6 + g % 2, P:P + HD]
                    pe.wait_ge(pm_copied, g + 1)
                    pe.matmul(dst, pT[g % 2][0:META, NT, :], vals[0:META, NT, h * HD:(h + 1) * HD],
                              start=True, stop=False)
                    pe.wait_ge(p_copied, g + 1)
                    for c in range(i + 1):
                        ins = pe.matmul(dst, pT[g % 2][:, c, :], vals[:, c, h * HD:(h + 1) * HD],
                                        start=False, stop=(c == i))
                    ins.then_inc(pv_done, 1)

            for n in range(len(units) - 4, len(units)):
                unit_emptied(pe, n)
            pe.wait_ge(v_copied, len(TOKEN_TILES))
            pe.wait_ge(turn_act, sum(by_act(u) for u in turns))
            pe.wait_ge(turn_dve, sum(not by_act(u) for u in turns))
            attend(0)

            pe.wait_ge(wup_in, 32)
            pe.wait_ge(o_done, UNITS)
            pe.wait_ge(p_copied, UNITS)

            def turn_up(n):
                kind, t = up_units[n]
                r = rows(t)
                pe.wait_ge(up_staged, n + 1)
                if n >= 2:
                    pe.wait_ge(up_out, n - 1)
                for h in range(H):
                    ins = pe.transpose(pair(4 + 2 * (n % 2), H * r)[0:MQK, h * r:(h + 1) * r],
                                       st_mla[n % 2][0:r, h, :], ident[0:r, 0:r])
                ins.then_inc(up_turned, 1)

            for n, (kind, t) in enumerate(up_units):
                r = rows(t)
                b0 = 2 * (n % 2)
                if n >= 2:
                    pe.wait_ge(up_staged, n - 1)
                    pe.wait_ge(up_vals, min(n - 1, len(TOKEN_TILES)))
                src, w, kk, nn = (ckvT, w_ukv, KVRK, KVUP // 2) if kind == "kv" else (cqT, w_uq, QRK, QUP // 2)
                for j in range(2):
                    for k in range(kk):
                        ins = pe.matmul(ps[0:r, b0 + j, 0:nn], src[:, k, cols(t)], w[:, k, j * nn:(j + 1) * nn],
                                        start=(k == 0), stop=(k == kk - 1))
                ins.then_inc(up_done, 1)
                if n >= 1:
                    turn_up(n - 1)
            turn_up(NU - 1)
            pe.wait_ge(up_vals, len(TOKEN_TILES))
            pe.wait_ge(up_out, NU)
            attend(1)

            def turn_mix(i):
                pe.wait_ge(mix_made, i + 1)
                if i >= 1:
                    pe.wait_ge(mix_out, i)
                else:
                    pe.wait_ge(p_copied, 2 * UNITS)
                    pe.wait_ge(o_done, 2 * UNITS)
                for k in range(DK):
                    q, kk = divmod(k, DK // 2)
                    ins = pe.transpose(ps[:, 4 + q, kk * P:(kk + 1) * P], mixn[:, k, :], ident[:, :])
                ins.then_inc(mix_turned, 1)

            def out_project(i):
                pe.wait_ge(mix_out, i + 1)
                if i >= 1:
                    pe.wait_ge(h_made, i)
                for q in range(2):
                    for k in range(DK):
                        ins = pe.matmul(ps[:, q, :], mixT[:, k, :], wo_chunk(k)[:, q * 512:(q + 1) * 512],
                                        start=(k == 0), stop=(k == DK - 1))
                ins.then_inc(wo_done, 1)

            def turn_u2(i):
                pe.wait_ge(u2_made, i + 1)
                if i >= 1:
                    pe.wait_ge(u2_out, i)
                for k in range(DK):
                    q, kk = divmod(k, DK // 2)
                    ins = pe.transpose(ps[:, 6 + q, kk * P:(kk + 1) * P], u2n[i % 2][:, k, :], ident[:, :])
                ins.then_inc(u2_turned, 1)

            def router(i):
                pe.wait_ge(u2_out, i + 1)
                if i >= 1:
                    pe.wait_ge(picks_made, i)
                for k in range(DK):
                    ins = pe.matmul(ps[:, 2, 0:ROUTE], u2T[:, k, :], w_route[:, k, :], start=(k == 0),
                                    stop=(k == DK - 1))
                ins.then_inc(logits_done, 1)

            def ranks(i):
                pe.wait_ge(picks_made, i + 1)
                if i >= 1:
                    pe.wait_ge(pos_made, i)
                for s in range(i):
                    pe.matmul(ps[:, 3, 0:NE], onesb[:, :], picks[:, s, :], start=(s == 0), stop=False)
                pe.matmul(ps[:, 3, 0:NE], before[:, :], picks[:, i, :], start=(i == 0), stop=True
                          ).then_inc(ranked, 1)

            pe.wait_ge(wo_in, 48)
            pe.wait_ge(route_in, 32)
            turn_mix(0)
            for i in range(NT):
                out_project(i)
                if i + 1 < NT:
                    turn_mix(i + 1)
                if i >= 1:
                    turn_u2(i - 1)
                    router(i - 1)
                if i >= 2:
                    ranks(i - 2)
            ranks(NT - 2)
            turn_u2(NT - 1)
            router(NT - 1)
            ranks(NT - 1)
            pe.wait_ge(pos_made, NT)
            for s in range(NT):
                ins = pe.matmul(ps[:, 3, 0:NE], onesb[:, :], picks[:, s, :], start=(s == 0), stop=(s == NT - 1))
            ins.then_inc(counted, 1)

            def turn_rows(bank, src):
                for k in range(DK):
                    ins = pe.transpose(ps[:, bank, k * slots:(k + 1) * slots], src[:, k, :], ident[0:slots, 0:slots])
                return ins

            def first_products(bank, w, src):
                for j in range(2):
                    for m in range(FK):
                        dst = ps[:, bank, (j * FK + m) * slots:(j * FK + m + 1) * slots]
                        for k in range(DK):
                            ins = pe.matmul(dst, w[:, j, k, m * P:(m + 1) * P], src[:, k, :], start=(k == 0),
                                            stop=(k == DK - 1))
                return ins

            def second_product(bank, w, src):
                for q in range(2):
                    for m in range(FK):
                        ins = pe.matmul(ps[0:slots, bank + q, :], src[:, m, :], w[:, m, q * 512:(q + 1) * 512],
                                        start=(m == 0), stop=(m == FK - 1))
                return ins

            def turn_gathered(it, s, first):
                e = it * RING + s
                b = s % 2
                pe.wait_ge(xg_in[b], 16 * (RING // 2 * it + s // 2 + 1))
                if not first or s >= 2:
                    pe.wait_ge(xt_out, e - 1)
                pe.sem_inc(waits_ended, 1)
                turn_rows(b, xg[b]).then_inc(xt_done, 1)

            def expert(it, s, first=False, last=False):
                e = it * RING + s
                b = s % 2
                pe.wait_ge(xt_out, e + 1)
                pe.wait_ge(w13_in[s], 32 * (it + 1))
                if not first or s >= 2:
                    pe.wait_ge(hT_made, e - 1)
                first_products(2 + b, w13[s], xt[b]).then_inc(h13_done, 1)
                if not (last and s == RING - 1):
                    if s == RING - 1:
                        turn_gathered(it + 1, 0, False)
                    else:
                        turn_gathered(it, s + 1, first)
                pe.wait_ge(hT_made, e + 1)
                pe.wait_ge(w2_in[s], 16 * (it + 1))
                if not first or s >= 2:
                    pe.wait_ge(y_copied, e - 1)
                second_product(4 + 2 * b, w2s[s], hT[b]).then_inc(y_done, 1)

            pe.wait_ge(over_made, 1)
            turn_gathered(0, 0, True)
            for s in range(RING):
                expert(0, s, first=True)
            with pe.Fori(1, NE // RING - 1) as it:
                for s in range(RING):
                    expert(it, s)
            for s in range(RING):
                expert(NE // RING - 1, s, last=True)

            tripped = pe.value_load(over[0:1, 0:1], min_val=0, max_val=1)
            with pe.If(tripped > 0):
                pe.wait_ge(y_copied, NE)
                with pe.Fori(0, NE) as e:
                    with pe.Fori(1, SEQ // slots) as c:
                        n = e * (SEQ // slots - 1) + c
                        pe.wait_ge(fb_xg, n * 16)
                        pe.sem_inc(waits_ended, 1)
                        turn_rows(0, xg[0]).then_inc(fb_xt, 1)
                        pe.wait_ge(fb_xt_out, n)
                        pe.wait_ge(fb_w, n * 48)
                        first_products(2, w13[0], xt[0]).then_inc(fb_h13, 1)
                        pe.wait_ge(fb_hT, n)
                        second_product(4, w2s[0], hT[0]).then_inc(fb_y, 1)


_INS = ['x', 'meta_tokens', 'g_attn', 'w_in', 'b_f', 'g_fox_q', 'g_fox_k', 'g_q_lat', 'w_uq', 'g_kv_lat', 'w_ukv',
        'g_mla_q', 'g_mla_k', 'g_fox_out', 'g_mla_out', 'w_o', 'g_ffn', 'w_group', 'b_group', 'w_expert',
        'b_expert', 'w1', 'w3', 'w2']


def rope_table():
    import numpy as np
    inv = np.exp(-np.float32(np.log(10000.0)) * np.arange(HALF, dtype=np.float32) / np.float32(HALF))
    ang = np.arange(L, dtype=np.float32)[:, None] * inv.astype(np.float32)[None, :]
    by_pos = np.concatenate([np.cos(ang), np.sin(ang)], axis=1).astype(np.float32)
    return np.concatenate([by_pos[META:], by_pos[:META], np.zeros((P - META, ROPE), np.float32)])


def kernel(**inputs):
    import numpy as _np
    import concourse.bacc as _bacc
    from concourse import mybir as _mybir
    from concourse.bass_utils import run_bass_kernel_spmd as _run

    nc = _bacc.Bacc("TRN2", target_bir_lowering=False, num_devices=1)
    arrays, args = {}, {}
    for name in _INS:
        v = _np.ascontiguousarray(inputs[name])
        arrays[f"in_{name}"] = v
        args[name] = nc.dram_tensor(f"in_{name}", v.shape, _mybir.dt.from_np(v.dtype), kind="ExternalInput").ap()
    arrays["in_rope"] = rope_table()
    args["rope"] = nc.dram_tensor("in_rope", arrays["in_rope"].shape, F32, kind="ExternalInput").ap()
    out = nc.dram_tensor("out_0", (1, SEQ, D), F32, kind="ExternalOutput").ap()
    build(nc, args, out)
    r = _run(nc, [arrays], core_ids=[0])
    return r.results[0]["out_0"]
```

```python
from contextlib import ExitStack

import concourse.bass as bass
from concourse import mybir

F32 = mybir.dt.float32
F32R = mybir.dt.float32r
BF16 = mybir.dt.bfloat16
I32 = mybir.dt.int32
U32 = mybir.dt.uint32
ALU = mybir.AluOpType
ACT = mybir.ActivationFunctionType
X = mybir.AxisListType.X

P = 128
EPS = 1e-6
NEG = -1e30
ARENA = 16512

D = 1024
SEQ = 512
META = 16
L = SEQ + META
NT = SEQ // P
MT = NT
TOKEN_TILES = [MT] + list(range(NT))
DK = D // P

H = 8
HD = 64
FOX = H * HD
FOX_AUG = HD + 2
QR = 384
KVR = 256
ROPE = 32
HALF = ROPE // 2
NOPE = 64
MQK = NOPE + ROPE
MLA = H * HD
QRK = QR // P
KVRK = KVR // P
QUP = H * MQK
KVUP = H * (NOPE + HD)
IN_COLS = 3 * FOX + H + QR + KVR + ROPE

NG = 4
EPG = 8
NE = NG * EPG
F = 256
FK = F // P
SLOTS = 64
RING = 4
ROUTE = NG + NE

BLOCKS = {
    "ffcq": (3 * FOX, H + QR),
    "v": (2 * FOX, FOX),
    "k": (FOX, FOX),
    "q": (0, FOX),
    "ckv": (3 * FOX + H + QR, KVR + ROPE),
}
BLOCK_ORDER = ["ffcq", "v", "k", "q", "ckv"]


def rows(t):
    return META if t == MT else P


def cols(t):
    return slice(t * P, t * P + rows(t))


def key_cols(t):
    return slice(0, META) if t == MT else slice(META + t * P, META + (t + 1) * P)


def projection_plan():
    units = [(b, t) for b in BLOCK_ORDER for t in TOKEN_TILES if not (b == "q" and t == MT)]
    turned = lambda u: u[0] in ("k", "q", "ckv") or (u[0] == "ffcq" and u[1] != MT)
    steps = [("turn", ("x", t)) for t in TOKEN_TILES]
    for n, u in enumerate(units):
        steps.append(("project", u))
        if n >= 1 and turned(units[n - 1]):
            steps.append(("turn", units[n - 1]))
        if u == ("v", NT - 1):
            steps.append(("turn", ("cum", 0)))
    steps.append(("turn", units[-1]))
    turns = [u for what, u in steps if what == "turn"]
    return units, steps, turns


def build(nc, a, out, slots=SLOTS):
    units, steps, turns = projection_plan()
    unit_no = {u: n for n, u in enumerate(units)}
    turn_no = {u: n for n, u in enumerate(turns)}
    by_act = lambda u: u[0] in ("k", "q")
    staged = [u for u in turns if u[0] not in ("x", "cum")]
    stage_no = {u: n for n, u in enumerate(staged)}
    headed = [u for u in units if u[0] in ("k", "q")]
    head_no = {u: n for n, u in enumerate(headed)}
    rooted = [("x", t) for t in TOKEN_TILES] + [u for u in units if u in headed or u in staged]
    root_no = {u: n for n, u in enumerate(rooted)}

    up_units = [("kv", t) for t in TOKEN_TILES] + [("uq", t) for t in range(NT)]
    NU = len(up_units)
    UNITS = H * NT
    heads = [(ph, h, i) for ph in range(2) for h in range(H) for i in range(NT)]

    with ExitStack() as ctx:
        sem_names = {}

        def sem(name):
            sem_names[name] = ctx.enter_context(nc.semaphore(name))
            return sem_names[name]

        end = [ARENA]

        def place(name, shape, dt, offset):
            return nc.alloc_sbuf_tensor_at(name, shape, dt, offset=offset)

        def region(size):
            start = end[0]
            end[0] = start + (size + 31) // 32 * 32
            return start

        def new(name, shape, dt=F32):
            n = 1
            for s in shape[1:]:
                n *= s
            return place(name, shape, dt, region(n * (2 if dt == BF16 else 4)))

        SLOT = (2 * DK * F + FK * D) * 4
        ring = region(RING * SLOT)
        w13 = [place(f"w13_{s}", [P, 2, DK, F], F32, ring + s * SLOT) for s in range(RING)]
        w2s = [place(f"w2_{s}", [P, FK, D], F32, ring + s * SLOT + 2 * DK * F * 4) for s in range(RING)]
        r_qk = ring + RING * SLOT + NT * D * 4
        block_bytes = {b: DK * BLOCKS[b][1] * 4 for b in BLOCK_ORDER}
        w_at, at = {}, ring + RING * SLOT
        for b in reversed(BLOCK_ORDER):
            at -= block_bytes[b]
            w_at[b] = at
        at -= DK * L * 4
        u_lo_at = w_at["q"] - DK * L * 4
        for b in ("ffcq", "v", "k"):
            w_at[b] -= DK * L * 4
        hi_at = {"ffcq": r_qk + D * 4, "v": r_qk + D * 4 + block_bytes["ffcq"], "k": ring,
                 "q": ring + block_bytes["k"], "ckv": w_at["k"]}
        assert at >= ring and ring + block_bytes["k"] <= w_at["v"]
        assert hi_at["q"] + block_bytes["q"] <= w_at["k"]
        w_in = {b: place(f"w_in_{b}", [P, DK, BLOCKS[b][1]], F32, w_at[b]) for b in BLOCK_ORDER}
        w_lo = {b: place(f"w_lo_{b}", [P, DK, BLOCKS[b][1]], F32R, w_at[b]) for b in BLOCK_ORDER}
        w_hi = {b: place(f"w_hi_{b}", [P, DK, BLOCKS[b][1]], F32R, hi_at[b]) for b in BLOCK_ORDER}
        u_full = place("u_full", [P, DK, L], F32, u_lo_at)
        uT_lo = place("uT_lo", [P, DK, L], F32R, u_lo_at)
        w_uq = place("w_uq", [P, QRK, QUP], F32, ring + 3 * SLOT)
        w_ukv = place("w_ukv", [P, KVRK, KVUP], F32, ring + 3 * SLOT + QRK * QUP * 4)
        WO_A = 6
        w_oa = place("w_oa", [P, WO_A, D], F32, ring + 2 * SLOT)

        x = new("x", [P, NT, D])
        assert region((NT * P + L) * H * 4) == r_qk
        xm = place("xm", [META, D], F32, r_qk)
        qT = place("qT", [MQK, H, SEQ], F32, r_qk)
        kT = place("kT", [MQK, H, L], F32, r_qk + H * SEQ * 4)
        mixn = place("mixn", [P, DK, P], F32, r_qk)
        mixT = place("mixT", [P, DK, P], F32, r_qk + 4096)
        u2n = [place(f"u2n{b}", [P, DK, P], F32, r_qk + 8192 + 4096 * b) for b in range(2)]
        u2T = place("u2T", [P, DK, P], F32, r_qk + 16384)
        xg = [place(f"xg{b}", [slots, DK, P], F32, r_qk + 20480 + 4096 * b) for b in range(2)]
        yg = [place(f"yg{b}", [P, D], F32, r_qk + 4096 * b) for b in range(4)]

        r_v = region((NT + 1) * FOX * 4)
        vals = place("vals", [P, NT + 1, FOX], F32, r_v)
        xt = [place(f"xt{b}", [P, DK, slots], F32, r_v + 2048 * b) for b in range(2)]
        sil = [place(f"sil{b}", [P, FK, slots], F32, r_v + 4096 + 512 * b) for b in range(2)]
        hT = [place(f"hT{b}", [P, FK, slots], F32, r_v + 5120 + 512 * b) for b in range(2)]

        r_u = region(DK * L * 4)
        uT_hi = place("uT_hi", [P, DK, L], F32R, r_u)
        o_all = place("o_all", [P, NT, D], F32, r_u)
        ysb = [place(f"ysb{b}", [slots, D], F32, r_u + 4096 * b) for b in range(2)]

        r_l = region((QRK * SEQ + KVRK * L) * 4)
        cqT = place("cqT", [P, QRK, SEQ], F32, r_l)
        ckvT = place("ckvT", [P, KVRK, L], F32, r_l + QRK * SEQ * 4)
        w_ob = place("w_ob", [P, DK - WO_A, D], F32, r_l)

        r_p = region(9344)
        xs = [place(f"xs{b}", [P, DK, P], F32, r_p + 4096 * b) for b in range(2)]
        sq = [place(f"sq{b}", [P, QUP], F32, r_p + 3072 * b) for b in range(2)]
        rope_g = place("rope_g", [P, H, ROPE], F32, r_p + 6144)
        rope_t = place("rope_t", [P, 4, H, HALF], F32, r_p + 7168)
        PROBS = 4
        probs = [place(f"probs{b}", [P, L], F32, r_p + L * 4 * b) for b in range(PROBS)]

        r_s = region(2 * QUP * 4)
        st_fox = [place(f"st_fox{b}", [P, H, FOX_AUG], F32, r_s + QUP * 4 * b) for b in range(2)]
        st_lat = [place(f"st_lat{b}", [P, QRK, P], F32, r_s + QUP * 4 * b) for b in range(2)]
        pT = [place(f"pT{b}", [P, NT + 1, P], F32, r_s + (NT + 1) * P * 4 * b) for b in range(2)]
        st_mla = [place(f"st_mla{b}", [P, H, MQK], F32, r_s + QUP * 4 * b) for b in range(2)]

        krg = place("krg", [P, NT + 1, ROPE], F32, r_p + 6144)
        krt = place("krt", [P, 4, NT + 1, HALF], F32, r_p + 6144 + (NT + 1) * ROPE * 4)

        ident = new("ident", [P, P])
        tri = new("tri", [P, P])
        ones = new("ones", [P, P])
        causal = new("causal", [P, P], BF16)
        identb = new("identb", [P, P], BF16)
        before = new("before", [P, P], BF16)
        onesb = new("onesb", [P, P], BF16)
        rope_cs = new("rope_cs", [P, NT + 1, ROPE])
        g_attn = new("g_attn_c", [P, DK])
        g_ffn = new("g_ffn_c", [P, DK])
        g_mix = new("g_mix_c", [P, DK])
        g_ql = new("g_ql_c", [P, QRK])
        g_kvl = new("g_kvl_c", [P, KVRK])
        gc_fox = [new("gc_foxq", [FOX_AUG, 1]), new("gc_foxk", [FOX_AUG, 1])]
        gc_mla = [new("gc_mlaq", [MQK, 1]), new("gc_mlak", [MQK, 1])]
        gr_q = new("gr_q", [P, ROPE])
        gr_k = new("gr_k", [P, ROPE])
        bf_b = new("bf_b", [P, H])
        ff = new("ff", [P, NT + 1, H])
        ff_e = new("ff_e", [P, NT + 1, H])
        logf = new("logf", [P, NT + 1, H])
        cum = new("cum", [P, NT + 1, H])
        kr = new("kr", [P, NT + 1, ROPE])
        krr = new("krr", [P, NT + 1, ROPE])
        kr_ss = new("kr_ss", [P, NT + 1])
        ss = [new(f"ss{b}", [P, H]) for b in range(2)]
        root = [new(f"root{b}", [P, H]) for b in range(2)]
        rinv = [new(f"rinv{b}", [P, H]) for b in range(2)]
        nmax = [new(f"nmax{b}", [P, 1]) for b in range(PROBS)]
        psums = [new(f"psums{b}", [P, 1]) for b in range(PROBS)]
        prinv = [new(f"prinv{b}", [P, 1]) for b in range(2)]
        junk = new("junk", [P, ROPE])
        w_route = new("w_route", [P, DK, ROUTE])
        b_route = new("b_route", [P, ROUTE])
        lg = new("lg", [P, NG + 4 + NE])
        gtop = new("gtop", [P, 8])
        gidx = new("gidx", [P, 8], U32)
        gf = new("gf", [P, 2])
        ghot = new("ghot", [P, NG])
        gprod = new("gprod", [P, EPG, NG])
        within = new("within", [P, EPG])
        etop = new("etop", [P, 8])
        eidx = new("eidx", [P, 8], U32)
        esel = new("esel", [P, 2])
        ehot = new("ehot", [P, 2, NE])
        ehots = new("ehots", [P, NT, 2, NE])
        picks = new("picks", [P, NT, NE], BF16)
        rprod = new("rprod", [P, 2, NE])
        ranks_all = new("ranks_all", [P, NT, 2])
        late = new("late", [P, 2, NT, 2])
        esels = new("esels", [P, NT, 2])
        wt = new("wt", [P, 8])
        gexp = new("gexp", [P, NG])
        coef = new("coef", [P, NT, 2])
        pos_t = new("pos_t", [P, NT, 2], I32)
        pos_y = new("pos_y", [P, NT, 2], I32)
        tok = new("tok", [P, NT], I32)
        iota_i = new("iota_i", [P, NE], I32)
        iota_f = new("iota_f", [P, NE])
        zero_i = new("zero_i", [P, P], I32)
        idx = new("idx", [slots, NE], I32)
        fb_idx = new("fb_idx", [slots, 1], I32)
        most = new("most", [P, 1])
        eps_c = new("eps_c", [P, 1])
        over = new("over", [P, 1], I32)
        assert end[0] <= 229344

        ps = ctx.enter_context(nc.psum_tensor("ps", [P, 8, 512], F32))

        def pair(b, n):
            return ps[:, b:b + 2, :].rearrange("p a n -> p (a n)")[:, 0:n]

        u2_rows = nc.dram_tensor("u2_rows", [SEQ, D], F32).ap()
        table = nc.dram_tensor("table", [SEQ * NE, 1], I32).ap()
        MAIN = NE * slots
        REST = SEQ - slots
        y_rows = nc.dram_tensor("y_rows", [MAIN + NE * REST, D], F32).ap()

        consts_in, masks_made, vecs_made = sem("consts_in"), sem("masks_made"), sem("vecs_made")
        ident_made, early_in, late_in = sem("ident_made"), sem("early_in"), sem("late_in")
        eps_made, dve_gf = sem("eps_made"), sem("dve_gf")
        x_in = [sem(f"x_in{t}") for t in range(NT + 1)]
        win_in = {b: sem(f"win_in_{b}") for b in BLOCK_ORDER}
        wup_in, wo_in, route_in = sem("wup_in"), sem("wo_in"), sem("route_in")
        act_step, dve_step, pool_step = sem("act_step"), sem("dve_step"), sem("pool_step")
        roots_made, xs_made = sem("roots_made"), sem("xs_made")
        u_hi_made, u_lo_made, w_hi_made, w_lo_made = (sem("u_hi_made"), sem("u_lo_made"), sem("w_hi_made"),
                                                      sem("w_lo_made"))
        projected, v_copied, unit_freed = sem("projected"), sem("v_copied"), sem("unit_freed")
        squares_made, sums_made, staged_done = sem("squares_made"), sem("sums_made"), sem("staged_done")
        turned, turn_act, turn_dve = sem("turned"), sem("turn_act"), sem("turn_dve")
        ff_in, ff_abs, ff_log, ff_exp, logf_made = (sem("ff_in"), sem("ff_abs"), sem("ff_log"), sem("ff_exp"),
                                                    sem("logf_made"))
        up_done, up_squares, up_sums, up_roots = sem("up_done"), sem("up_squares"), sem("up_sums"), sem("up_roots")
        up_vals, up_staged, up_turned, up_out = sem("up_vals"), sem("up_staged"), sem("up_turned"), sem("up_out")
        scored, maxed, exped = sem("scored"), sem("maxed"), sem("exped")
        pm_turned, p_turned, pm_copied, p_copied = (sem("pm_turned"), sem("p_turned"), sem("pm_copied"),
                                                    sem("p_copied"))
        pv_done, sums_inv, o_done = sem("pv_done"), sem("sums_inv"), sem("o_done")
        mix_roots, mix_inv, mix_made, mix_turned, mix_out = (sem("mix_roots"), sem("mix_inv"), sem("mix_made"),
                                                    sem("mix_turned"), sem("mix_out"))
        wo_done, h_made, h_roots, h_inv, u2_made = (sem("wo_done"), sem("h_made"), sem("h_roots"), sem("h_inv"),
                                                    sem("u2_made"))
        u2_stored = [sem(f"u2_stored{b}") for b in range(2)]
        u2_turned, u2_out, logits_done = sem("u2_turned"), sem("u2_out"), sem("logits_done")
        gmax_made, gexp_made, gap_made, gap_exp = (sem("gmax_made"), sem("gexp_made"), sem("gap_made"),
                                                   sem("gap_exp"))
        picks_made, ranked, pos_made, counted, over_made = (sem("picks_made"), sem("ranked"), sem("pos_made"),
                                                            sem("counted"), sem("over_made"))
        table_zeroed, table_filled, idx_in = sem("table_zeroed"), sem("table_filled"), sem("idx_in")
        w13_in = [sem(f"w13_in{s}") for s in range(RING)]
        w2_in = [sem(f"w2_in{s}") for s in range(RING)]
        xg_in = [sem(f"xg_in{b}") for b in range(2)]
        waits_ended = sem("waits_ended")
        xt_done, xt_out, h13_done, silu_done, hT_made = (sem("xt_done"), sem("xt_out"), sem("h13_done"),
                                                         sem("silu_done"), sem("hT_made"))
        y_done, y_copied = sem("y_done"), sem("y_copied")
        y_stored = [sem(f"y_stored{b}") for b in range(2)]
        fb_w, fb_idx_in, fb_xg, fb_xt, fb_xt_out, fb_h13, fb_silu, fb_hT, fb_y, fb_y_out, fb_stored = (
            sem(n) for n in ("fb_w", "fb_idx_in", "fb_xg", "fb_xt", "fb_xt_out", "fb_h13", "fb_silu", "fb_hT",
                             "fb_y", "fb_y_out", "fb_stored"))
        fb_pos, fb_blank, fb_zeroed = sem("fb_pos"), sem("fb_blank"), sem("fb_zeroed")
        yg_in = [sem(f"yg_in{b}") for b in range(4)]
        yg_used, out_made, out_stored = sem("yg_used"), sem("out_made"), sem("out_stored")

        x_tiles = a["x"][0].rearrange("(t p) d -> t p d", p=P)
        w_in_v = a["w_in"][0].rearrange("(p k) n -> p k n", k=DK)
        w_o_v = a["w_o"][0].rearrange("(g p k) n -> g p k n", g=2, k=DK // 2)
        w1_v = a["w1"][0].rearrange("e (p k) f -> e p k f", k=DK)
        w3_v = a["w3"][0].rearrange("e (p k) f -> e p k f", k=DK)
        w2_v = a["w2"][0].rearrange("e (m p) n -> e p m n", p=P)
        y_main = y_rows[0:MAIN, :].rearrange("(e r) d -> e r d", r=slots)
        y_over = y_rows[MAIN:, :].rearrange("(e r) d -> e r d", r=REST)
        y_over_tiles = y_rows[MAIN:, :].rearrange("(n p) d -> n p d", p=P)
        table_by_rank = table.rearrange("(r e) o -> r (e o)", e=NE)
        out_tiles = out[0].rearrange("(t p) d -> t p d", p=P)

        def wo_chunk(c):
            return w_oa[:, c, :] if c < WO_A else w_ob[:, c - WO_A, :]

        AHEAD = 3
        SINGLES = NT

        def score_bank(g):
            i = g % NT
            return SINGLES if i == NT - 1 else (g // NT * (NT - 1) + i) % SINGLES

        def bank_user_before(g):
            return max((f for f in range(g) if score_bank(f) == score_bank(g)), default=-1)

        def unit_scores(g):
            return pair(score_bank(g), L)[:, 0:META + P * (g % NT + 1)] if g % NT == NT - 1 else \
                ps[:, score_bank(g), 0:META + P * (g % NT + 1)]

        split_order = BLOCK_ORDER

        def stepper(eng, signal):
            count = [0]

            def step(instruction):
                count[0] += 1
                instruction.then_inc(signal, 1)
                eng.wait_ge(signal, count[0])

            return step

        def turn_freed(eng, n):
            if n < 2:
                return
            u = turns[n - 2]
            if by_act(u):
                eng.wait_ge(turn_act, sum(by_act(v) for v in turns[:n - 1]))
            else:
                eng.wait_ge(turn_dve, sum(not by_act(v) for v in turns[:n - 1]))

        def unit_emptied(eng, n):
            of_act = lambda u: u[0] == "v"
            if of_act(units[n]):
                eng.wait_ge(v_copied, sum(of_act(u) for u in units[:n + 1]))
            else:
                eng.wait_ge(unit_freed, sum(not of_act(u) for u in units[:n + 1]))

        block = ctx.enter_context(nc.Block())

        EARLY, LATE = 7, 8

        @block.sync
        def _(sp):
            sp.dma_start(xm[:, :], a["meta_tokens"]).then_inc(x_in[MT], 16)
            sp.dma_start(x[:, 0, :], x_tiles[0]).then_inc(x_in[0], 16)
            sp.dma_start(g_attn[:, :], a["g_attn"][0].rearrange("(p k) -> p k", k=DK)).then_inc(consts_in, 16)
            for t in range(1, NT):
                sp.dma_start(x[:, t, :], x_tiles[t]).then_inc(x_in[t], 16)
            for b in BLOCK_ORDER:
                c0, n = BLOCKS[b]
                sp.dma_start(w_in[b][:, :, :], w_in_v[:, :, c0:c0 + n]).then_inc(win_in[b], 16)
            with nc.allow_non_contiguous_dma("router weights, 36 columns"):
                sp.dma_start(w_route[:, :, 0:NG], a["w_group"][0].rearrange("(p k) n -> p k n", k=DK)
                             ).then_inc(route_in, 16)
                sp.dma_start(w_route[:, :, NG:], a["w_expert"][0].rearrange("(p k) n -> p k n", k=DK)
                             ).then_inc(route_in, 16)

            def load_expert(s, e):
                sp.dma_start(w13[s][:, 0, :, :], w1_v[e]).then_inc(w13_in[s], 16)
                sp.dma_start(w13[s][:, 1, :, :], w3_v[e]).then_inc(w13_in[s], 16)
                sp.dma_start(w2s[s][:, :, :], w2_v[e]).then_inc(w2_in[s], 16)

            sp.wait_ge(projected, len(units))
            sp.dma_start(w_uq[:, :, :], a["w_uq"][0].rearrange("(p k) n -> p k n", k=QRK)).then_inc(wup_in, 16)
            sp.dma_start(w_ukv[:, :, :], a["w_ukv"][0].rearrange("(p k) n -> p k n", k=KVRK)).then_inc(wup_in, 16)
            load_expert(0, 0)
            load_expert(1, 1)
            sp.dma_start(w_oa[:, 0:4, :], w_o_v[0]).then_inc(wo_in, 16)
            sp.dma_start(w_oa[:, 4:6, :], w_o_v[1][:, 0:2, :]).then_inc(wo_in, 16)
            sp.wait_ge(up_done, NU)
            sp.dma_start(w_ob[:, :, :], w_o_v[1][:, 2:4, :]).then_inc(wo_in, 16)
            load_expert(3, 3)
            sp.wait_ge(wo_done, NT)
            load_expert(2, 2)

            def load_w13(it, s):
                e = it * RING + s
                sp.wait_ge(h13_done, e - RING + 1)
                sp.dma_start(w13[s][:, 0, :, :], w1_v[e]).then_inc(w13_in[s], 16)
                sp.dma_start(w13[s][:, 1, :, :], w3_v[e]).then_inc(w13_in[s], 16)

            def load_w2(it, s):
                e = it * RING + s
                sp.wait_ge(y_done, e - RING + 1)
                sp.dma_start(w2s[s][:, :, :], w2_v[e]).then_inc(w2_in[s], 16)

            for s in range(RING):
                load_w13(1, s)
                if s >= 1:
                    load_w2(1, s - 1)
            with sp.Fori(2, NE // RING) as it:
                for s in range(RING):
                    load_w13(it, s)
                    if s >= 1:
                        load_w2(it, s - 1)
                    else:
                        load_w2(it - 1, RING - 1)
            load_w2(NE // RING - 1, RING - 1)

            sp.wait_ge(over_made, 1)
            tripped = sp.value_load(over[0:1, 0:1], min_val=0, max_val=1)
            with sp.If(tripped > 0):
                sp.wait_ge(y_done, NE)
                with sp.Fori(0, NE) as e:
                    with sp.Fori(1, SEQ // slots) as c:
                        n = e * (SEQ // slots - 1) + c
                        sp.dma_start(w13[0][:, 0, :, :], w1_v[e]).then_inc(fb_w, 16)
                        sp.dma_start(w13[0][:, 1, :, :], w3_v[e]).then_inc(fb_w, 16)
                        sp.dma_start(w2s[0][:, :, :], w2_v[e]).then_inc(fb_w, 16)
                        sp.wait_ge(fb_stored, n * 16)
                        sp.sem_inc(waits_ended, 1)

            for t in range(NT):
                sp.wait_ge(out_made, t + 1)
                sp.dma_start(out_tiles[t], x[:, t, :]).then_inc(out_stored, 16)
            sp.wait_ge(out_stored, NT * 16)

        @block.gpsimd
        def _(pool):
            step = stepper(pool, pool_step)
            step(pool.memset(ident[:, :], 0.0))
            pool.affine_select(out=ident[:, :], in_=ident[:, :], compare_op=ALU.not_equal, fill=1.0, base=0,
                               pattern=[[-1, P]], channel_multiplier=1).then_inc(ident_made, 1)
            with nc.allow_non_contiguous_dma("small vectors"):
                def early(dst, src):
                    pool.dma_start(dst, src).then_inc(early_in, 16)

                def late_const(dst, src):
                    pool.dma_start(dst, src).then_inc(late_in, 16)
                early(bf_b[:, :], a["b_f"][0].partition_broadcast(P))
                early(g_ql[:, :], a["g_q_lat"][0].rearrange("(p k) -> p k", k=QRK))
                early(g_kvl[:, :], a["g_kv_lat"][0].rearrange("(p k) -> p k", k=KVRK))
                early(gc_fox[0][0:HD, :], a["g_fox_q"][0].rearrange("(p o) -> p o", o=1))
                early(gc_fox[1][0:HD, :], a["g_fox_k"][0].rearrange("(p o) -> p o", o=1))
                early(gc_mla[0][0:NOPE, :], a["g_mla_q"][0][0:NOPE].rearrange("(p o) -> p o", o=1))
                early(gc_mla[1][0:NOPE, :], a["g_mla_k"][0][0:NOPE].rearrange("(p o) -> p o", o=1))
                late_const(gr_q[:, :], a["g_mla_q"][0][NOPE:MQK].partition_broadcast(P))
                late_const(gr_k[:, :], a["g_mla_k"][0][NOPE:MQK].partition_broadcast(P))
                late_const(g_mix[:, 0:DK // 2], a["g_fox_out"][0].rearrange("(p k) -> p k", k=DK // 2))
                late_const(g_mix[:, DK // 2:], a["g_mla_out"][0].rearrange("(p k) -> p k", k=DK // 2))
                late_const(g_ffn[:, :], a["g_ffn"][0].rearrange("(p k) -> p k", k=DK))
                late_const(b_route[:, 0:NG], a["b_group"][0].partition_broadcast(P))
                late_const(b_route[:, NG:], a["b_expert"][0].partition_broadcast(P))
                late_const(rope_cs[:, :, :], a["rope"].rearrange("(t p) c -> p t c", p=P))
            step(pool.memset(identb[:, :], 0.0))
            pool.affine_select(out=identb[:, :], in_=identb[:, :], compare_op=ALU.not_equal, fill=1.0, base=0,
                               pattern=[[-1, P]], channel_multiplier=1).then_inc(masks_made, 1)
            step(pool.memset(causal[:, :], 0.0))
            pool.affine_select(out=causal[:, :], in_=causal[:, :], compare_op=ALU.is_ge, fill=NEG, base=0,
                               pattern=[[-1, P]], channel_multiplier=1).then_inc(masks_made, 1)
            step(pool.memset(tri[:, :], 1.0))
            pool.affine_select(out=tri[:, :], in_=tri[:, :], compare_op=ALU.is_ge, fill=0.0, base=0,
                               pattern=[[1, P]], channel_multiplier=-1).then_inc(masks_made, 1)
            step(pool.memset(before[:, :], 1.0))
            pool.affine_select(out=before[:, :], in_=before[:, :], compare_op=ALU.is_ge, fill=0.0, base=-1,
                               pattern=[[1, P]], channel_multiplier=-1).then_inc(masks_made, 1)
            pool.memset(ones[:, :], 1.0).then_inc(masks_made, 1)
            pool.memset(onesb[:, :], 1.0).then_inc(masks_made, 1)
            pool.iota(tok[:, :], pattern=[[P, NT]], base=0, channel_multiplier=1).then_inc(masks_made, 1)
            step(pool.iota(iota_i[:, :], pattern=[[1, NE]], base=0, channel_multiplier=0))
            pool.tensor_copy(iota_f[:, :], iota_i[:, :]).then_inc(masks_made, 1)
            step(pool.memset(zero_i[:, :], 0))
            pool.dma_start(table.rearrange("(p n) o -> p (n o)", p=P), zero_i[:, :]).then_inc(table_zeroed, 16)

            pool.wait_ge(table_zeroed, 16)
            for t in range(NT):
                pool.wait_ge(pos_made, t + 1)
                for k in range(2):
                    pool.indirect_dma_start(
                        out=table, out_offset=bass.IndirectOffsetOnAxis(ap=pos_t[:, t, k:k + 1].bitcast(U32), axis=0),
                        in_=tok[:, t:t + 1], in_offset=None).then_inc(table_filled, 16)
            pool.wait_ge(table_filled, 2 * NT * 16)
            pool.dma_start(idx[:, :], table_by_rank[0:slots, :]).then_inc(idx_in, 16)
            pool.wait_ge(idx_in, 16)
            for b in range(2):
                pool.wait_ge(u2_stored[b], 16 * NT // 2)

            for e in range(NE):
                if e >= 2:
                    pool.wait_ge(xt_done, e - 1)
                pool.indirect_dma_start(
                    out=xg[e % 2][:, :, :].rearrange("p k n -> p (k n)"), out_offset=None, in_=u2_rows,
                    in_offset=bass.IndirectOffsetOnAxis(ap=idx[:, e:e + 1].bitcast(U32), axis=0)
                ).then_inc(xg_in[e % 2], 16)

            def fetch_outputs(source):
                for b in range(2):
                    pool.wait_ge(y_stored[b], 16 * NE // 2)
                for t in range(NT):
                    for k in range(2):
                        n = 2 * t + k
                        if n >= 4:
                            pool.wait_ge(yg_used, n - 3)
                        pool.indirect_dma_start(
                            out=yg[n % 4][:, :], out_offset=None, in_=source,
                            in_offset=bass.IndirectOffsetOnAxis(ap=pos_y[:, t, k:k + 1].bitcast(U32), axis=0)
                        ).then_inc(yg_in[n % 4], 16)

            pool.wait_ge(over_made, 1)
            tripped = pool.value_load(over[0:1, 0:1], min_val=0, max_val=1)
            with pool.If(tripped > 0):
                pool.wait_ge(xt_done, NE)
                pool.memset(yg[0][:, :], 0.0).then_inc(fb_blank, 1)
                pool.wait_ge(fb_blank, 1)
                with pool.Fori(0, NE * REST // P) as n:
                    pool.dma_start(y_over_tiles[n, :, :], yg[0][:, :]).then_inc(fb_zeroed, 16)
                    pool.wait_ge(fb_zeroed, n * 16 + 16)
                with pool.Fori(0, NE) as e:
                    with pool.Fori(1, SEQ // slots) as c:
                        n = e * (SEQ // slots - 1) + c
                        with nc.allow_non_contiguous_dma("one expert's tokens"):
                            pool.dma_start(fb_idx[:, :], table_by_rank[bass.ds(c * slots, slots), bass.ds(e, 1)]
                                           ).then_inc(fb_idx_in, 16)
                        pool.wait_ge(fb_idx_in, n * 16)
                        pool.sem_inc(waits_ended, 1)
                        pool.indirect_dma_start(
                            out=xg[0][:, :, :].rearrange("p k n -> p (k n)"), out_offset=None, in_=u2_rows,
                            in_offset=bass.IndirectOffsetOnAxis(ap=fb_idx[:, :].bitcast(U32), axis=0)
                        ).then_inc(fb_xg, 16)
                        pool.wait_ge(fb_stored, n * 16)
                pool.wait_ge(fb_pos, 1)
                fetch_outputs(y_rows)
            with pool.Else():
                fetch_outputs(y_rows[0:MAIN, :])

        @block.scalar
        def _(act):
            step = stepper(act, act_step)
            def u_high(j):
                c = cols(TOKEN_TILES[j])
                act.wait_ge(turn_dve, j + 1)
                act.activation(uT_hi[:, :, c], u_full[:, :, c], ACT.Copy).then_inc(u_hi_made, 1)

            def w_high(b):
                act.wait_ge(win_in[b], 16)
                if b in ("k", "q", "ckv"):
                    before_b = BLOCK_ORDER[BLOCK_ORDER.index(b) - 2]
                    act.wait_ge(projected, unit_no[(before_b, NT - 1)] + 1)
                for k0 in range(0, DK, DK // 2):
                    act.activation(w_hi[b][:, k0:k0 + DK // 2, :], w_in[b][:, k0:k0 + DK // 2, :], ACT.Copy
                                   ).then_inc(w_hi_made, 1)

            act.wait_ge(eps_made, 1)
            act.activation(root[0][:, 0:1], eps_c[:, :], ACT.Sqrt)
            for j, t in enumerate(TOKEN_TILES):
                r = rows(t)
                src = xm[:, :] if t == MT else x[:, t, :]
                act.wait_ge(x_in[t], 16)
                if j >= 2:
                    act.wait_ge(turned, j - 1)
                step(act.activation(xs[j % 2][0:r, :, :].rearrange("p k n -> p (k n)"), src, ACT.Square,
                                    accum_out=ss[j % 2][0:r, 0:1]))
                act.activation(root[j % 2][0:r, 0:1], ss[j % 2][0:r, 0:1], ACT.Sqrt, scale=1.0 / D,
                               bias=eps_c[0:r, :]).then_inc(roots_made, 1)
                if j >= 1:
                    u_high(j - 1)
            w_high("ffcq")
            u_high(len(TOKEN_TILES) - 1)
            w_high("v")

            def empty_turn(u):
                n = turn_no[u]
                t = u[1]
                r = rows(t)
                act.wait_ge(turned, n + 1)
                src = pair(4 + 2 * (n % 2), H * r)[0:FOX_AUG, :].rearrange("p (h c) -> p h c", h=H)
                if u == ("k", MT):
                    act.wait_ge(vecs_made, 1)
                which = 0 if u[0] == "q" else 1
                dst = qT[0:FOX_AUG, :, cols(t)] if u[0] == "q" else kT[0:FOX_AUG, :, key_cols(t)]
                act.activation(dst, src, ACT.Copy, scale=gc_fox[which][:, :]).then_inc(turn_act, 1)

            for n, u in enumerate(units):
                b, t = u
                r = rows(t)
                bank = ps[0:r, n % 4, :]
                if t == NT - 1 and b in ("ffcq", "v", "k"):
                    split_next = BLOCK_ORDER[BLOCK_ORDER.index(b) + 2]
                else:
                    split_next = None
                act.wait_ge(projected, n + 1)
                if b == "v":
                    act.activation(vals[0:r, t, :], bank, ACT.Copy).then_inc(v_copied, 1)
                elif b in ("k", "q"):
                    m = head_no[u]
                    if m >= 2:
                        act.wait_ge(sums_made, m - 1)
                    act.activation(sq[m % 2][0:r, 0:FOX], bank, ACT.Square).then_inc(squares_made, 1)
                    act.wait_ge(sums_made, m + 1)
                    k = root_no[u]
                    act.activation(root[k % 2][0:r, :], ss[k % 2][0:r, :], ACT.Sqrt, scale=1.0 / HD,
                                   bias=eps_c[0:r, :]).then_inc(roots_made, 1)
                elif b == "ckv" or t != MT:
                    k = root_no[u]
                    w, c0 = (KVR, 0) if b == "ckv" else (QR, H)
                    if b == "ckv":
                        step(act.activation(junk[0:r, :], bank[:, KVR:KVR + ROPE], ACT.Square,
                                            accum_out=kr_ss[0:r, t:t + 1]))
                    step(act.activation(sq[k % 2][0:r, 0:w], bank[:, c0:c0 + w], ACT.Square,
                                        accum_out=ss[k % 2][0:r, 0:1]))
                    act.activation(root[k % 2][0:r, 0:1], ss[k % 2][0:r, 0:1], ACT.Sqrt, scale=1.0 / w,
                                   bias=eps_c[0:r, :]).then_inc(roots_made, 1)
                if u == ("ffcq", NT - 1):
                    act.wait_ge(ff_in, 1)
                    act.activation(ff_e[:, :, :], ff[:, :, :], ACT.Abs).then_inc(ff_abs, 1)
                    act.wait_ge(ff_abs, 1)
                    act.activation(ff_e[:, :, :], ff_e[:, :, :], ACT.Exp, scale=-1.0).then_inc(ff_exp, 1)
                    act.wait_ge(ff_exp, 1)
                    act.activation(ff_e[:, :, :], ff_e[:, :, :], ACT.Ln, bias=1.0).then_inc(ff_log, 1)
                if split_next:
                    w_high(split_next)
                if n >= 2 and by_act(units[n - 2]):
                    empty_turn(units[n - 2])
            for u in units[-2:]:
                if by_act(u):
                    empty_turn(u)

            def attend(ph):
                g0 = ph * UNITS

                def exp(g):
                    act.wait_ge(maxed, g + 1)
                    act.activation(probs[g % PROBS][:, 0:META + P * (g % NT + 1)], unit_scores(g), ACT.Exp,
                                   bias=nmax[g % PROBS][:, :], accum_out=psums[g % PROBS][:, :]).then_inc(exped, 1)

                def copy_meta(g):
                    act.wait_ge(pm_turned, g + 1)
                    act.activation(pT[g % 2][0:META, NT, :], ps[0:META, score_bank(g), 0:P], ACT.Copy
                                   ).then_inc(pm_copied, 1)

                def output(g):
                    h, i = g % UNITS // NT, g % NT
                    act.wait_ge(pv_done, g + 1)
                    act.wait_ge(sums_inv, g + 1)
                    c = ph * FOX + h * HD
                    act.activation(o_all[:, i, c:c + HD], ps[:, score_bank(g), P:P + HD], ACT.Copy,
                                   scale=prinv[g % 2][:, :]).then_inc(o_done, 1)

                for g in range(g0, g0 + AHEAD):
                    exp(g)
                for g in range(g0, g0 + UNITS):
                    copy_meta(g)
                    if g > g0:
                        output(g - 1)
                    if g + AHEAD < g0 + UNITS:
                        exp(g + AHEAD)
                output(g0 + UNITS - 1)

            attend(0)

            def empty_up(n):
                kind, t = up_units[n]
                r = rows(t)
                act.wait_ge(up_turned, n + 1)
                src = pair(4 + 2 * (n % 2), H * r)[0:MQK, :].rearrange("p (h c) -> p h c", h=H)
                which = 0 if kind == "uq" else 1
                dst = qT[:, :, cols(t)] if kind == "uq" else kT[:, :, key_cols(t)]
                act.activation(dst, src, ACT.Copy, scale=gc_mla[which][:, :]).then_inc(up_out, 1)

            for n, (kind, t) in enumerate(up_units):
                r = rows(t)
                b0 = 2 * (n % 2)
                act.wait_ge(up_done, n + 1)
                if n >= 2:
                    act.wait_ge(up_sums, n - 1)
                if kind == "kv":
                    kv = pair(b0, KVUP)[0:r, :].rearrange("p (h c) -> p h c", h=H)
                    act.activation(sq[n % 2][0:r, 0:H * NOPE].rearrange("p (h c) -> p h c", h=H),
                                   kv[:, :, 0:NOPE], ACT.Square).then_inc(up_squares, 1)
                    act.activation(vals[0:r, t, :].rearrange("p (h c) -> p h c", h=H), kv[:, :, NOPE:],
                                   ACT.Copy).then_inc(up_vals, 1)
                else:
                    act.activation(sq[n % 2][0:r, :].rearrange("p (j c) -> p j c", j=2),
                                   ps[0:r, b0:b0 + 2, 0:QUP // 2], ACT.Square).then_inc(up_squares, 1)
                act.wait_ge(up_sums, n + 1)
                act.activation(root[n % 2][0:r, :], ss[n % 2][0:r, :], ACT.Sqrt, scale=1.0 / MQK,
                               bias=eps_c[0:r, :]).then_inc(up_roots, 1)
                if n >= 1:
                    empty_up(n - 1)
            empty_up(NU - 1)

            attend(1)

            def mix_norm(i):
                r2 = ss[i % 2]
                if i >= 1:
                    act.wait_ge(mix_turned, i)
                for gr in range(2):
                    ins = act.activation(mixn[:, gr * DK // 2:(gr + 1) * DK // 2, :].rearrange("p k n -> p (k n)"),
                                         o_all[:, i, gr * FOX:(gr + 1) * FOX], ACT.Square,
                                         accum_out=r2[:, gr:gr + 1])
                step(ins)
                act.activation(root[i % 2][:, 0:2], r2[:, 0:2], ACT.Sqrt, scale=1.0 / FOX,
                               bias=eps_c[:, :]).then_inc(mix_roots, 1)
                act.wait_ge(mix_inv, i + 1)
                for gr in range(2):
                    ins = act.activation(
                        mixn[:, gr * DK // 2:(gr + 1) * DK // 2, :],
                        o_all[:, i, gr * FOX:(gr + 1) * FOX].rearrange("p (n k) -> p k n", k=DK // 2),
                        ACT.Copy, scale=rinv[i % 2][:, gr:gr + 1])
                ins.then_inc(mix_made, 1)

            def h_norm(i):
                act.wait_ge(h_made, i + 1)
                if i >= 2:
                    act.wait_ge(u2_stored[i % 2], 16 * (i // 2))
                    act.wait_ge(u2_turned, i - 1)
                u = u2n[i % 2]
                step(act.activation(u[:, :, :].rearrange("p k n -> p (k n)"), x[:, i, :], ACT.Square,
                                    accum_out=ss[i % 2][:, 2:3]))
                act.activation(root[i % 2][:, 2:3], ss[i % 2][:, 2:3], ACT.Sqrt, scale=1.0 / D,
                               bias=eps_c[:, :]).then_inc(h_roots, 1)
                act.wait_ge(h_inv, i + 1)
                act.activation(u[:, :, :], x[:, i, :].rearrange("p (n k) -> p k n", k=DK), ACT.Copy,
                               scale=rinv[i % 2][:, 2:3]).then_inc(u2_made, 1)
                act.wait_ge(u2_made, i + 1)
                act.dma_start(u2_rows[i * P:(i + 1) * P, :], u[:, :, :].rearrange("p k n -> p (k n)")
                              ).then_inc(u2_stored[i % 2], 16)

            def route_exps(i):
                act.wait_ge(gmax_made, i + 1)
                act.activation(gexp[:, :], lg[:, 0:NG], ACT.Exp, bias=wt[:, 0:1],
                               accum_out=wt[:, 1:2]).then_inc(gexp_made, 1)
                act.wait_ge(gap_made, i + 1)
                act.activation(wt[:, 4:5], wt[:, 3:4], ACT.Exp).then_inc(gap_exp, 1)

            mix_norm(0)
            for i in range(NT):
                if i + 1 < NT:
                    mix_norm(i + 1)
                h_norm(i)
                if i >= 1:
                    route_exps(i - 1)
            route_exps(NT - 1)

            def silu(it, s, first=False):
                e = it * RING + s
                b = s % 2
                act.wait_ge(h13_done, e + 1)
                if not first or s >= 2:
                    act.wait_ge(hT_made, e - 1)
                act.activation(sil[b][:, :, :], ps[:, 2 + b, 0:FK * slots].rearrange("p (m n) -> p m n", m=FK),
                               ACT.Silu).then_inc(silu_done, 1)

            def store_rows(it, s, first=False):
                e = it * RING + s
                b = s % 2
                act.wait_ge(y_done, e + 1)
                if not first or s >= 2:
                    act.wait_ge(y_stored[b], 16 * (RING // 2 * it + s // 2))
                act.activation(ysb[b][:, :], pair(4 + 2 * b, D)[0:slots, :], ACT.Copy).then_inc(y_copied, 1)
                act.wait_ge(y_copied, e + 1)
                act.dma_start(y_main[e, :, :], ysb[b][:, :]).then_inc(y_stored[b], 16)

            for s in range(RING):
                silu(0, s, first=True)
                if s >= 1:
                    store_rows(0, s - 1, first=True)
            with act.Fori(1, NE // RING) as it:
                for s in range(RING):
                    silu(it, s)
                    if s >= 1:
                        store_rows(it, s - 1)
                    else:
                        store_rows(it - 1, RING - 1)
            store_rows(NE // RING - 1, RING - 1)

            act.wait_ge(over_made, 1)
            tripped = act.value_load(over[0:1, 0:1], min_val=0, max_val=1)
            with act.If(tripped > 0):
                for b in range(2):
                    act.wait_ge(y_stored[b], 16 * NE // 2)
                with act.Fori(0, NE) as e:
                    with act.Fori(1, SEQ // slots) as c:
                        n = e * (SEQ // slots - 1) + c
                        act.wait_ge(fb_h13, n)
                        act.activation(sil[0][:, :, :],
                                       ps[:, 2, 0:FK * slots].rearrange("p (m n) -> p m n", m=FK),
                                       ACT.Silu).then_inc(fb_silu, 1)
                        act.wait_ge(fb_y, n)
                        act.activation(ysb[0][:, :], pair(4, D)[0:slots, :], ACT.Copy).then_inc(fb_y_out, 1)
                        act.wait_ge(fb_y_out, n)
                        act.dma_start(y_over[e, bass.ds((c - 1) * slots, slots), :], ysb[0][:, :]
                                      ).then_inc(fb_stored, 16)

        @block.vector
        def _(dve):
            step = stepper(dve, dve_step)
            dve.memset(eps_c[:, :], EPS).then_inc(eps_made, 1)
            dve.memset(ff[:, :, :], 0.0)
            dve.memset(kr[:, :, :], 0.0)
            step(dve.memset(lg[:, :], -3e38))
            def u_low(j):
                c = cols(TOKEN_TILES[j])
                dve.wait_ge(u_hi_made, j + 1)
                dve.tensor_tensor(uT_lo[:, :, c], u_full[:, :, c], uT_hi[:, :, c].bitcast(F32), ALU.subtract
                                  ).then_inc(u_lo_made, 1)

            def w_low(b):
                for q in range(2):
                    k0 = q * DK // 2
                    dve.wait_ge(w_hi_made, 2 * split_order.index(b) + q + 1)
                    dve.tensor_tensor(w_lo[b][:, k0:k0 + DK // 2, :], w_in[b][:, k0:k0 + DK // 2, :],
                                      w_hi[b][:, k0:k0 + DK // 2, :].bitcast(F32), ALU.subtract
                                      ).then_inc(w_lo_made, 1)

            for j, t in enumerate(TOKEN_TILES):
                r = rows(t)
                src = (xm[:, :] if t == MT else x[:, t, :]).rearrange("p (n k) -> p k n", k=DK)
                dve.wait_ge(roots_made, j + 1)
                step(dve.reciprocal(rinv[j % 2][0:r, 0:1], root[j % 2][0:r, 0:1]))
                dve.tensor_scalar(xs[j % 2][0:r, :, :], src, rinv[j % 2][0:r, 0:1], None, ALU.mult
                                  ).then_inc(xs_made, 1)
                if j == 0:
                    dve.wait_ge(consts_in, 16)
                dve.wait_ge(turned, j + 1)
                for q in range(2):
                    k0 = q * DK // 2
                    ins = dve.tensor_tensor(
                        u_full[:, k0:k0 + DK // 2, cols(t)],
                        ps[:, 4 + 2 * (j % 2) + q, 0:DK // 2 * r].rearrange("p (k n) -> p k n", k=DK // 2),
                        g_attn[:, k0:k0 + DK // 2].unsqueeze(2).to_broadcast([P, DK // 2, r]), ALU.mult)
                ins.then_inc(turn_dve, 1)
                if j >= 1:
                    u_low(j - 1)
            u_low(len(TOKEN_TILES) - 1)
            w_low("ffcq")
            dve.wait_ge(early_in, EARLY * 16)
            dve.tensor_scalar(gc_fox[0][0:HD, :], gc_fox[0][0:HD, :], HD ** -0.5, None, ALU.mult)
            dve.tensor_scalar(gc_mla[0][0:NOPE, :], gc_mla[0][0:NOPE, :], MQK ** -0.5, None, ALU.mult)
            dve.memset(gc_mla[0][NOPE:MQK, :], MQK ** -0.5)
            dve.memset(gc_mla[1][NOPE:MQK, :], 1.0)
            dve.memset(gc_fox[0][HD:FOX_AUG, :], 1.0)
            dve.memset(gc_fox[1][HD:FOX_AUG, :], 1.0).then_inc(vecs_made, 1)
            w_low("v")

            def empty_turn(u):
                n = turn_no[u]
                b, t = u
                r = rows(t)
                dve.wait_ge(turned, n + 1)
                bank = ps[:, 4 + 2 * (n % 2), :]
                if b == "cum":
                    dve.tensor_copy(cum[:, :, :], bank[:, 0:(NT + 1) * H].rearrange("p (t h) -> p t h", h=H)
                                    ).then_inc(turn_dve, 1)
                    dve.wait_ge(turn_dve, sum(not by_act(v) for v in turns[:n + 1]))
                else:
                    dst, g, kk = (cqT, g_ql, QRK) if b == "ffcq" else (ckvT, g_kvl, KVRK)
                    dve.tensor_tensor(dst[:, :, cols(t)], bank[:, 0:kk * r].rearrange("p (k n) -> p k n", k=kk),
                                      g[:, :].unsqueeze(2).to_broadcast([P, kk, r]), ALU.mult
                                      ).then_inc(turn_dve, 1)

            for n, u in enumerate(units):
                b, t = u
                r = rows(t)
                bank = ps[0:r, n % 4, :]
                if b == "ffcq":
                    dve.wait_ge(projected, n + 1)
                    if t != MT:
                        dve.wait_ge(roots_made, root_no[u] + 1)
                    ins = dve.tensor_tensor(ff[0:r, t, :], bank[:, 0:H], bf_b[0:r, :], ALU.add)
                    if t == MT:
                        ins.then_inc(unit_freed, 1)
                    elif t == NT - 1:
                        ins.then_inc(ff_in, 1)
                if u in stage_no:
                    m = stage_no[u]
                    k = root_no[u]
                    if u in head_no:
                        hn = head_no[u]
                        dve.wait_ge(squares_made, hn + 1)
                        dve.tensor_reduce(ss[k % 2][0:r, :],
                                          sq[hn % 2][0:r, 0:FOX].rearrange("p (h c) -> p h c", h=H), X,
                                          ALU.add).then_inc(sums_made, 1)
                    dve.wait_ge(roots_made, k + 1)
                    w = H if u in head_no else 1
                    step(dve.reciprocal(rinv[k % 2][0:r, 0:w], root[k % 2][0:r, 0:w]))
                    if m >= 2:
                        dve.wait_ge(turned, turn_no[staged[m - 2]] + 1)
                    if u in head_no:
                        st = st_fox[m % 2]
                        dve.tensor_tensor(st[0:r, :, 0:HD], bank.rearrange("p (h c) -> p h c", h=H),
                                          rinv[k % 2][0:r, :].unsqueeze(2).to_broadcast([r, H, HD]), ALU.mult
                                          ).then_inc(unit_freed, 1)
                        one, c = (HD, HD + 1) if b == "k" else (HD + 1, HD)
                        dve.memset(st[0:r, :, one:one + 1], 1.0)
                        dve.tensor_scalar(st[0:r, :, c:c + 1], cum[0:r, t, :].unsqueeze(2),
                                          -1.0 if b == "k" else 1.0, None, ALU.mult).then_inc(staged_done, 1)
                    else:
                        kk, c0, w = (KVRK, 0, KVR) if b == "ckv" else (QRK, H, QR)
                        if b == "ckv":
                            dve.tensor_copy(kr[0:r, t, :], bank[:, KVR:KVR + ROPE])
                        dve.tensor_scalar(st_lat[m % 2][0:r, 0:kk, :],
                                          bank[:, c0:c0 + w].rearrange("p (n k) -> p k n", k=kk),
                                          rinv[k % 2][0:r, 0:1], None, ALU.mult).then_inc(staged_done, 1)
                        dve.wait_ge(staged_done, m + 1)
                        dve.sem_inc(unit_freed, 1)
                if u == ("ffcq", NT - 1):
                    dve.wait_ge(ff_log, 1)
                    dve.scalar_tensor_tensor(out=logf[:, :, :], in0=ff[:, :, :], scalar=0.0, in1=ff_e[:, :, :],
                                             op0=ALU.min, op1=ALU.subtract).then_inc(logf_made, 1)
                if u == ("v", NT - 1):
                    empty_turn(("cum", 0))
                if n >= 1 and units[n - 1] in stage_no and not by_act(units[n - 1]):
                    empty_turn(units[n - 1])
                if t == NT - 1 and b in ("ffcq", "v", "k"):
                    w_low(BLOCK_ORDER[BLOCK_ORDER.index(b) + 2])
            empty_turn(units[-1])

            def attend(ph):
                g0 = ph * UNITS

                def row_max(g):
                    dve.wait_ge(scored, g + 1)
                    dve.tensor_reduce(nmax[g % PROBS][:, :], unit_scores(g), X, ALU.max, negate=True
                                      ).then_inc(maxed, 1)

                for g in range(g0, g0 + AHEAD):
                    row_max(g)
                for g in range(g0, g0 + UNITS):
                    n = P * (g % NT + 1)
                    dve.wait_ge(p_turned, g + 1)
                    dve.tensor_copy(pT[g % 2][:, 0:g % NT + 1, :].rearrange("p c n -> p (c n)"),
                                    ps[:, 6 + g % 2, 0:n]).then_inc(p_copied, 1)
                    if g >= 2:
                        dve.wait_ge(o_done, g - 1)
                    dve.reciprocal(prinv[g % 2][:, :], psums[g % PROBS][:, :]).then_inc(sums_inv, 1)
                    if g + AHEAD < g0 + UNITS:
                        row_max(g + AHEAD)

            attend(0)

            def rotate(dst1, dst2, a1, a2, cos, sin, tmp):
                dve.tensor_tensor(tmp[0], a1, cos, ALU.mult)
                dve.tensor_tensor(tmp[1], a2, sin, ALU.mult)
                dve.tensor_tensor(tmp[2], a1, sin, ALU.mult)
                step(dve.tensor_tensor(tmp[3], a2, cos, ALU.mult))
                dve.tensor_tensor(dst1, tmp[0], tmp[1], ALU.subtract)
                return dve.tensor_tensor(dst2, tmp[2], tmp[3], ALU.add)

            dve.wait_ge(late_in, LATE * 16)
            step(dve.tensor_tensor(krg[:, :, :], kr[:, :, :], gr_k[:, :].unsqueeze(1).to_broadcast([P, NT + 1, ROPE]),
                                   ALU.mult))
            step(rotate(krr[:, :, 0:HALF], krr[:, :, HALF:], krg[:, :, 0:HALF], krg[:, :, HALF:],
                        rope_cs[:, :, 0:HALF], rope_cs[:, :, HALF:], [krt[:, j, :, :] for j in range(4)]))
            for n, (kind, t) in enumerate(up_units):
                r = rows(t)
                b0 = 2 * (n % 2)
                st = st_mla[n % 2]
                dve.wait_ge(up_squares, n + 1)
                if kind == "kv":
                    step(dve.tensor_reduce(ss[n % 2][0:r, :],
                                           sq[n % 2][0:r, 0:H * NOPE].rearrange("p (h c) -> p h c", h=H), X, ALU.add))
                    dve.tensor_scalar(ss[n % 2][0:r, :], ss[n % 2][0:r, :], kr_ss[0:r, t:t + 1], None, ALU.add
                                      ).then_inc(up_sums, 1)
                else:
                    dve.tensor_reduce(ss[n % 2][0:r, :], sq[n % 2][0:r, :].rearrange("p (h c) -> p h c", h=H), X,
                                      ALU.add).then_inc(up_sums, 1)
                dve.wait_ge(up_roots, n + 1)
                step(dve.reciprocal(rinv[n % 2][0:r, :], root[n % 2][0:r, :]))
                if n >= 2:
                    dve.wait_ge(up_turned, n - 1)
                if kind == "kv":
                    kv = pair(b0, KVUP)[0:r, :].rearrange("p (h c) -> p h c", h=H)
                    dve.tensor_tensor(st[0:r, :, NOPE:], krr[0:r, t, :].unsqueeze(1).to_broadcast([r, H, ROPE]),
                                      rinv[n % 2][0:r, :].unsqueeze(2).to_broadcast([r, H, ROPE]), ALU.mult)
                    dve.tensor_tensor(st[0:r, :, 0:NOPE], kv[:, :, 0:NOPE],
                                      rinv[n % 2][0:r, :].unsqueeze(2).to_broadcast([r, H, NOPE]), ALU.mult
                                      ).then_inc(up_staged, 1)
                else:
                    hh = H // 2
                    step(dve.tensor_tensor(
                        st[:, :, :].rearrange("p (j h) c -> p j h c", j=2),
                        ps[:, b0:b0 + 2, 0:QUP // 2].rearrange("p j (h c) -> p j h c", h=hh),
                        rinv[n % 2][:, :].rearrange("p (j h) -> p j h", j=2).unsqueeze(3)
                        .to_broadcast([P, 2, hh, MQK]), ALU.mult))
                    step(dve.tensor_tensor(rope_g[:, :, :], st[:, :, NOPE:],
                                           gr_q[:, :].unsqueeze(1).to_broadcast([P, H, ROPE]), ALU.mult))
                    rotate(st[:, :, NOPE:NOPE + HALF], st[:, :, NOPE + HALF:], rope_g[:, :, 0:HALF],
                           rope_g[:, :, HALF:], rope_cs[:, t, 0:HALF].unsqueeze(1).to_broadcast([P, H, HALF]),
                           rope_cs[:, t, HALF:].unsqueeze(1).to_broadcast([P, H, HALF]),
                           [rope_t[:, j, :, :] for j in range(4)]).then_inc(up_staged, 1)

            attend(1)

            def mix_inverse(i):
                dve.wait_ge(mix_roots, i + 1)
                dve.reciprocal(rinv[i % 2][:, 0:2], root[i % 2][:, 0:2]).then_inc(mix_inv, 1)

            def gained(dst, bank0, gain, signal):
                for q in range(2):
                    k0 = q * DK // 2
                    ins = dve.tensor_tensor(
                        dst[:, k0:k0 + DK // 2, :],
                        ps[:, bank0 + q, :].rearrange("p (k n) -> p k n", k=DK // 2),
                        gain[:, k0:k0 + DK // 2].unsqueeze(2).to_broadcast([P, DK // 2, P]), ALU.mult)
                ins.then_inc(signal, 1)

            def mix_empty(i):
                dve.wait_ge(mix_turned, i + 1)
                if i >= 1:
                    dve.wait_ge(wo_done, i)
                gained(mixT, 4, g_mix, mix_out)

            def residual(i):
                dve.wait_ge(wo_done, i + 1)
                dve.tensor_tensor(x[:, i, :], x[:, i, :], pair(0, D), ALU.add).then_inc(h_made, 1)
                dve.wait_ge(h_roots, i + 1)
                dve.reciprocal(rinv[i % 2][:, 2:3], root[i % 2][:, 2:3]).then_inc(h_inv, 1)

            def route(i):
                dve.wait_ge(u2_turned, i + 1)
                if i >= 1:
                    dve.wait_ge(logits_done, i)
                gained(u2T, 6, g_ffn, u2_out)
                dve.wait_ge(logits_done, i + 1)
                dve.tensor_tensor(lg[:, 0:NG], ps[:, 2, 0:NG], b_route[:, 0:NG], ALU.add)
                step(dve.tensor_tensor(lg[:, 8:8 + NE], ps[:, 2, NG:ROUTE], b_route[:, NG:], ALU.add))
                step(dve.max(gtop[:, :], lg[:, 0:8]))
                dve.tensor_scalar(wt[:, 0:1], gtop[:, 0:1], -1.0, None, ALU.mult).then_inc(gmax_made, 1)
                step(dve.max_index(gidx[:, :], gtop[:, :], lg[:, 0:8]))
                step(dve.tensor_copy(gf[:, 0:1], gidx[:, 0:1]))
                step(dve.tensor_scalar(ghot[:, :], iota_f[:, 0:NG], gf[:, 0:1], None, ALU.is_equal))
                step(dve.tensor_tensor(gprod[:, :, :], lg[:, 8:8 + NE].rearrange("p (g e) -> p e g", g=NG),
                                       ghot[:, :].unsqueeze(1).to_broadcast([P, EPG, NG]), ALU.mult))
                step(dve.tensor_reduce(within[:, :], gprod[:, :, :], X, ALU.add))
                step(dve.max(etop[:, :], within[:, :]))
                dve.tensor_tensor(wt[:, 3:4], etop[:, 1:2], etop[:, 0:1], ALU.subtract).then_inc(gap_made, 1)
                step(dve.max_index(eidx[:, :], etop[:, :], within[:, :]))
                step(dve.tensor_copy(esel[:, :], eidx[:, 0:2]))
                dve.tensor_scalar(gf[:, 1:2], gf[:, 0:1], float(EPG), None, ALU.mult).then_inc(dve_gf, 1)
                dve.wait_ge(dve_gf, i + 1)
                step(dve.tensor_scalar(esels[:, i, :], esel[:, :], gf[:, 1:2], None, ALU.add))
                for k in range(2):
                    ins = dve.tensor_scalar(ehots[:, i, k, :], iota_f[:, :], esels[:, i, k:k + 1], None,
                                            ALU.is_equal)
                step(ins)
                dve.tensor_tensor(picks[:, i, :], ehots[:, i, 0, :], ehots[:, i, 1, :], ALU.add
                                  ).then_inc(picks_made, 1)
                dve.wait_ge(gexp_made, i + 1)
                dve.wait_ge(gap_exp, i + 1)
                step(dve.tensor_scalar(wt[:, 5:6], wt[:, 4:5], 1.0, None, ALU.add))
                step(dve.tensor_tensor(wt[:, 6:7], wt[:, 5:6], wt[:, 1:2], ALU.mult))
                step(dve.reciprocal(coef[:, i, 0:1], wt[:, 6:7]))
                step(dve.tensor_tensor(coef[:, i, 1:2], coef[:, i, 0:1], wt[:, 4:5], ALU.mult))

            def positions(i):
                dve.wait_ge(ranked, i + 1)
                step(dve.tensor_tensor(rprod[:, :, :], ehots[:, i, :, :],
                                       ps[:, 3, 0:NE].unsqueeze(1).to_broadcast([P, 2, NE]), ALU.mult))
                step(dve.tensor_reduce(ranks_all[:, i, :], rprod[:, :, :], X, ALU.add))
                dve.scalar_tensor_tensor(out=pos_t[:, i, :], in0=ranks_all[:, i, :], scalar=float(NE),
                                         in1=esels[:, i, :], op0=ALU.mult, op1=ALU.add)
                dve.scalar_tensor_tensor(out=pos_y[:, i, :], in0=esels[:, i, :], scalar=float(slots),
                                         in1=ranks_all[:, i, :], op0=ALU.mult, op1=ALU.add).then_inc(pos_made, 1)

            mix_inverse(0)
            mix_empty(0)
            for i in range(NT):
                if i + 1 < NT:
                    mix_inverse(i + 1)
                residual(i)
                if i + 1 < NT:
                    mix_empty(i + 1)
                if i >= 1:
                    route(i - 1)
                if i >= 2:
                    positions(i - 2)
            positions(NT - 2)
            route(NT - 1)
            positions(NT - 1)
            dve.wait_ge(counted, 1)
            step(dve.tensor_reduce(most[:, :], ps[:, 3, 0:NE], X, ALU.max))
            dve.tensor_scalar(over[:, :], most[:, :], float(slots), None, ALU.is_gt).then_inc(over_made, 1)

            def dve_turned(it, s, first):
                e = it * RING + s
                b = s % 2
                dve.wait_ge(xt_done, e + 1)
                if not first or s >= 2:
                    dve.wait_ge(h13_done, e - 1)
                dve.tensor_tensor(xt[b][:, :, :], ps[:, b, 0:DK * slots].rearrange("p (k n) -> p k n", k=DK),
                                  g_ffn[:, :].unsqueeze(2).to_broadcast([P, DK, slots]), ALU.mult
                                  ).then_inc(xt_out, 1)

            def dve_gate(it, s, first):
                e = it * RING + s
                b = s % 2
                dve.wait_ge(silu_done, e + 1)
                if not first or s >= 2:
                    dve.wait_ge(y_done, e - 1)
                dve.tensor_tensor(hT[b][:, :, :], sil[b][:, :, :],
                                  ps[:, 2 + b, FK * slots:2 * FK * slots].rearrange("p (m n) -> p m n", m=FK),
                                  ALU.mult).then_inc(hT_made, 1)

            def dve_expert(it, s, first=False, last=False):
                dve_gate(it, s, first)
                if not (last and s == RING - 1):
                    if s == RING - 1:
                        dve_turned(it + 1, 0, False)
                    else:
                        dve_turned(it, s + 1, first)

            dve_turned(0, 0, True)
            for s in range(RING):
                dve_expert(0, s, first=True)
            with dve.Fori(1, NE // RING - 1) as it:
                for s in range(RING):
                    dve_expert(it, s)
            for s in range(RING):
                dve_expert(NE // RING - 1, s, last=True)

            tripped = dve.value_load(over[0:1, 0:1], min_val=0, max_val=1)
            with dve.If(tripped > 0):
                dve.tensor_scalar(late[:, 0, :, :], ranks_all[:, :, :], float(slots), None, ALU.is_ge)
                step(dve.tensor_scalar(late[:, 1, :, :], esels[:, :, :], float(REST - slots), float(MAIN - slots),
                                       ALU.mult, ALU.add))
                step(dve.tensor_tensor(late[:, 0, :, :], late[:, 0, :, :], late[:, 1, :, :], ALU.mult))
                step(dve.scalar_tensor_tensor(out=late[:, 1, :, :], in0=esels[:, :, :], scalar=float(slots),
                                              in1=ranks_all[:, :, :], op0=ALU.mult, op1=ALU.add))
                dve.tensor_tensor(pos_y[:, :, :], late[:, 0, :, :], late[:, 1, :, :], ALU.add).then_inc(fb_pos, 1)
                dve.wait_ge(y_done, NE)
                with dve.Fori(0, NE) as e:
                    with dve.Fori(1, SEQ // slots) as c:
                        n = e * (SEQ // slots - 1) + c
                        dve.wait_ge(fb_xt, n)
                        dve.tensor_tensor(xt[0][:, :, :],
                                          ps[:, 0, 0:DK * slots].rearrange("p (k n) -> p k n", k=DK),
                                          g_ffn[:, :].unsqueeze(2).to_broadcast([P, DK, slots]), ALU.mult
                                          ).then_inc(fb_xt_out, 1)
                        dve.wait_ge(fb_silu, n)
                        dve.tensor_tensor(hT[0][:, :, :], sil[0][:, :, :],
                                          ps[:, 2, FK * slots:2 * FK * slots].rearrange("p (m n) -> p m n", m=FK),
                                          ALU.mult).then_inc(fb_hT, 1)

            for t in range(NT):
                for k in range(2):
                    n = 2 * t + k
                    dve.wait_ge(yg_in[n % 4], 16 * (n // 4 + 1))
                    if k == 1:
                        dve.wait_ge(yg_used, n)
                    ins = dve.scalar_tensor_tensor(out=x[:, t, :], in0=yg[n % 4][:, :],
                                                   scalar=coef[:, t, k:k + 1], in1=x[:, t, :], op0=ALU.mult,
                                                   op1=ALU.add)
                    ins.then_inc(out_made if k == 1 else yg_used, 1)
                    if k == 1:
                        dve.wait_ge(out_made, t + 1)
                        dve.sem_inc(yg_used, 1)

        @block.tensor
        def _(pe):
            pe.wait_ge(ident_made, 1)

            def keep_warm(bank, count):
                for _ in range(count):
                    pe.matmul(ps[:, bank, :], identb[:, :], onesb[:, :].unsqueeze(1).to_broadcast([P, 4, P]),
                              start=True, stop=True)

            def turn(u):
                n = turn_no[u]
                b, t = u
                r = rows(t)
                b0 = 4 + 2 * (n % 2)
                turn_freed(pe, n)
                if b == "cum":
                    pe.wait_ge(logf_made, 1)
                    pe.wait_ge(masks_made, 8)
                    for t in TOKEN_TILES:
                        dst = ps[:, b0, t * H:(t + 1) * H]
                        earlier = [] if t == MT else [MT] + list(range(t))
                        for s in earlier:
                            pe.matmul(dst, ones[0:rows(s), :], logf[0:rows(s), s, :], start=(s == MT), stop=False)
                        ins = pe.matmul(dst, tri[:, :], logf[:, t, :], start=not earlier, stop=True)
                    ins.then_inc(turned, 1)
                    return
                if b == "x":
                    j = TOKEN_TILES.index(t)
                    pe.wait_ge(xs_made, j + 1)
                    for k in range(DK):
                        q, kk = divmod(k, DK // 2)
                        ins = pe.transpose(ps[:, b0 + q, kk * r:(kk + 1) * r], xs[j % 2][0:r, k, :],
                                           ident[0:r, 0:r])
                    ins.then_inc(turned, 1)
                    return
                m = stage_no[u]
                pe.wait_ge(staged_done, m + 1)
                if b in ("k", "q"):
                    for h in range(H):
                        ins = pe.transpose(pair(b0, H * r)[0:FOX_AUG, h * r:(h + 1) * r], st_fox[m % 2][0:r, h, :],
                                           ident[0:r, 0:r])
                else:
                    for k in range(KVRK if b == "ckv" else QRK):
                        ins = pe.transpose(ps[:, b0, k * r:(k + 1) * r], st_lat[m % 2][0:r, k, :],
                                           ident[0:r, 0:r])
                ins.then_inc(turned, 1)

            def project(u):
                n = unit_no[u]
                b, t = u
                c0, w = BLOCKS[b]
                if u == ("ffcq", MT):
                    w = H
                    pe.wait_ge(u_lo_made, len(TOKEN_TILES))
                if n >= 4:
                    unit_emptied(pe, n - 4)
                done = 2 * split_order.index(b)
                for p, (ua, wa) in enumerate(((uT_hi, w_hi), (uT_lo, w_hi), (uT_hi, w_lo))):
                    for k in range(DK):
                        if k % (DK // 2) == 0 and t == MT and p != 1:
                            pe.wait_ge(w_lo_made if p else w_hi_made, done + k // (DK // 2) + 1)
                        elif k == 0 and b == "q" and t == 0 and p != 1:
                            pe.wait_ge(w_lo_made if p else w_hi_made, done + 2)
                        ins = pe.matmul(ps[0:rows(t), n % 4, 0:w], ua[:, k, cols(t)], wa[b][:, k, 0:w],
                                        start=(k == 0 and p == 0), stop=(k == DK - 1 and p == 2))
                ins.then_inc(projected, 1)

            for what, u in steps:
                if u == steps[-1][1] and what == "turn":
                    unit_emptied(pe, len(units) - 4)
                    keep_warm((len(units) - 4) % 4, 14)
                turn(u) if what == "turn" else project(u)

            def attend(ph):
                g0 = ph * UNITS
                depth = FOX_AUG if ph == 0 else MQK

                def score(g):
                    h, i = g % UNITS // NT, g % NT
                    b0, n = score_bank(g), META + P * (i + 1)
                    q = qT[0:depth, h, i * P:(i + 1) * P]
                    if bank_user_before(g) >= g0:
                        pe.wait_ge(o_done, bank_user_before(g) + 1)
                    for c0 in range(0, n, 512):
                        c1 = min(n, c0 + 512)
                        m0 = max(c0, n - P)
                        pe.matmul(ps[:, b0 + c0 // 512, 0:c1 - c0], q, kT[0:depth, h, c0:c1], start=True,
                                  stop=False)
                        ins = pe.matmul(ps[:, b0 + c0 // 512, m0 - c0:c1 - c0], identb[:, :],
                                        causal[:, m0 - (n - P):c1 - (n - P)], start=False, stop=True)
                    ins.then_inc(scored, 1)

                def turn_probs(g):
                    pe.wait_ge(exped, g + 1)
                    if g >= 2:
                        pe.wait_ge(p_copied, g - 1)
                    pr = probs[g % PROBS]
                    pe.transpose(ps[0:META, score_bank(g), 0:P], pr[:, 0:META], ident[:, :]
                                 ).then_inc(pm_turned, 1)
                    for c in range(g % NT + 1):
                        ins = pe.transpose(ps[:, 6 + g % 2, c * P:(c + 1) * P],
                                           pr[:, META + c * P:META + (c + 1) * P], ident[:, :])
                    ins.then_inc(p_turned, 1)

                def apply(g):
                    h, i = g % UNITS // NT, g % NT
                    dst = ps[:, score_bank(g), P:P + HD]
                    pe.wait_ge(pm_copied, g + 1)
                    pe.matmul(dst, pT[g % 2][0:META, NT, :], vals[0:META, NT, h * HD:(h + 1) * HD],
                              start=True, stop=False)
                    pe.wait_ge(p_copied, g + 1)
                    for c in range(i + 1):
                        ins = pe.matmul(dst, pT[g % 2][:, c, :], vals[:, c, h * HD:(h + 1) * HD],
                                        start=False, stop=(c == i))
                    ins.then_inc(pv_done, 1)

                for g in range(g0, g0 + AHEAD):
                    score(g)
                for g in range(g0, g0 + UNITS):
                    turn_probs(g)
                    if g > g0:
                        apply(g - 1)
                    if g + AHEAD < g0 + UNITS:
                        score(g + AHEAD)
                apply(g0 + UNITS - 1)

            for n in range(len(units) - 4, len(units)):
                unit_emptied(pe, n)
            pe.wait_ge(v_copied, len(TOKEN_TILES))
            pe.wait_ge(turn_act, sum(by_act(u) for u in turns))
            pe.wait_ge(turn_dve, sum(not by_act(u) for u in turns))
            attend(0)

            pe.wait_ge(wup_in, 32)
            pe.wait_ge(o_done, UNITS)
            pe.wait_ge(p_copied, UNITS)

            def turn_up(n):
                kind, t = up_units[n]
                r = rows(t)
                pe.wait_ge(up_staged, n + 1)
                if n >= 2:
                    pe.wait_ge(up_out, n - 1)
                for h in range(H):
                    ins = pe.transpose(pair(4 + 2 * (n % 2), H * r)[0:MQK, h * r:(h + 1) * r],
                                       st_mla[n % 2][0:r, h, :], ident[0:r, 0:r])
                ins.then_inc(up_turned, 1)

            for n, (kind, t) in enumerate(up_units):
                r = rows(t)
                b0 = 2 * (n % 2)
                if n >= 2:
                    pe.wait_ge(up_staged, n - 1)
                    pe.wait_ge(up_vals, min(n - 1, len(TOKEN_TILES)))
                src, w, kk, nn = (ckvT, w_ukv, KVRK, KVUP // 2) if kind == "kv" else (cqT, w_uq, QRK, QUP // 2)
                for j in range(2):
                    for k in range(kk):
                        ins = pe.matmul(ps[0:r, b0 + j, 0:nn], src[:, k, cols(t)], w[:, k, j * nn:(j + 1) * nn],
                                        start=(k == 0), stop=(k == kk - 1))
                ins.then_inc(up_done, 1)
                if n >= 1:
                    turn_up(n - 1)
            turn_up(NU - 1)
            pe.wait_ge(up_vals, len(TOKEN_TILES))
            pe.wait_ge(up_out, NU)
            attend(1)

            def turn_mix(i):
                pe.wait_ge(mix_made, i + 1)
                if i >= 1:
                    pe.wait_ge(mix_out, i)
                else:
                    pe.wait_ge(p_copied, 2 * UNITS)
                    pe.wait_ge(o_done, 2 * UNITS)
                for k in range(DK):
                    q, kk = divmod(k, DK // 2)
                    ins = pe.transpose(ps[:, 4 + q, kk * P:(kk + 1) * P], mixn[:, k, :], ident[:, :])
                ins.then_inc(mix_turned, 1)

            def out_project(i):
                pe.wait_ge(mix_out, i + 1)
                if i >= 1:
                    pe.wait_ge(h_made, i)
                for q in range(2):
                    for k in range(DK):
                        ins = pe.matmul(ps[:, q, :], mixT[:, k, :], wo_chunk(k)[:, q * 512:(q + 1) * 512],
                                        start=(k == 0), stop=(k == DK - 1))
                ins.then_inc(wo_done, 1)

            def turn_u2(i):
                pe.wait_ge(u2_made, i + 1)
                if i >= 1:
                    pe.wait_ge(u2_out, i)
                for k in range(DK):
                    q, kk = divmod(k, DK // 2)
                    ins = pe.transpose(ps[:, 6 + q, kk * P:(kk + 1) * P], u2n[i % 2][:, k, :], ident[:, :])
                ins.then_inc(u2_turned, 1)

            def router(i):
                pe.wait_ge(u2_out, i + 1)
                if i >= 1:
                    pe.wait_ge(picks_made, i)
                for k in range(DK):
                    ins = pe.matmul(ps[:, 2, 0:ROUTE], u2T[:, k, :], w_route[:, k, :], start=(k == 0),
                                    stop=(k == DK - 1))
                ins.then_inc(logits_done, 1)

            def ranks(i):
                pe.wait_ge(picks_made, i + 1)
                if i >= 1:
                    pe.wait_ge(pos_made, i)
                for s in range(i):
                    pe.matmul(ps[:, 3, 0:NE], onesb[:, :], picks[:, s, :], start=(s == 0), stop=False)
                pe.matmul(ps[:, 3, 0:NE], before[:, :], picks[:, i, :], start=(i == 0), stop=True
                          ).then_inc(ranked, 1)

            pe.wait_ge(wo_in, 48)
            pe.wait_ge(route_in, 32)
            turn_mix(0)
            for i in range(NT):
                out_project(i)
                if i + 1 < NT:
                    turn_mix(i + 1)
                if i >= 1:
                    turn_u2(i - 1)
                    router(i - 1)
                if i >= 2:
                    ranks(i - 2)
            ranks(NT - 2)
            turn_u2(NT - 1)
            router(NT - 1)
            ranks(NT - 1)
            pe.wait_ge(pos_made, NT)
            for s in range(NT):
                ins = pe.matmul(ps[:, 3, 0:NE], onesb[:, :], picks[:, s, :], start=(s == 0), stop=(s == NT - 1))
            ins.then_inc(counted, 1)

            def turn_rows(bank, src):
                for k in range(DK):
                    ins = pe.transpose(ps[:, bank, k * slots:(k + 1) * slots], src[:, k, :], ident[0:slots, 0:slots])
                return ins

            def first_products(bank, w, src):
                for j in range(2):
                    for m in range(FK):
                        dst = ps[:, bank, (j * FK + m) * slots:(j * FK + m + 1) * slots]
                        for k in range(DK):
                            ins = pe.matmul(dst, w[:, j, k, m * P:(m + 1) * P], src[:, k, :], start=(k == 0),
                                            stop=(k == DK - 1))
                return ins

            def second_product(bank, w, src):
                for q in range(2):
                    for m in range(FK):
                        ins = pe.matmul(ps[0:slots, bank + q, :], src[:, m, :], w[:, m, q * 512:(q + 1) * 512],
                                        start=(m == 0), stop=(m == FK - 1))
                return ins

            def turn_gathered(it, s, first):
                e = it * RING + s
                b = s % 2
                pe.wait_ge(xg_in[b], 16 * (RING // 2 * it + s // 2 + 1))
                if not first or s >= 2:
                    pe.wait_ge(xt_out, e - 1)
                pe.sem_inc(waits_ended, 1)
                turn_rows(b, xg[b]).then_inc(xt_done, 1)

            def expand(it, s, first=False):
                e = it * RING + s
                b = s % 2
                pe.wait_ge(xt_out, e + 1)
                pe.wait_ge(w13_in[s], 32 * (it + 1))
                if not first or s >= 2:
                    pe.wait_ge(hT_made, e - 1)
                first_products(2 + b, w13[s], xt[b]).then_inc(h13_done, 1)

            def contract(it, s, first=False):
                e = it * RING + s
                b = s % 2
                pe.wait_ge(hT_made, e + 1)
                pe.wait_ge(w2_in[s], 16 * (it + 1))
                if not first or s >= 2:
                    pe.wait_ge(y_copied, e - 1)
                second_product(4 + 2 * b, w2s[s], hT[b]).then_inc(y_done, 1)

            def pe_expert(it, s, first=False, last=False):
                expand(it, s, first)
                if s < RING - 1:
                    turn_gathered(it, s + 1, first)
                elif not last:
                    turn_gathered(it + 1, 0, False)
                if s >= 1:
                    contract(it, s - 1, first)
                elif not first:
                    contract(it - 1, RING - 1)

            pe.wait_ge(over_made, 1)
            turn_gathered(0, 0, True)
            for s in range(RING):
                pe_expert(0, s, first=True)
            with pe.Fori(1, NE // RING - 1) as it:
                for s in range(RING):
                    pe_expert(it, s)
            for s in range(RING):
                pe_expert(NE // RING - 1, s, last=True)
            contract(NE // RING - 1, RING - 1)

            tripped = pe.value_load(over[0:1, 0:1], min_val=0, max_val=1)
            with pe.If(tripped > 0):
                pe.wait_ge(y_copied, NE)
                with pe.Fori(0, NE) as e:
                    with pe.Fori(1, SEQ // slots) as c:
                        n = e * (SEQ // slots - 1) + c
                        pe.wait_ge(fb_xg, n * 16)
                        pe.sem_inc(waits_ended, 1)
                        turn_rows(0, xg[0]).then_inc(fb_xt, 1)
                        pe.wait_ge(fb_xt_out, n)
                        pe.wait_ge(fb_w, n * 48)
                        first_products(2, w13[0], xt[0]).then_inc(fb_h13, 1)
                        pe.wait_ge(fb_hT, n)
                        second_product(4, w2s[0], hT[0]).then_inc(fb_y, 1)


_INS = ['x', 'meta_tokens', 'g_attn', 'w_in', 'b_f', 'g_fox_q', 'g_fox_k', 'g_q_lat', 'w_uq', 'g_kv_lat', 'w_ukv',
        'g_mla_q', 'g_mla_k', 'g_fox_out', 'g_mla_out', 'w_o', 'g_ffn', 'w_group', 'b_group', 'w_expert',
        'b_expert', 'w1', 'w3', 'w2']


def rope_table():
    import numpy as np
    inv = np.exp(-np.float32(np.log(10000.0)) * np.arange(HALF, dtype=np.float32) / np.float32(HALF))
    ang = np.arange(L, dtype=np.float32)[:, None] * inv.astype(np.float32)[None, :]
    by_pos = np.concatenate([np.cos(ang), np.sin(ang)], axis=1).astype(np.float32)
    return np.concatenate([by_pos[META:], by_pos[:META], np.zeros((P - META, ROPE), np.float32)])


def kernel(**inputs):
    import numpy as _np
    import concourse.bacc as _bacc
    from concourse import mybir as _mybir
    from concourse.bass_utils import run_bass_kernel_spmd as _run

    nc = _bacc.Bacc("TRN2", target_bir_lowering=False, num_devices=1)
    arrays, args = {}, {}
    for name in _INS:
        v = _np.ascontiguousarray(inputs[name])
        arrays[f"in_{name}"] = v
        args[name] = nc.dram_tensor(f"in_{name}", v.shape, _mybir.dt.from_np(v.dtype), kind="ExternalInput").ap()
    arrays["in_rope"] = rope_table()
    args["rope"] = nc.dram_tensor("in_rope", arrays["in_rope"].shape, F32, kind="ExternalInput").ap()
    out = nc.dram_tensor("out_0", (1, SEQ, D), F32, kind="ExternalOutput").ap()
    build(nc, args, out)
    r = _run(nc, [arrays], core_ids=[0])
    return r.results[0]["out_0"]
```

```python
from contextlib import ExitStack

import concourse.bass as bass
from concourse import mybir

F32 = mybir.dt.float32
F32R = mybir.dt.float32r
BF16 = mybir.dt.bfloat16
I32 = mybir.dt.int32
U32 = mybir.dt.uint32
ALU = mybir.AluOpType
ACT = mybir.ActivationFunctionType
X = mybir.AxisListType.X

P = 128
EPS = 1e-6
NEG = -1e30
ARENA = 16512

D = 1024
SEQ = 512
META = 16
L = SEQ + META
NT = SEQ // P
MT = NT
TOKEN_TILES = [MT] + list(range(NT))
DK = D // P

H = 8
HD = 64
FOX = H * HD
FOX_AUG = HD + 2
QR = 384
KVR = 256
ROPE = 32
HALF = ROPE // 2
NOPE = 64
MQK = NOPE + ROPE
MLA = H * HD
QRK = QR // P
KVRK = KVR // P
QUP = H * MQK
KVUP = H * (NOPE + HD)
IN_COLS = 3 * FOX + H + QR + KVR + ROPE

NG = 4
EPG = 8
NE = NG * EPG
F = 256
FK = F // P
SLOTS = 64
RING = 4
ROUTE = NG + NE

BLOCKS = {
    "ffcq": (3 * FOX, H + QR),
    "v": (2 * FOX, FOX),
    "k": (FOX, FOX),
    "q": (0, FOX),
    "ckv": (3 * FOX + H + QR, KVR + ROPE),
}
BLOCK_ORDER = ["ffcq", "v", "k", "q", "ckv"]


def rows(t):
    return META if t == MT else P


def cols(t):
    return slice(t * P, t * P + rows(t))


def key_cols(t):
    return slice(0, META) if t == MT else slice(META + t * P, META + (t + 1) * P)


def projection_plan():
    units = [(b, t) for b in BLOCK_ORDER for t in TOKEN_TILES if not (b == "q" and t == MT)]
    turned = lambda u: u[0] in ("k", "q", "ckv") or (u[0] == "ffcq" and u[1] != MT)
    steps = [("turn", ("x", t)) for t in TOKEN_TILES]
    for n, u in enumerate(units):
        steps.append(("project", u))
        if n >= 1 and turned(units[n - 1]):
            steps.append(("turn", units[n - 1]))
        if u == ("v", NT - 1):
            steps.append(("turn", ("cum", 0)))
    steps.append(("turn", units[-1]))
    turns = [u for what, u in steps if what == "turn"]
    return units, steps, turns


def build(nc, a, out, slots=SLOTS):
    units, steps, turns = projection_plan()
    unit_no = {u: n for n, u in enumerate(units)}
    turn_no = {u: n for n, u in enumerate(turns)}
    by_act = lambda u: u[0] in ("k", "q")
    staged = [u for u in turns if u[0] not in ("x", "cum")]
    stage_no = {u: n for n, u in enumerate(staged)}
    headed = [u for u in units if u[0] in ("k", "q")]
    head_no = {u: n for n, u in enumerate(headed)}
    rooted = [("x", t) for t in TOKEN_TILES] + [u for u in units if u in headed or u in staged]
    root_no = {u: n for n, u in enumerate(rooted)}

    up_units = [("kv", t) for t in TOKEN_TILES] + [("uq", t) for t in range(NT)]
    NU = len(up_units)
    UNITS = H * NT
    TILE_ORDER = list(reversed(range(NT)))
    LAST = NT - 1

    with ExitStack() as ctx:
        sem_names = {}

        def sem(name):
            sem_names[name] = ctx.enter_context(nc.semaphore(name))
            return sem_names[name]

        end = [ARENA]

        def place(name, shape, dt, offset):
            return nc.alloc_sbuf_tensor_at(name, shape, dt, offset=offset)

        def region(size):
            start = end[0]
            end[0] = start + (size + 31) // 32 * 32
            return start

        def new(name, shape, dt=F32):
            n = 1
            for s in shape[1:]:
                n *= s
            return place(name, shape, dt, region(n * (2 if dt == BF16 else 4)))

        SLOT = (2 * DK * F + FK * D) * 4
        ring = region(RING * SLOT)
        w13 = [place(f"w13_{s}", [P, 2, DK, F], F32, ring + s * SLOT) for s in range(RING)]
        w2s = [place(f"w2_{s}", [P, FK, D], F32, ring + s * SLOT + 2 * DK * F * 4) for s in range(RING)]
        r_qk = ring + RING * SLOT + NT * D * 4
        block_bytes = {b: DK * BLOCKS[b][1] * 4 for b in BLOCK_ORDER}
        w_at, at = {}, ring + RING * SLOT
        for b in reversed(BLOCK_ORDER):
            at -= block_bytes[b]
            w_at[b] = at
        at -= DK * L * 4
        u_lo_at = w_at["q"] - DK * L * 4
        for b in ("ffcq", "v", "k"):
            w_at[b] -= DK * L * 4
        hi_at = {"ffcq": r_qk + D * 4, "v": r_qk + D * 4 + block_bytes["ffcq"], "k": ring,
                 "q": ring + block_bytes["k"], "ckv": w_at["k"]}
        assert at >= ring and ring + block_bytes["k"] <= w_at["v"]
        assert hi_at["q"] + block_bytes["q"] <= w_at["k"]
        w_in = {b: place(f"w_in_{b}", [P, DK, BLOCKS[b][1]], F32, w_at[b]) for b in BLOCK_ORDER}
        w_lo = {b: place(f"w_lo_{b}", [P, DK, BLOCKS[b][1]], F32R, w_at[b]) for b in BLOCK_ORDER}
        w_hi = {b: place(f"w_hi_{b}", [P, DK, BLOCKS[b][1]], F32R, hi_at[b]) for b in BLOCK_ORDER}
        u_full = place("u_full", [P, DK, L], F32, u_lo_at)
        uT_lo = place("uT_lo", [P, DK, L], F32R, u_lo_at)
        w2_lo = [place(f"w2_lo_{s}", [P, FK, D], F32R, ring + s * SLOT + 2 * DK * F * 4) for s in range(RING)]
        w_uq = place("w_uq", [P, QRK, QUP], F32, ring + 3 * SLOT)
        w_ukv = place("w_ukv", [P, KVRK, KVUP], F32, ring + 3 * SLOT + QRK * QUP * 4)
        WO_A = 6
        w_oa = place("w_oa", [P, WO_A, D], F32, ring + 2 * SLOT)

        x = new("x", [P, NT, D])
        assert region((NT * P + L) * H * 4) == r_qk
        xm = place("xm", [META, D], F32, r_qk)
        qT = place("qT", [MQK, H, SEQ], F32, r_qk)
        kT = place("kT", [MQK, H, L], F32, r_qk + H * SEQ * 4)
        tail = ring + 3 * SLOT
        mixn = place("mixn", [P, DK, P], F32, tail)
        mixT = place("mixT", [P, DK, P], F32, tail + 4096)
        u2n = [place(f"u2n{b}", [P, DK, P], F32, tail + 8192 + 4096 * b) for b in range(2)]
        u2T = place("u2T", [P, DK, P], F32, tail + 16384)
        xg = [place(f"xg{b}", [slots, DK, P], F32, r_qk + 20480 + 4096 * b) for b in range(2)]
        w2_hi = [place(f"w2_hi_{b}", [P, FK, D], F32R, r_qk + 8192 * b) for b in range(2)]
        yg = [place(f"yg{n}", [P, D], F32, r_qk + 4096 * n) for n in range(2 * NT)]

        r_v = region((NT + 1) * FOX * 4)
        vals = place("vals", [P, NT + 1, FOX], F32, r_v)
        xt = [place(f"xt{b}", [P, DK, slots], F32, r_v + 2048 * b) for b in range(2)]
        sil = [place(f"sil{b}", [P, FK, slots], F32, r_v + 4096 + 512 * b) for b in range(2)]
        hT_hi = [place(f"hT_hi{b}", [P, FK, slots], F32R, r_v + 5120 + 512 * b) for b in range(2)]
        hT_lo = [place(f"hT_lo{b}", [P, FK, slots], F32R, r_v + 6144 + 512 * b) for b in range(2)]

        r_u = region(DK * L * 4)
        uT_hi = place("uT_hi", [P, DK, L], F32R, r_u)
        o_all = place("o_all", [P, NT, D], F32, r_u)
        ysb = [place(f"ysb{b}", [slots, D], F32, r_u + 4096 * b) for b in range(2)]

        r_l = region((QRK * SEQ + KVRK * L) * 4)
        cqT = place("cqT", [P, QRK, SEQ], F32, r_l)
        ckvT = place("ckvT", [P, KVRK, L], F32, r_l + QRK * SEQ * 4)
        w_ob = place("w_ob", [P, DK - WO_A, D], F32, r_l)

        r_p = region(9344)
        xs = [place(f"xs{b}", [P, DK, P], F32, r_p + 4096 * b) for b in range(2)]
        sq = [place(f"sq{b}", [P, QUP], F32, r_p + 3072 * b) for b in range(2)]
        rope_g = place("rope_g", [P, H, ROPE], F32, r_p + 6144)
        rope_t = place("rope_t", [P, 4, H, HALF], F32, r_p + 7168)
        PROBS = 4
        probs = [place(f"probs{b}", [P, L], F32, r_p + L * 4 * b) for b in range(PROBS)]

        r_s = region(2 * QUP * 4)
        scrap = place("scrap", [P, D], F32, r_s)
        st_fox = [place(f"st_fox{b}", [P, H, FOX_AUG], F32, r_s + QUP * 4 * b) for b in range(2)]
        st_lat = [place(f"st_lat{b}", [P, QRK, P], F32, r_s + QUP * 4 * b) for b in range(2)]
        pT = [place(f"pT{b}", [P, NT + 1, P], F32, r_s + (NT + 1) * P * 4 * b) for b in range(2)]
        st_mla = [place(f"st_mla{b}", [P, H, MQK], F32, r_s + QUP * 4 * b) for b in range(2)]

        krg = place("krg", [P, NT + 1, ROPE], F32, r_p + 6144)
        krt = place("krt", [P, 4, NT + 1, HALF], F32, r_p + 6144 + (NT + 1) * ROPE * 4)

        ident = new("ident", [P, P])
        tri = new("tri", [P, P])
        ones = new("ones", [P, P])
        causal = new("causal", [P, P], BF16)
        identb = new("identb", [P, P], BF16)
        before = new("before", [P, P], BF16)
        onesb = new("onesb", [P, P], BF16)
        rope_cs = new("rope_cs", [P, NT + 1, ROPE])
        g_attn = new("g_attn_c", [P, DK])
        g_ffn = new("g_ffn_c", [P, DK])
        g_mix = new("g_mix_c", [P, DK])
        g_ql = new("g_ql_c", [P, QRK])
        g_kvl = new("g_kvl_c", [P, KVRK])
        gc_fox = [new("gc_foxq", [FOX_AUG, 1]), new("gc_foxk", [FOX_AUG, 1])]
        gc_mla = [new("gc_mlaq", [MQK, 1]), new("gc_mlak", [MQK, 1])]
        gr_q = new("gr_q", [P, ROPE])
        gr_k = new("gr_k", [P, ROPE])
        bf_b = new("bf_b", [P, H])
        ff = new("ff", [P, NT + 1, H])
        ff_e = new("ff_e", [P, NT + 1, H])
        logf = new("logf", [P, NT + 1, H])
        cum = new("cum", [P, NT + 1, H])
        kr = new("kr", [P, NT + 1, ROPE])
        krr = new("krr", [P, NT + 1, ROPE])
        kr_ss = new("kr_ss", [P, NT + 1])
        ss = [new(f"ss{b}", [P, H]) for b in range(2)]
        root = [new(f"root{b}", [P, H]) for b in range(2)]
        rinv = [new(f"rinv{b}", [P, H]) for b in range(2)]
        nmax = [new(f"nmax{b}", [P, 1]) for b in range(PROBS)]
        psums = [new(f"psums{b}", [P, 1]) for b in range(PROBS)]
        prinv = [new(f"prinv{b}", [P, 1]) for b in range(2)]
        junk = new("junk", [P, ROPE])
        w_route = new("w_route", [P, DK, ROUTE])
        b_route = new("b_route", [P, ROUTE])
        lg = new("lg", [P, NG + 4 + NE])
        gtop = new("gtop", [P, 8])
        gidx = new("gidx", [P, 8], U32)
        gf = new("gf", [P, 2])
        ghot = new("ghot", [P, NG])
        gprod = new("gprod", [P, EPG, NG])
        within = new("within", [P, EPG])
        etop = new("etop", [P, 8])
        eidx = new("eidx", [P, 8], U32)
        esel = new("esel", [P, 2])
        ehots = new("ehots", [P, NT, 2, NE])
        picks = new("picks", [P, NT, NE], BF16)
        rprod = new("rprod", [P, 2, NE])
        ranks_all = new("ranks_all", [P, NT, 2])
        late = new("late", [P, 2, NT, 2])
        esels = new("esels", [P, NT, 2])
        wt = new("wt", [P, 8])
        gexp = new("gexp", [P, NG])
        coef = new("coef", [P, NT, 2])
        pos_t = new("pos_t", [P, NT, 2], I32)
        pos_y = new("pos_y", [P, NT, 2], I32)
        tok = new("tok", [P, NT], I32)
        iota_i = new("iota_i", [P, NE], I32)
        iota_f = new("iota_f", [P, NE])
        zero_i = new("zero_i", [P, P], I32)
        idx = new("idx", [slots, NE], I32)
        fb_idx = new("fb_idx", [slots, 1], I32)
        most = new("most", [P, 1])
        eps_c = new("eps_c", [P, 1])
        over = new("over", [P, 1], I32)
        newton = new("newton", [P, 4])
        assert end[0] <= 229344

        ps = ctx.enter_context(nc.psum_tensor("ps", [P, 8, 512], F32))

        def pair(b, n):
            return ps[:, b:b + 2, :].rearrange("p a n -> p (a n)")[:, 0:n]

        u2_rows = nc.dram_tensor("u2_rows", [SEQ, D], F32).ap()
        table = nc.dram_tensor("table", [SEQ * NE, 1], I32).ap()
        MAIN = NE * slots
        REST = SEQ - slots
        y_rows = nc.dram_tensor("y_rows", [MAIN + NE * REST, D], F32).ap()

        consts_in, masks_made, vecs_made = sem("consts_in"), sem("masks_made"), sem("vecs_made")
        ident_made, early_in, late_in = sem("ident_made"), sem("early_in"), sem("late_in")
        eps_made, dve_gf = sem("eps_made"), sem("dve_gf")
        x_in = [sem(f"x_in{t}") for t in range(NT + 1)]
        win_in = {b: sem(f"win_in_{b}") for b in BLOCK_ORDER}
        wup_in, wo_in, route_in = sem("wup_in"), sem("wo_in"), sem("route_in")
        act_step, dve_step, pool_step = sem("act_step"), sem("dve_step"), sem("pool_step")
        roots_made, xs_made = sem("roots_made"), sem("xs_made")
        u_hi_made, u_lo_made, w_hi_made, w_lo_made = (sem("u_hi_made"), sem("u_lo_made"), sem("w_hi_made"),
                                                      sem("w_lo_made"))
        projected, v_copied, unit_freed = sem("projected"), sem("v_copied"), sem("unit_freed")
        squares_made, sums_made, staged_done = sem("squares_made"), sem("sums_made"), sem("staged_done")
        turned, turn_act, turn_dve = sem("turned"), sem("turn_act"), sem("turn_dve")
        ff_in, ff_abs, ff_log, ff_exp, logf_made = (sem("ff_in"), sem("ff_abs"), sem("ff_log"), sem("ff_exp"),
                                                    sem("logf_made"))
        up_done, up_squares, up_sums, up_roots = sem("up_done"), sem("up_squares"), sem("up_sums"), sem("up_roots")
        up_vals, up_staged, up_turned, up_out = sem("up_vals"), sem("up_staged"), sem("up_turned"), sem("up_out")
        scored, maxed, exped = sem("scored"), sem("maxed"), sem("exped")
        pm_turned, p_turned, pm_copied, p_copied = (sem("pm_turned"), sem("p_turned"), sem("pm_copied"),
                                                    sem("p_copied"))
        pv_done, sums_inv, o_done = sem("pv_done"), sem("sums_inv"), sem("o_done")
        mix_squares, mix_inv, mix_made, mix_turned, mix_out = (sem("mix_squares"), sem("mix_inv"), sem("mix_made"),
                                                    sem("mix_turned"), sem("mix_out"))
        logits_read = sem("logits_read")
        last_mix_root, last_mix_inv = sem("last_mix_root"), sem("last_mix_inv")
        last_h_root, last_h_inv = sem("last_h_root"), sem("last_h_inv")
        wo_done, h_made, h_squares, h_inv, u2_made = (sem("wo_done"), sem("h_made"), sem("h_squares"), sem("h_inv"),
                                                    sem("u2_made"))
        u2_stored = [sem(f"u2_stored{b}") for b in range(2)]
        u2_turned, u2_out, logits_done = sem("u2_turned"), sem("u2_out"), sem("logits_done")
        gmax_made, gexp_made, gap_made, gap_exp = (sem("gmax_made"), sem("gexp_made"), sem("gap_made"),
                                                   sem("gap_exp"))
        picks_made, ranked, pos_made, counted, over_made = (sem("picks_made"), sem("ranked"), sem("pos_made"),
                                                            sem("counted"), sem("over_made"))
        table_zeroed, table_filled, idx_in = sem("table_zeroed"), sem("table_filled"), sem("idx_in")
        w13_in = [sem(f"w13_in{s}") for s in range(RING)]
        w2_in = [sem(f"w2_in{s}") for s in range(RING)]
        xg_in = [sem(f"xg_in{b}") for b in range(2)]
        waits_ended = sem("waits_ended")
        xt_done, xt_out, h13_done, silu_done, hT_made = (sem("xt_done"), sem("xt_out"), sem("h13_done"),
                                                         sem("silu_done"), sem("hT_made"))
        y_done, y_copied = sem("y_done"), sem("y_copied")
        gated, hT_high, w2_hi_made, w2_lo_made = (sem("gated"), sem("hT_high"), sem("w2_hi_made"),
                                                  sem("w2_lo_made"))
        y_stored = [sem(f"y_stored{b}") for b in range(2)]
        fb_w, fb_idx_in, fb_xg, fb_xt, fb_xt_out, fb_h13, fb_silu, fb_hT, fb_y, fb_y_out, fb_stored = (
            sem(n) for n in ("fb_w", "fb_idx_in", "fb_xg", "fb_xt", "fb_xt_out", "fb_h13", "fb_silu", "fb_hT",
                             "fb_y", "fb_y_out", "fb_stored"))
        fb_pos, fb_blank, fb_zeroed = sem("fb_pos"), sem("fb_blank"), sem("fb_zeroed")
        yg_in = [sem(f"yg_in{n}") for n in range(2 * NT)]
        first_added, out_made, out_stored = sem("first_added"), sem("out_made"), sem("out_stored")

        x_tiles = a["x"][0].rearrange("(t p) d -> t p d", p=P)
        w_in_v = a["w_in"][0].rearrange("(p k) n -> p k n", k=DK)
        w_o_v = a["w_o"][0].rearrange("(g p k) n -> g p k n", g=2, k=DK // 2)
        w1_v = a["w1"][0].rearrange("e (p k) f -> e p k f", k=DK)
        w3_v = a["w3"][0].rearrange("e (p k) f -> e p k f", k=DK)
        w2_v = a["w2"][0].rearrange("e (m p) n -> e p m n", p=P)
        y_main = y_rows[0:MAIN, :].rearrange("(e r) d -> e r d", r=slots)
        y_over = y_rows[MAIN:, :].rearrange("(e r) d -> e r d", r=REST)
        y_over_tiles = y_rows[MAIN:, :].rearrange("(n p) d -> n p d", p=P)
        table_by_rank = table.rearrange("(r e) o -> r (e o)", e=NE)
        out_tiles = out[0].rearrange("(t p) d -> t p d", p=P)

        def wo_chunk(c):
            return w_oa[:, c, :] if c < WO_A else w_ob[:, c - WO_A, :]

        def unit(g):
            return g % H, TILE_ORDER[g % UNITS // H]

        AHEAD = 2
        MISC = 3
        ACCUM = 4

        def score_bank(g):
            j = g % UNITS
            if unit(g)[1] == NT - 1:
                return j % 3 * 2
            return (j - H + 4) % 6 if g < UNITS else (j - H) % 3

        def due(g):
            ahead = lambda u: 3 if H <= u < UNITS else AHEAD
            return [u for u in range(g + AHEAD, min(g // UNITS * UNITS + UNITS, g + 4)) if u - ahead(u) == g]

        def banks_of(g):
            return {score_bank(g), score_bank(g) + (unit(g)[1] == NT - 1)}

        def bank_user_before(g):
            return max((f for f in range(g) if banks_of(f) & banks_of(g)), default=-1)

        def output_apart(g):
            return g >= UNITS or unit(g)[1] == NT - 1

        def output_place(g):
            return ps[:, 6 + g % 2, P:P + HD] if output_apart(g) else ps[:, score_bank(g), P:P + HD]

        def unit_keys(g):
            return META + P * (unit(g)[1] + 1)

        def unit_scores(g):
            n = unit_keys(g)
            return pair(score_bank(g), n) if n > 512 else ps[:, score_bank(g), 0:n]

        def router_bank(p):
            return MISC if p < LAST - 1 else 2

        split_order = BLOCK_ORDER

        def stepper(eng, signal):
            count = [0]

            def step(instruction):
                count[0] += 1
                instruction.then_inc(signal, 1)
                eng.wait_ge(signal, count[0])

            return step

        def turn_freed(eng, n):
            if n < 2:
                return
            u = turns[n - 2]
            if by_act(u):
                eng.wait_ge(turn_act, sum(by_act(v) for v in turns[:n - 1]))
            else:
                eng.wait_ge(turn_dve, sum(not by_act(v) for v in turns[:n - 1]))

        def unit_emptied(eng, n):
            of_act = lambda u: u[0] == "v"
            if of_act(units[n]):
                eng.wait_ge(v_copied, sum(of_act(u) for u in units[:n + 1]))
            else:
                eng.wait_ge(unit_freed, sum(not of_act(u) for u in units[:n + 1]))

        block = ctx.enter_context(nc.Block())

        EARLY, LATE = 7, 8

        @block.sync
        def _(sp):
            sp.dma_start(xm[:, :], a["meta_tokens"]).then_inc(x_in[MT], 16)
            sp.dma_start(x[:, 0, :], x_tiles[0]).then_inc(x_in[0], 16)
            sp.dma_start(g_attn[:, :], a["g_attn"][0].rearrange("(p k) -> p k", k=DK)).then_inc(consts_in, 16)
            for t in range(1, NT):
                sp.dma_start(x[:, t, :], x_tiles[t]).then_inc(x_in[t], 16)
            for b in BLOCK_ORDER:
                c0, n = BLOCKS[b]
                if b == BLOCK_ORDER[1]:
                    sp.wait_ge(early_in, EARLY * 16)
                sp.dma_start(w_in[b][:, :, :], w_in_v[:, :, c0:c0 + n]).then_inc(win_in[b], 16)
            with nc.allow_non_contiguous_dma("router weights, 36 columns"):
                sp.dma_start(w_route[:, :, 0:NG], a["w_group"][0].rearrange("(p k) n -> p k n", k=DK)
                             ).then_inc(route_in, 16)
                sp.dma_start(w_route[:, :, NG:], a["w_expert"][0].rearrange("(p k) n -> p k n", k=DK)
                             ).then_inc(route_in, 16)

            def load_expert(s, e):
                sp.dma_start(w13[s][:, 0, :, :], w1_v[e]).then_inc(w13_in[s], 16)
                sp.dma_start(w13[s][:, 1, :, :], w3_v[e]).then_inc(w13_in[s], 16)
                sp.dma_start(w2s[s][:, :, :], w2_v[e]).then_inc(w2_in[s], 16)

            sp.wait_ge(projected, len(units))
            sp.dma_start(w_uq[:, :, :], a["w_uq"][0].rearrange("(p k) n -> p k n", k=QRK)).then_inc(wup_in, 16)
            sp.dma_start(w_ukv[:, :, :], a["w_ukv"][0].rearrange("(p k) n -> p k n", k=KVRK)).then_inc(wup_in, 16)
            load_expert(0, 0)
            load_expert(1, 1)
            sp.dma_start(w_oa[:, 0:4, :], w_o_v[0]).then_inc(wo_in, 16)
            sp.dma_start(w_oa[:, 4:6, :], w_o_v[1][:, 0:2, :]).then_inc(wo_in, 16)
            sp.wait_ge(up_done, NU)
            sp.dma_start(w_ob[:, :, :], w_o_v[1][:, 2:4, :]).then_inc(wo_in, 16)
            for p, i in enumerate(TILE_ORDER):
                if p == LAST:
                    sp.wait_ge(wo_done, 2 * NT)
                    load_expert(2, 2)
                sp.wait_ge(u2_made, p + 1)
                sp.dma_start(u2_rows[i * P:(i + 1) * P, :], u2n[p % 2][:, :, :].rearrange("p k n -> p (k n)")
                             ).then_inc(u2_stored[p % 2], 16)
            sp.wait_ge(table_filled, 2 * NT * 16)
            sp.dma_start(idx[:, :], table_by_rank[0:slots, :]).then_inc(idx_in, 16)
            for b in range(2):
                sp.wait_ge(xg_in[b], 16)
            sp.wait_ge(logits_done, NT)
            for b in range(2):
                sp.wait_ge(u2_stored[b], 16 * NT // 2)
            load_expert(3, 3)

            def load_w13(it, s):
                e = it * RING + s
                sp.wait_ge(h13_done, e - RING + 1)
                sp.dma_start(w13[s][:, 0, :, :], w1_v[e]).then_inc(w13_in[s], 16)
                sp.dma_start(w13[s][:, 1, :, :], w3_v[e]).then_inc(w13_in[s], 16)

            def load_w2(it, s):
                e = it * RING + s
                sp.wait_ge(y_done, e - RING + 1)
                sp.dma_start(w2s[s][:, :, :], w2_v[e]).then_inc(w2_in[s], 16)

            for s in range(RING):
                load_w13(1, s)
                if s >= 1:
                    load_w2(1, s - 1)
            with sp.Fori(2, NE // RING) as it:
                for s in range(RING):
                    load_w13(it, s)
                    if s >= 1:
                        load_w2(it, s - 1)
                    else:
                        load_w2(it - 1, RING - 1)
            load_w2(NE // RING - 1, RING - 1)

            sp.wait_ge(over_made, 1)
            tripped = sp.value_load(over[0:1, 0:1], min_val=0, max_val=1)
            with sp.If(tripped > 0):
                sp.wait_ge(y_done, NE)
                with sp.Fori(0, NE) as e:
                    with sp.Fori(1, SEQ // slots) as c:
                        n = e * (SEQ // slots - 1) + c
                        sp.dma_start(w13[0][:, 0, :, :], w1_v[e]).then_inc(fb_w, 16)
                        sp.dma_start(w13[0][:, 1, :, :], w3_v[e]).then_inc(fb_w, 16)
                        sp.dma_start(w2s[0][:, :, :], w2_v[e]).then_inc(fb_w, 16)
                        sp.wait_ge(fb_stored, n * 16)
                        sp.sem_inc(waits_ended, 1)

            for t in range(NT):
                sp.wait_ge(out_made, t + 1)
                sp.dma_start(out_tiles[t], x[:, t, :]).then_inc(out_stored, 16)
            sp.wait_ge(out_stored, NT * 16)

        @block.gpsimd
        def _(pool):
            step = stepper(pool, pool_step)
            step(pool.memset(ident[:, :], 0.0))
            pool.affine_select(out=ident[:, :], in_=ident[:, :], compare_op=ALU.not_equal, fill=1.0, base=0,
                               pattern=[[-1, P]], channel_multiplier=1).then_inc(ident_made, 1)
            with nc.allow_non_contiguous_dma("small vectors"):
                def early(dst, src):
                    pool.dma_start(dst, src).then_inc(early_in, 16)

                def late_const(dst, src):
                    pool.dma_start(dst, src).then_inc(late_in, 16)
                early(bf_b[:, :], a["b_f"][0].partition_broadcast(P))
                early(g_ql[:, :], a["g_q_lat"][0].rearrange("(p k) -> p k", k=QRK))
                early(g_kvl[:, :], a["g_kv_lat"][0].rearrange("(p k) -> p k", k=KVRK))
                early(gc_fox[0][0:HD, :], a["g_fox_q"][0].rearrange("(p o) -> p o", o=1))
                early(gc_fox[1][0:HD, :], a["g_fox_k"][0].rearrange("(p o) -> p o", o=1))
                early(gc_mla[0][0:NOPE, :], a["g_mla_q"][0][0:NOPE].rearrange("(p o) -> p o", o=1))
                early(gc_mla[1][0:NOPE, :], a["g_mla_k"][0][0:NOPE].rearrange("(p o) -> p o", o=1))
                late_const(gr_q[:, :], a["g_mla_q"][0][NOPE:MQK].partition_broadcast(P))
                late_const(gr_k[:, :], a["g_mla_k"][0][NOPE:MQK].partition_broadcast(P))
                late_const(g_mix[:, 0:DK // 2], a["g_fox_out"][0].rearrange("(p k) -> p k", k=DK // 2))
                late_const(g_mix[:, DK // 2:], a["g_mla_out"][0].rearrange("(p k) -> p k", k=DK // 2))
                late_const(g_ffn[:, :], a["g_ffn"][0].rearrange("(p k) -> p k", k=DK))
                late_const(b_route[:, 0:NG], a["b_group"][0].partition_broadcast(P))
                late_const(b_route[:, NG:], a["b_expert"][0].partition_broadcast(P))
                late_const(rope_cs[:, :, :], a["rope"].rearrange("(t p) c -> p t c", p=P))
            step(pool.memset(identb[:, :], 0.0))
            pool.affine_select(out=identb[:, :], in_=identb[:, :], compare_op=ALU.not_equal, fill=1.0, base=0,
                               pattern=[[-1, P]], channel_multiplier=1).then_inc(masks_made, 1)
            step(pool.memset(causal[:, :], 0.0))
            pool.affine_select(out=causal[:, :], in_=causal[:, :], compare_op=ALU.is_ge, fill=NEG, base=0,
                               pattern=[[-1, P]], channel_multiplier=1).then_inc(masks_made, 1)
            step(pool.memset(tri[:, :], 1.0))
            pool.affine_select(out=tri[:, :], in_=tri[:, :], compare_op=ALU.is_ge, fill=0.0, base=0,
                               pattern=[[1, P]], channel_multiplier=-1).then_inc(masks_made, 1)
            step(pool.memset(before[:, :], 1.0))
            pool.affine_select(out=before[:, :], in_=before[:, :], compare_op=ALU.is_ge, fill=0.0, base=-1,
                               pattern=[[1, P]], channel_multiplier=-1).then_inc(masks_made, 1)
            pool.memset(ones[:, :], 1.0).then_inc(masks_made, 1)
            pool.memset(onesb[:, :], 1.0).then_inc(masks_made, 1)
            pool.iota(tok[:, :], pattern=[[P, NT]], base=0, channel_multiplier=1).then_inc(masks_made, 1)
            step(pool.iota(iota_i[:, :], pattern=[[1, NE]], base=0, channel_multiplier=0))
            pool.tensor_copy(iota_f[:, :], iota_i[:, :]).then_inc(masks_made, 1)
            step(pool.memset(zero_i[:, :], 0))
            pool.dma_start(table.rearrange("(p n) o -> p (n o)", p=P), zero_i[:, :]).then_inc(table_zeroed, 16)

            def inverse_root(b, c, scale):
                mean, y, t, mean_half = (newton[:, j:j + 1] for j in range(4))
                step(pool.tensor_scalar(mean, ss[b][:, c:c + 1], scale, EPS, ALU.mult, ALU.add))
                pool.tensor_scalar(y.bitcast(I32), mean.bitcast(I32), -0.5, float(0x5f3759df), ALU.mult, ALU.add)
                step(pool.tensor_scalar(mean_half, mean, -0.5, None, ALU.mult))
                for n in range(3):
                    step(pool.tensor_scalar(t, y, y, mean_half, ALU.mult, ALU.mult))
                    to = rinv[b][:, c:c + 1] if n == 2 else y
                    ins = pool.tensor_scalar(to, t, 1.5, y, ALU.add, ALU.mult)
                    if n < 2:
                        step(ins)
                return ins

            def mix_inverse(n):
                pool.wait_ge(mix_squares, n + 1)
                inverse_root(n % 2, 0, 1.0 / FOX).then_inc(mix_inv, 1)

            def h_inverse(p):
                pool.wait_ge(h_squares, p + 1)
                inverse_root(p % 2, 2, 1.0 / D).then_inc(h_inv, 1)

            def scatter(p):
                t = TILE_ORDER[p]
                pool.wait_ge(pos_made, p + 1)
                for k in range(2):
                    pool.indirect_dma_start(
                        out=table, out_offset=bass.IndirectOffsetOnAxis(ap=pos_t[:, t, k:k + 1].bitcast(U32), axis=0),
                        in_=tok[:, t:t + 1], in_offset=None).then_inc(table_filled, 16)

            pool.wait_ge(table_zeroed, 16)
            mix_inverse(0)
            for p in range(1, NT):
                mix_inverse(2 * p - 1)
                mix_inverse(2 * p)
                h_inverse(p - 1)
                if p >= 2:
                    scatter(p - 2)
            scatter(LAST - 1)
            scatter(LAST)
            pool.wait_ge(idx_in, 16)
            for b in range(2):
                pool.wait_ge(u2_stored[b], 16 * NT // 2)

            for e in range(NE):
                if e >= 2:
                    pool.wait_ge(xt_done, e - 1)
                pool.indirect_dma_start(
                    out=xg[e % 2][:, :, :].rearrange("p k n -> p (k n)"), out_offset=None, in_=u2_rows,
                    in_offset=bass.IndirectOffsetOnAxis(ap=idx[:, e:e + 1].bitcast(U32), axis=0)
                ).then_inc(xg_in[e % 2], 16)

            def fetch_outputs(source):
                for b in range(2):
                    pool.wait_ge(y_stored[b], 16 * NE // 2)
                for t in range(NT):
                    for k in range(2):
                        n = 2 * t + k
                        pool.indirect_dma_start(
                            out=yg[n][:, :], out_offset=None, in_=source,
                            in_offset=bass.IndirectOffsetOnAxis(ap=pos_y[:, t, k:k + 1].bitcast(U32), axis=0)
                        ).then_inc(yg_in[n], 16)

            pool.wait_ge(over_made, 1)
            tripped = pool.value_load(over[0:1, 0:1], min_val=0, max_val=1)
            with pool.If(tripped > 0):
                pool.wait_ge(y_done, NE)
                pool.memset(yg[0][:, :], 0.0).then_inc(fb_blank, 1)
                pool.wait_ge(fb_blank, 1)
                with pool.Fori(0, NE * REST // P) as n:
                    pool.dma_start(y_over_tiles[n, :, :], yg[0][:, :]).then_inc(fb_zeroed, 16)
                    pool.wait_ge(fb_zeroed, n * 16 + 16)
                with pool.Fori(0, NE) as e:
                    with pool.Fori(1, SEQ // slots) as c:
                        n = e * (SEQ // slots - 1) + c
                        with nc.allow_non_contiguous_dma("one expert's tokens"):
                            pool.dma_start(fb_idx[:, :], table_by_rank[bass.ds(c * slots, slots), bass.ds(e, 1)]
                                           ).then_inc(fb_idx_in, 16)
                        pool.wait_ge(fb_idx_in, n * 16)
                        pool.sem_inc(waits_ended, 1)
                        pool.indirect_dma_start(
                            out=xg[0][:, :, :].rearrange("p k n -> p (k n)"), out_offset=None, in_=u2_rows,
                            in_offset=bass.IndirectOffsetOnAxis(ap=fb_idx[:, :].bitcast(U32), axis=0)
                        ).then_inc(fb_xg, 16)
                        pool.wait_ge(fb_stored, n * 16)
                pool.wait_ge(fb_pos, 1)
                fetch_outputs(y_rows)
            with pool.Else():
                fetch_outputs(y_rows[0:MAIN, :])

        @block.scalar
        def _(act):
            step = stepper(act, act_step)
            def u_high(j):
                c = cols(TOKEN_TILES[j])
                act.wait_ge(turn_dve, j + 1)
                act.activation(uT_hi[:, :, c], u_full[:, :, c], ACT.Copy).then_inc(u_hi_made, 1)

            def w_high(b):
                act.wait_ge(win_in[b], 16)
                if b in ("k", "q", "ckv"):
                    before_b = BLOCK_ORDER[BLOCK_ORDER.index(b) - 2]
                    act.wait_ge(projected, unit_no[(before_b, NT - 1)] + 1)
                for k0 in range(0, DK, DK // 2):
                    act.activation(w_hi[b][:, k0:k0 + DK // 2, :], w_in[b][:, k0:k0 + DK // 2, :], ACT.Copy
                                   ).then_inc(w_hi_made, 1)

            act.wait_ge(eps_made, 1)
            act.activation(root[0][:, 0:1], eps_c[:, :], ACT.Sqrt)
            for j, t in enumerate(TOKEN_TILES):
                r = rows(t)
                src = xm[:, :] if t == MT else x[:, t, :]
                act.wait_ge(x_in[t], 16)
                step(act.activation(scrap[0:r, :], src, ACT.Square, accum_out=ss[0][0:r, j:j + 1]))
                act.activation(root[0][0:r, j:j + 1], ss[0][0:r, j:j + 1], ACT.Sqrt, scale=1.0 / D,
                               bias=eps_c[0:r, :]).then_inc(roots_made, 1)
            for j in range(len(TOKEN_TILES) - 1):
                u_high(j)
            w_high("ffcq")
            u_high(len(TOKEN_TILES) - 1)
            w_high("v")

            def empty_turn(u):
                n = turn_no[u]
                t = u[1]
                r = rows(t)
                act.wait_ge(turned, n + 1)
                src = pair(4 + 2 * (n % 2), H * r)[0:FOX_AUG, :].rearrange("p (h c) -> p h c", h=H)
                if u == ("k", MT):
                    act.wait_ge(vecs_made, 1)
                which = 0 if u[0] == "q" else 1
                dst = qT[0:FOX_AUG, :, cols(t)] if u[0] == "q" else kT[0:FOX_AUG, :, key_cols(t)]
                act.activation(dst, src, ACT.Copy, scale=gc_fox[which][:, :]).then_inc(turn_act, 1)

            for n, u in enumerate(units):
                b, t = u
                r = rows(t)
                bank = ps[0:r, n % 4, :]
                if t == NT - 1 and b in ("ffcq", "v", "k"):
                    split_next = BLOCK_ORDER[BLOCK_ORDER.index(b) + 2]
                else:
                    split_next = None
                act.wait_ge(projected, n + 1)
                if b == "v":
                    act.activation(vals[0:r, t, :], bank, ACT.Copy).then_inc(v_copied, 1)
                elif b in ("k", "q"):
                    m = head_no[u]
                    if m >= 2:
                        act.wait_ge(sums_made, m - 1)
                    act.activation(sq[m % 2][0:r, 0:FOX], bank, ACT.Square).then_inc(squares_made, 1)
                    act.wait_ge(sums_made, m + 1)
                    k = root_no[u]
                    act.activation(root[k % 2][0:r, :], ss[k % 2][0:r, :], ACT.Sqrt, scale=1.0 / HD,
                                   bias=eps_c[0:r, :]).then_inc(roots_made, 1)
                elif b == "ckv" or t != MT:
                    k = root_no[u]
                    w, c0 = (KVR, 0) if b == "ckv" else (QR, H)
                    if b == "ckv":
                        step(act.activation(junk[0:r, :], bank[:, KVR:KVR + ROPE], ACT.Square,
                                            accum_out=kr_ss[0:r, t:t + 1]))
                    step(act.activation(sq[k % 2][0:r, 0:w], bank[:, c0:c0 + w], ACT.Square,
                                        accum_out=ss[k % 2][0:r, 0:1]))
                    act.activation(root[k % 2][0:r, 0:1], ss[k % 2][0:r, 0:1], ACT.Sqrt, scale=1.0 / w,
                                   bias=eps_c[0:r, :]).then_inc(roots_made, 1)
                if u == ("ffcq", NT - 1):
                    act.wait_ge(ff_in, 1)
                    act.activation(ff_e[:, :, :], ff[:, :, :], ACT.Abs).then_inc(ff_abs, 1)
                    act.wait_ge(ff_abs, 1)
                    act.activation(ff_e[:, :, :], ff_e[:, :, :], ACT.Exp, scale=-1.0).then_inc(ff_exp, 1)
                    act.wait_ge(ff_exp, 1)
                    act.activation(ff_e[:, :, :], ff_e[:, :, :], ACT.Ln, bias=1.0).then_inc(ff_log, 1)
                if split_next:
                    w_high(split_next)
                if n >= 2 and by_act(units[n - 2]):
                    empty_turn(units[n - 2])
            for u in units[-2:]:
                if by_act(u):
                    empty_turn(u)

            def mix_square(n):
                p, half = divmod(n, 2)
                act.wait_ge(o_done, UNITS + (H * (p + 1) if half else 0))
                if n >= 2:
                    act.wait_ge(mix_turned, n - 1)
                k0 = half * DK // 2
                act.activation(mixn[:, k0:k0 + DK // 2, :].rearrange("p k n -> p (k n)"),
                               o_all[:, TILE_ORDER[p], half * FOX:(half + 1) * FOX], ACT.Square,
                               accum_out=ss[half][:, 0:1]).then_inc(mix_squares, 1)

            def mix_scale(n):
                p, half = divmod(n, 2)
                if p == LAST and half:
                    act.wait_ge(last_mix_inv, 1)
                else:
                    act.wait_ge(mix_inv, n + 1)
                k0 = half * DK // 2
                act.activation(mixn[:, k0:k0 + DK // 2, :],
                               o_all[:, TILE_ORDER[p], half * FOX:(half + 1) * FOX]
                               .rearrange("p (n k) -> p k n", k=DK // 2),
                               ACT.Copy, scale=rinv[half][:, 0:1]).then_inc(mix_made, 1)

            def h_square(p):
                act.wait_ge(h_made, p + 1)
                if p >= 2:
                    act.wait_ge(u2_stored[p % 2], 16 * (p // 2))
                    act.wait_ge(u2_turned, 2 * (p - 1))
                act.activation(u2n[p % 2][:, :, :].rearrange("p k n -> p (k n)"), x[:, TILE_ORDER[p], :],
                               ACT.Square, accum_out=ss[p % 2][:, 2:3]).then_inc(h_squares, 1)

            def last_root(b, c, scale, squares, count, signal):
                act.wait_ge(squares, count)
                act.activation(root[b][:, c:c + 1], ss[b][:, c:c + 1], ACT.Sqrt, scale=scale,
                               bias=eps_c[:, :]).then_inc(signal, 1)

            def load_root_table():
                act.activation(junk[:, 0:1], eps_c[:, :], ACT.Sqrt)

            def h_scale(p):
                if p == LAST:
                    act.wait_ge(last_h_inv, 1)
                else:
                    act.wait_ge(h_inv, p + 1)
                act.activation(u2n[p % 2][:, :, :], x[:, TILE_ORDER[p], :].rearrange("p (n k) -> p k n", k=DK),
                               ACT.Copy, scale=rinv[p % 2][:, 2:3]).then_inc(u2_made, 1)

            def route_exps(p):
                act.wait_ge(gmax_made, p + 1)
                act.activation(gexp[:, :], lg[:, 0:NG], ACT.Exp, bias=wt[:, 0:1],
                               accum_out=wt[:, 1:2]).then_inc(gexp_made, 1)
                act.wait_ge(gap_made, p + 1)
                act.activation(wt[:, 4:5], wt[:, 3:4], ACT.Exp).then_inc(gap_exp, 1)

            def between(p, h):
                if h == 0 and p >= 1:
                    mix_square(2 * p - 1)
                if h == 0 and p >= 2:
                    h_scale(p - 2)
                if h == 2 and p >= 1:
                    mix_scale(2 * p - 1)
                if h == 3:
                    mix_square(2 * p)
                if h == 5:
                    mix_scale(2 * p)
                if h == 6 and p >= 2:
                    route_exps(p - 2)
                if h == 7 and p >= 1:
                    h_square(p - 1)

            def attend(ph):
                g0 = ph * UNITS

                def exp(g):
                    act.wait_ge(maxed, g + 1)
                    act.activation(probs[g % PROBS][:, 0:unit_keys(g)], unit_scores(g), ACT.Exp,
                                   bias=nmax[g % PROBS][:, :], accum_out=psums[g % PROBS][:, :]).then_inc(exped, 1)

                def copy_meta(g):
                    act.wait_ge(pm_turned, g + 1)
                    act.activation(pT[g % 2][0:META, NT, :], ps[0:META, score_bank(g), 0:P], ACT.Copy
                                   ).then_inc(pm_copied, 1)

                def output(g):
                    h, i = unit(g)
                    act.wait_ge(pv_done, g + 1)
                    act.wait_ge(sums_inv, g + 1)
                    c = ph * FOX + h * HD
                    act.activation(o_all[:, i, c:c + HD], output_place(g), ACT.Copy,
                                   scale=prinv[g % 2][:, :]).then_inc(o_done, 1)

                for g in range(g0, g0 + AHEAD):
                    exp(g)
                for g in range(g0, g0 + UNITS):
                    copy_meta(g)
                    if g > g0:
                        output(g - 1)
                    if ph == 1:
                        between(*divmod(g - g0, H))
                    for u in due(g):
                        exp(u)
                if ph == 1:
                    load_root_table()
                output(g0 + UNITS - 1)

            attend(0)

            def empty_up(n):
                kind, t = up_units[n]
                r = rows(t)
                act.wait_ge(up_turned, n + 1)
                src = pair(4 + 2 * (n % 2), H * r)[0:MQK, :].rearrange("p (h c) -> p h c", h=H)
                which = 0 if kind == "uq" else 1
                dst = qT[:, :, cols(t)] if kind == "uq" else kT[:, :, key_cols(t)]
                act.activation(dst, src, ACT.Copy, scale=gc_mla[which][:, :]).then_inc(up_out, 1)

            for n, (kind, t) in enumerate(up_units):
                r = rows(t)
                b0 = 2 * (n % 2)
                act.wait_ge(up_done, n + 1)
                if n >= 2:
                    act.wait_ge(up_sums, n - 1)
                if kind == "kv":
                    kv = pair(b0, KVUP)[0:r, :].rearrange("p (h c) -> p h c", h=H)
                    act.activation(sq[n % 2][0:r, 0:H * NOPE].rearrange("p (h c) -> p h c", h=H),
                                   kv[:, :, 0:NOPE], ACT.Square).then_inc(up_squares, 1)
                    act.activation(vals[0:r, t, :].rearrange("p (h c) -> p h c", h=H), kv[:, :, NOPE:],
                                   ACT.Copy).then_inc(up_vals, 1)
                else:
                    act.activation(sq[n % 2][0:r, :].rearrange("p (j c) -> p j c", j=2),
                                   ps[0:r, b0:b0 + 2, 0:QUP // 2], ACT.Square).then_inc(up_squares, 1)
                act.wait_ge(up_sums, n + 1)
                act.activation(root[n % 2][0:r, :], ss[n % 2][0:r, :], ACT.Sqrt, scale=1.0 / MQK,
                               bias=eps_c[0:r, :]).then_inc(up_roots, 1)
                if n >= 1:
                    empty_up(n - 1)
            empty_up(NU - 1)

            attend(1)

            mix_square(2 * NT - 1)
            last_root(1, 0, 1.0 / FOX, mix_squares, 2 * NT, last_mix_root)
            h_scale(LAST - 1)
            mix_scale(2 * NT - 1)
            route_exps(LAST - 1)
            load_root_table()
            h_square(LAST)
            last_root(LAST % 2, 2, 1.0 / D, h_squares, NT, last_h_root)
            h_scale(LAST)
            route_exps(LAST)

            def silu(it, s, first=False):
                e = it * RING + s
                b = s % 2
                act.wait_ge(h13_done, e + 1)
                if not first or s >= 2:
                    act.wait_ge(hT_made, e - 1)
                act.activation(sil[b][:, :, :], ps[:, 2 + b, 0:FK * slots].rearrange("p (m n) -> p m n", m=FK),
                               ACT.Silu).then_inc(silu_done, 1)

            def store_rows(it, s, first=False):
                e = it * RING + s
                b = s % 2
                act.wait_ge(y_done, e + 1)
                if not first or s >= 2:
                    act.wait_ge(y_stored[b], 16 * (RING // 2 * it + s // 2))
                act.activation(ysb[b][:, :], pair(4 + 2 * b, D)[0:slots, :], ACT.Copy).then_inc(y_copied, 1)
                act.wait_ge(y_copied, e + 1)
                act.dma_start(y_main[e, :, :], ysb[b][:, :]).then_inc(y_stored[b], 16)

            def w2_high(it, s, first=False):
                e = it * RING + s
                act.wait_ge(w2_in[s], 16 * (it + 1))
                if not first or s >= 2:
                    act.wait_ge(y_done, e - 1)
                for m in range(FK):
                    act.activation(w2_hi[s % 2][:, m, :], w2s[s][:, m, :], ACT.Copy).then_inc(w2_hi_made, 1)

            for s in range(RING):
                silu(0, s, first=True)
                if s >= 1:
                    store_rows(0, s - 1, first=True)
                w2_high(0, s, first=True)
            def act_round(it, last=False):
                for s in range(RING):
                    early_split = last and s == RING - 1
                    if early_split:
                        w2_high(it, s)
                    silu(it, s)
                    if s >= 1:
                        store_rows(it, s - 1)
                    else:
                        store_rows(it - 1, RING - 1)
                    if not early_split:
                        w2_high(it, s)

            with act.Fori(1, NE // RING - 1) as it:
                act_round(it)
            act_round(NE // RING - 1, last=True)
            store_rows(NE // RING - 1, RING - 1)

            act.wait_ge(over_made, 1)
            tripped = act.value_load(over[0:1, 0:1], min_val=0, max_val=1)
            with act.If(tripped > 0):
                for b in range(2):
                    act.wait_ge(y_stored[b], 16 * NE // 2)
                with act.Fori(0, NE) as e:
                    with act.Fori(1, SEQ // slots) as c:
                        n = e * (SEQ // slots - 1) + c
                        act.wait_ge(fb_h13, n)
                        act.activation(sil[0][:, :, :],
                                       ps[:, 2, 0:FK * slots].rearrange("p (m n) -> p m n", m=FK),
                                       ACT.Silu).then_inc(fb_silu, 1)
                        act.wait_ge(fb_y, n)
                        act.activation(ysb[0][:, :], pair(4, D)[0:slots, :], ACT.Copy).then_inc(fb_y_out, 1)
                        act.wait_ge(fb_y_out, n)
                        act.dma_start(y_over[e, bass.ds((c - 1) * slots, slots), :], ysb[0][:, :]
                                      ).then_inc(fb_stored, 16)

        @block.vector
        def _(dve):
            step = stepper(dve, dve_step)
            dve.memset(eps_c[:, :], EPS).then_inc(eps_made, 1)
            dve.memset(ff[:, :, :], 0.0)
            dve.memset(kr[:, :, :], 0.0)
            step(dve.memset(lg[:, :], -3e38))
            def u_low(j):
                c = cols(TOKEN_TILES[j])
                dve.wait_ge(u_hi_made, j + 1)
                dve.tensor_tensor(uT_lo[:, :, c], u_full[:, :, c], uT_hi[:, :, c].bitcast(F32), ALU.subtract
                                  ).then_inc(u_lo_made, 1)

            def w_low(b, halves=(0, 1)):
                for q in halves:
                    k0 = q * DK // 2
                    dve.wait_ge(w_hi_made, 2 * split_order.index(b) + q + 1)
                    dve.tensor_tensor(w_lo[b][:, k0:k0 + DK // 2, :], w_in[b][:, k0:k0 + DK // 2, :],
                                      w_hi[b][:, k0:k0 + DK // 2, :].bitcast(F32), ALU.subtract
                                      ).then_inc(w_lo_made, 1)

            def norm_tokens(j):
                t = TOKEN_TILES[j]
                r = rows(t)
                src = (xm[:, :] if t == MT else x[:, t, :]).rearrange("p (n k) -> p k n", k=DK)
                dve.wait_ge(roots_made, j + 1)
                if j >= 2:
                    dve.wait_ge(turned, j - 1)
                step(dve.reciprocal(rinv[j % 2][0:r, 0:1], root[0][0:r, j:j + 1]))
                dve.tensor_scalar(xs[j % 2][0:r, :, :], src, rinv[j % 2][0:r, 0:1], None, ALU.mult
                                  ).then_inc(xs_made, 1)

            norm_tokens(0)
            for j, t in enumerate(TOKEN_TILES):
                r = rows(t)
                if j + 1 < len(TOKEN_TILES):
                    norm_tokens(j + 1)
                if j == 0:
                    dve.wait_ge(consts_in, 16)
                dve.wait_ge(turned, j + 1)
                for q in range(2):
                    k0 = q * DK // 2
                    ins = dve.tensor_tensor(
                        u_full[:, k0:k0 + DK // 2, cols(t)],
                        ps[:, 4 + 2 * (j % 2) + q, 0:DK // 2 * r].rearrange("p (k n) -> p k n", k=DK // 2),
                        g_attn[:, k0:k0 + DK // 2].unsqueeze(2).to_broadcast([P, DK // 2, r]), ALU.mult)
                ins.then_inc(turn_dve, 1)
                if j >= 1:
                    u_low(j - 1)
            w_low("ffcq")
            u_low(len(TOKEN_TILES) - 1)
            dve.wait_ge(early_in, EARLY * 16)
            dve.tensor_scalar(gc_fox[0][0:HD, :], gc_fox[0][0:HD, :], HD ** -0.5, None, ALU.mult)
            dve.tensor_scalar(gc_mla[0][0:NOPE, :], gc_mla[0][0:NOPE, :], MQK ** -0.5, None, ALU.mult)
            dve.memset(gc_mla[0][NOPE:MQK, :], MQK ** -0.5)
            dve.memset(gc_mla[1][NOPE:MQK, :], 1.0)
            dve.memset(gc_fox[0][HD:FOX_AUG, :], 1.0)
            dve.memset(gc_fox[1][HD:FOX_AUG, :], 1.0).then_inc(vecs_made, 1)

            def empty_turn(u):
                n = turn_no[u]
                b, t = u
                r = rows(t)
                dve.wait_ge(turned, n + 1)
                bank = ps[:, 4 + 2 * (n % 2), :]
                if b == "cum":
                    dve.tensor_copy(cum[:, :, :], bank[:, 0:(NT + 1) * H].rearrange("p (t h) -> p t h", h=H)
                                    ).then_inc(turn_dve, 1)
                    dve.wait_ge(turn_dve, sum(not by_act(v) for v in turns[:n + 1]))
                else:
                    dst, g, kk = (cqT, g_ql, QRK) if b == "ffcq" else (ckvT, g_kvl, KVRK)
                    dve.tensor_tensor(dst[:, :, cols(t)], bank[:, 0:kk * r].rearrange("p (k n) -> p k n", k=kk),
                                      g[:, :].unsqueeze(2).to_broadcast([P, kk, r]), ALU.mult
                                      ).then_inc(turn_dve, 1)

            for n, u in enumerate(units):
                b, t = u
                r = rows(t)
                bank = ps[0:r, n % 4, :]
                if b == "ffcq":
                    dve.wait_ge(projected, n + 1)
                    if t != MT:
                        dve.wait_ge(roots_made, root_no[u] + 1)
                    ins = dve.tensor_tensor(ff[0:r, t, :], bank[:, 0:H], bf_b[0:r, :], ALU.add)
                    if t == MT:
                        ins.then_inc(unit_freed, 1)
                    elif t == NT - 1:
                        ins.then_inc(ff_in, 1)
                if u in stage_no:
                    m = stage_no[u]
                    k = root_no[u]
                    if u in head_no:
                        hn = head_no[u]
                        dve.wait_ge(squares_made, hn + 1)
                        dve.tensor_reduce(ss[k % 2][0:r, :],
                                          sq[hn % 2][0:r, 0:FOX].rearrange("p (h c) -> p h c", h=H), X,
                                          ALU.add).then_inc(sums_made, 1)
                    dve.wait_ge(roots_made, k + 1)
                    w = H if u in head_no else 1
                    step(dve.reciprocal(rinv[k % 2][0:r, 0:w], root[k % 2][0:r, 0:w]))
                    if m >= 2:
                        dve.wait_ge(turned, turn_no[staged[m - 2]] + 1)
                    if u in head_no:
                        st = st_fox[m % 2]
                        dve.tensor_tensor(st[0:r, :, 0:HD], bank.rearrange("p (h c) -> p h c", h=H),
                                          rinv[k % 2][0:r, :].unsqueeze(2).to_broadcast([r, H, HD]), ALU.mult
                                          ).then_inc(unit_freed, 1)
                        one, c = (HD, HD + 1) if b == "k" else (HD + 1, HD)
                        dve.memset(st[0:r, :, one:one + 1], 1.0)
                        dve.tensor_scalar(st[0:r, :, c:c + 1], cum[0:r, t, :].unsqueeze(2),
                                          -1.0 if b == "k" else 1.0, None, ALU.mult).then_inc(staged_done, 1)
                    else:
                        kk, c0, w = (KVRK, 0, KVR) if b == "ckv" else (QRK, H, QR)
                        if b == "ckv":
                            dve.tensor_copy(kr[0:r, t, :], bank[:, KVR:KVR + ROPE])
                        dve.tensor_scalar(st_lat[m % 2][0:r, 0:kk, :],
                                          bank[:, c0:c0 + w].rearrange("p (n k) -> p k n", k=kk),
                                          rinv[k % 2][0:r, 0:1], None, ALU.mult).then_inc(staged_done, 1)
                        dve.wait_ge(staged_done, m + 1)
                        dve.sem_inc(unit_freed, 1)
                if u == ("ffcq", NT - 1):
                    dve.wait_ge(ff_log, 1)
                    dve.scalar_tensor_tensor(out=logf[:, :, :], in0=ff[:, :, :], scalar=0.0, in1=ff_e[:, :, :],
                                             op0=ALU.min, op1=ALU.subtract).then_inc(logf_made, 1)
                if u == ("v", NT - 1):
                    empty_turn(("cum", 0))
                if n >= 1 and units[n - 1] in stage_no and not by_act(units[n - 1]):
                    empty_turn(units[n - 1])
                if u in (("ffcq", 0), ("ffcq", 1)):
                    w_low("v", [t])
                if t == NT - 1 and b in ("ffcq", "v", "k"):
                    w_low(BLOCK_ORDER[BLOCK_ORDER.index(b) + 2])
            empty_turn(units[-1])

            def gained(dst, half, bank, gain, signal):
                k0 = half * DK // 2
                dve.tensor_tensor(
                    dst[:, k0:k0 + DK // 2, :], ps[:, bank, :].rearrange("p (k n) -> p k n", k=DK // 2),
                    gain[:, k0:k0 + DK // 2].unsqueeze(2).to_broadcast([P, DK // 2, P]), ALU.mult
                ).then_inc(signal, 1)

            def mix_empty(n):
                dve.wait_ge(mix_turned, n + 1)
                if n >= 2:
                    dve.wait_ge(wo_done, n - 1)
                gained(mixT, n % 2, MISC, g_mix, mix_out)

            def residual(p):
                dve.wait_ge(wo_done, 2 * p + 2)
                dve.tensor_tensor(x[:, TILE_ORDER[p], :], x[:, TILE_ORDER[p], :], pair(ACCUM, D), ALU.add
                                  ).then_inc(h_made, 1)

            def u2_empty(p, half, bank=MISC):
                dve.wait_ge(u2_turned, 2 * p + half + 1)
                if p >= 1:
                    dve.wait_ge(logits_done, p)
                gained(u2T, half, bank, g_ffn, u2_out)

            def choose_group(p):
                dve.wait_ge(logits_done, p + 1)
                bank = router_bank(p)
                dve.tensor_tensor(lg[:, 0:NG], ps[:, bank, 0:NG], b_route[:, 0:NG], ALU.add)
                dve.tensor_tensor(lg[:, 8:8 + NE], ps[:, bank, NG:ROUTE], b_route[:, NG:], ALU.add
                                  ).then_inc(logits_read, 1)
                dve.wait_ge(logits_read, p + 1)
                step(dve.max(gtop[:, :], lg[:, 0:8]))
                dve.tensor_scalar(wt[:, 0:1], gtop[:, 0:1], -1.0, None, ALU.mult).then_inc(gmax_made, 1)
                step(dve.max_index(gidx[:, :], gtop[:, :], lg[:, 0:8]))
                step(dve.tensor_copy(gf[:, 0:1], gidx[:, 0:1]))
                step(dve.tensor_scalar(ghot[:, :], iota_f[:, 0:NG], gf[:, 0:1], None, ALU.is_equal))
                step(dve.tensor_tensor(gprod[:, :, :], lg[:, 8:8 + NE].rearrange("p (g e) -> p e g", g=NG),
                                       ghot[:, :].unsqueeze(1).to_broadcast([P, EPG, NG]), ALU.mult))
                step(dve.tensor_reduce(within[:, :], gprod[:, :, :], X, ALU.add))
                step(dve.max(etop[:, :], within[:, :]))
                dve.tensor_tensor(wt[:, 3:4], etop[:, 1:2], etop[:, 0:1], ALU.subtract).then_inc(gap_made, 1)

            def choose_experts(p):
                i = TILE_ORDER[p]
                step(dve.max_index(eidx[:, :], etop[:, :], within[:, :]))
                step(dve.tensor_copy(esel[:, :], eidx[:, 0:2]))
                dve.tensor_scalar(gf[:, 1:2], gf[:, 0:1], float(EPG), None, ALU.mult).then_inc(dve_gf, 1)
                dve.wait_ge(dve_gf, p + 1)
                step(dve.tensor_scalar(esels[:, i, :], esel[:, :], gf[:, 1:2], None, ALU.add))
                for k in range(2):
                    ins = dve.tensor_scalar(ehots[:, i, k, :], iota_f[:, :], esels[:, i, k:k + 1], None,
                                            ALU.is_equal)
                step(ins)
                dve.tensor_tensor(picks[:, i, :], ehots[:, i, 0, :], ehots[:, i, 1, :], ALU.add
                                  ).then_inc(picks_made, 1)

            def weigh(p):
                i = TILE_ORDER[p]
                dve.wait_ge(gexp_made, p + 1)
                dve.wait_ge(gap_exp, p + 1)
                step(dve.tensor_scalar(wt[:, 5:6], wt[:, 4:5], 1.0, None, ALU.add))
                step(dve.tensor_tensor(wt[:, 6:7], wt[:, 5:6], wt[:, 1:2], ALU.mult))
                step(dve.reciprocal(coef[:, i, 0:1], wt[:, 6:7]))
                step(dve.tensor_tensor(coef[:, i, 1:2], coef[:, i, 0:1], wt[:, 4:5], ALU.mult))

            def positions(p):
                i = TILE_ORDER[p]
                dve.wait_ge(ranked, p + 1)
                step(dve.tensor_tensor(rprod[:, :, :], ehots[:, i, :, :],
                                       ps[:, MISC, 0:NE].unsqueeze(1).to_broadcast([P, 2, NE]), ALU.mult))
                step(dve.tensor_reduce(ranks_all[:, i, :], rprod[:, :, :], X, ALU.add))
                dve.scalar_tensor_tensor(out=pos_t[:, i, :], in0=ranks_all[:, i, :], scalar=float(NE),
                                         in1=esels[:, i, :], op0=ALU.mult, op1=ALU.add)
                dve.scalar_tensor_tensor(out=pos_y[:, i, :], in0=esels[:, i, :], scalar=float(slots),
                                         in1=ranks_all[:, i, :], op0=ALU.mult, op1=ALU.add).then_inc(pos_made, 1)

            def between(p, h):
                if h == 0 and p >= 1:
                    mix_empty(2 * p - 2)
                if h in (1, 2) and p >= 2:
                    u2_empty(p - 2, h - 1)
                if h == 3 and p >= 1:
                    mix_empty(2 * p - 1)
                if h == 4 and p >= 2:
                    choose_group(p - 2)
                if h == 5 and p >= 2:
                    choose_experts(p - 2)
                if h == 6 and p >= 1:
                    residual(p - 1)
                if h == 6 and p == LAST:
                    mix_empty(2 * p)
                if h == 7 and p >= 2:
                    positions(p - 2)
                    weigh(p - 2)

            def attend(ph):
                g0 = ph * UNITS

                def row_max(g):
                    dve.wait_ge(scored, g + 1)
                    dve.tensor_reduce(nmax[g % PROBS][:, :], unit_scores(g), X, ALU.max, negate=True
                                      ).then_inc(maxed, 1)

                for g in range(g0, g0 + AHEAD):
                    row_max(g)
                for g in range(g0, g0 + UNITS):
                    chunks = unit(g)[1] + 1
                    dve.wait_ge(p_turned, g + 1)
                    dve.tensor_copy(pT[g % 2][:, 0:chunks, :].rearrange("p c n -> p (c n)"),
                                    ps[:, 6 + g % 2, 0:P * chunks]).then_inc(p_copied, 1)
                    if g >= 2:
                        dve.wait_ge(o_done, g - 1)
                    dve.reciprocal(prinv[g % 2][:, :], psums[g % PROBS][:, :]).then_inc(sums_inv, 1)
                    if ph == 1:
                        between(*divmod(g - g0, H))
                    for u in due(g):
                        row_max(u)

            attend(0)

            def rotate(dst1, dst2, a1, a2, cos, sin, tmp):
                dve.tensor_tensor(tmp[0], a1, cos, ALU.mult)
                dve.tensor_tensor(tmp[1], a2, sin, ALU.mult)
                dve.tensor_tensor(tmp[2], a1, sin, ALU.mult)
                step(dve.tensor_tensor(tmp[3], a2, cos, ALU.mult))
                dve.tensor_tensor(dst1, tmp[0], tmp[1], ALU.subtract)
                return dve.tensor_tensor(dst2, tmp[2], tmp[3], ALU.add)

            dve.wait_ge(late_in, LATE * 16)
            step(dve.tensor_tensor(krg[:, :, :], kr[:, :, :], gr_k[:, :].unsqueeze(1).to_broadcast([P, NT + 1, ROPE]),
                                   ALU.mult))
            step(rotate(krr[:, :, 0:HALF], krr[:, :, HALF:], krg[:, :, 0:HALF], krg[:, :, HALF:],
                        rope_cs[:, :, 0:HALF], rope_cs[:, :, HALF:], [krt[:, j, :, :] for j in range(4)]))
            for n, (kind, t) in enumerate(up_units):
                r = rows(t)
                b0 = 2 * (n % 2)
                st = st_mla[n % 2]
                dve.wait_ge(up_squares, n + 1)
                if kind == "kv":
                    step(dve.tensor_reduce(ss[n % 2][0:r, :],
                                           sq[n % 2][0:r, 0:H * NOPE].rearrange("p (h c) -> p h c", h=H), X, ALU.add))
                    dve.tensor_scalar(ss[n % 2][0:r, :], ss[n % 2][0:r, :], kr_ss[0:r, t:t + 1], None, ALU.add
                                      ).then_inc(up_sums, 1)
                else:
                    dve.tensor_reduce(ss[n % 2][0:r, :], sq[n % 2][0:r, :].rearrange("p (h c) -> p h c", h=H), X,
                                      ALU.add).then_inc(up_sums, 1)
                dve.wait_ge(up_roots, n + 1)
                step(dve.reciprocal(rinv[n % 2][0:r, :], root[n % 2][0:r, :]))
                if n >= 2:
                    dve.wait_ge(up_turned, n - 1)
                if kind == "kv":
                    kv = pair(b0, KVUP)[0:r, :].rearrange("p (h c) -> p h c", h=H)
                    dve.tensor_tensor(st[0:r, :, NOPE:], krr[0:r, t, :].unsqueeze(1).to_broadcast([r, H, ROPE]),
                                      rinv[n % 2][0:r, :].unsqueeze(2).to_broadcast([r, H, ROPE]), ALU.mult)
                    dve.tensor_tensor(st[0:r, :, 0:NOPE], kv[:, :, 0:NOPE],
                                      rinv[n % 2][0:r, :].unsqueeze(2).to_broadcast([r, H, NOPE]), ALU.mult
                                      ).then_inc(up_staged, 1)
                else:
                    hh = H // 2
                    step(dve.tensor_tensor(
                        st[:, :, :].rearrange("p (j h) c -> p j h c", j=2),
                        ps[:, b0:b0 + 2, 0:QUP // 2].rearrange("p j (h c) -> p j h c", h=hh),
                        rinv[n % 2][:, :].rearrange("p (j h) -> p j h", j=2).unsqueeze(3)
                        .to_broadcast([P, 2, hh, MQK]), ALU.mult))
                    step(dve.tensor_tensor(rope_g[:, :, :], st[:, :, NOPE:],
                                           gr_q[:, :].unsqueeze(1).to_broadcast([P, H, ROPE]), ALU.mult))
                    rotate(st[:, :, NOPE:NOPE + HALF], st[:, :, NOPE + HALF:], rope_g[:, :, 0:HALF],
                           rope_g[:, :, HALF:], rope_cs[:, t, 0:HALF].unsqueeze(1).to_broadcast([P, H, HALF]),
                           rope_cs[:, t, HALF:].unsqueeze(1).to_broadcast([P, H, HALF]),
                           [rope_t[:, j, :, :] for j in range(4)]).then_inc(up_staged, 1)

            attend(1)

            dve.wait_ge(last_mix_root, 1)
            dve.reciprocal(rinv[1][:, 0:1], root[1][:, 0:1]).then_inc(last_mix_inv, 1)
            for half in range(2):
                u2_empty(LAST - 1, half, bank=half)
            mix_empty(2 * NT - 1)
            choose_group(LAST - 1)
            choose_experts(LAST - 1)
            residual(LAST)
            positions(LAST - 1)
            dve.wait_ge(last_h_root, 1)
            dve.reciprocal(rinv[LAST % 2][:, 2:3], root[LAST % 2][:, 2:3]).then_inc(last_h_inv, 1)
            weigh(LAST - 1)
            for half in range(2):
                u2_empty(LAST, half, bank=half)
            choose_group(LAST)
            choose_experts(LAST)
            positions(LAST)
            dve.wait_ge(counted, 1)
            step(dve.tensor_reduce(most[:, :], ps[:, 0, 0:NE], X, ALU.max))
            dve.tensor_scalar(over[:, :], most[:, :], float(slots), None, ALU.is_gt).then_inc(over_made, 1)
            weigh(LAST)

            def dve_turned(it, s, first):
                e = it * RING + s
                b = s % 2
                dve.wait_ge(xt_done, e + 1)
                if not first or s >= 2:
                    dve.wait_ge(h13_done, e - 1)
                dve.tensor_tensor(xt[b][:, :, :], ps[:, b, 0:DK * slots].rearrange("p (k n) -> p k n", k=DK),
                                  g_ffn[:, :].unsqueeze(2).to_broadcast([P, DK, slots]), ALU.mult
                                  ).then_inc(xt_out, 1)

            def dve_gate(it, s, first):
                e = it * RING + s
                b = s % 2
                dve.wait_ge(silu_done, e + 1)
                if not first or s >= 2:
                    dve.wait_ge(y_done, e - 1)
                dve.tensor_tensor(sil[b][:, :, :], sil[b][:, :, :],
                                  ps[:, 2 + b, FK * slots:2 * FK * slots].rearrange("p (m n) -> p m n", m=FK),
                                  ALU.mult).then_inc(gated, 1)

            def split_hidden(it, s):
                e = it * RING + s
                b = s % 2
                dve.wait_ge(gated, e + 1)
                dve.tensor_copy(hT_hi[b][:, :, :], sil[b][:, :, :]).then_inc(hT_high, 1)
                dve.wait_ge(hT_high, e + 1)
                dve.tensor_tensor(hT_lo[b][:, :, :], sil[b][:, :, :], hT_hi[b][:, :, :].bitcast(F32), ALU.subtract
                                  ).then_inc(hT_made, 1)

            def w2_low(it, s):
                e = it * RING + s
                b = s % 2
                for m in range(FK):
                    dve.wait_ge(w2_hi_made, FK * e + m + 1)
                    dve.tensor_tensor(w2_lo[s][:, m, :], w2s[s][:, m, :], w2_hi[b][:, m, :].bitcast(F32),
                                      ALU.subtract).then_inc(w2_lo_made, 1)

            def dve_expert(it, s, first=False, last=False):
                if last and s == RING - 1:
                    w2_low(it, s)
                    dve_gate(it, s, first)
                    split_hidden(it, s)
                    return
                dve_gate(it, s, first)
                if s == RING - 1:
                    dve_turned(it + 1, 0, False)
                else:
                    dve_turned(it, s + 1, first)
                split_hidden(it, s)
                w2_low(it, s)

            dve_turned(0, 0, True)
            for s in range(RING):
                dve_expert(0, s, first=True)
            with dve.Fori(1, NE // RING - 1) as it:
                for s in range(RING):
                    dve_expert(it, s)
            for s in range(RING):
                dve_expert(NE // RING - 1, s, last=True)

            tripped = dve.value_load(over[0:1, 0:1], min_val=0, max_val=1)
            with dve.If(tripped > 0):
                dve.tensor_scalar(late[:, 0, :, :], ranks_all[:, :, :], float(slots), None, ALU.is_ge)
                step(dve.tensor_scalar(late[:, 1, :, :], esels[:, :, :], float(REST - slots), float(MAIN - slots),
                                       ALU.mult, ALU.add))
                step(dve.tensor_tensor(late[:, 0, :, :], late[:, 0, :, :], late[:, 1, :, :], ALU.mult))
                step(dve.scalar_tensor_tensor(out=late[:, 1, :, :], in0=esels[:, :, :], scalar=float(slots),
                                              in1=ranks_all[:, :, :], op0=ALU.mult, op1=ALU.add))
                dve.tensor_tensor(pos_y[:, :, :], late[:, 0, :, :], late[:, 1, :, :], ALU.add).then_inc(fb_pos, 1)
                dve.wait_ge(y_done, NE)
                with dve.Fori(0, NE) as e:
                    with dve.Fori(1, SEQ // slots) as c:
                        n = e * (SEQ // slots - 1) + c
                        dve.wait_ge(fb_xt, n)
                        dve.tensor_tensor(xt[0][:, :, :],
                                          ps[:, 0, 0:DK * slots].rearrange("p (k n) -> p k n", k=DK),
                                          g_ffn[:, :].unsqueeze(2).to_broadcast([P, DK, slots]), ALU.mult
                                          ).then_inc(fb_xt_out, 1)
                        dve.wait_ge(fb_silu, n)
                        dve.tensor_tensor(sil[0][:, :, :], sil[0][:, :, :],
                                          ps[:, 2, FK * slots:2 * FK * slots].rearrange("p (m n) -> p m n", m=FK),
                                          ALU.mult).then_inc(fb_hT, 1)

            for t in range(NT):
                for k in range(2):
                    n = 2 * t + k
                    dve.wait_ge(yg_in[n], 16)
                    if k == 1:
                        dve.wait_ge(first_added, t + 1)
                    ins = dve.scalar_tensor_tensor(out=x[:, t, :], in0=yg[n][:, :],
                                                   scalar=coef[:, t, k:k + 1], in1=x[:, t, :], op0=ALU.mult,
                                                   op1=ALU.add)
                    ins.then_inc(out_made if k == 1 else first_added, 1)

        @block.tensor
        def _(pe):
            pe.wait_ge(ident_made, 1)

            def keep_warm(bank, count):
                for _ in range(count):
                    pe.matmul(ps[:, bank, :], identb[:, :], onesb[:, :].unsqueeze(1).to_broadcast([P, 4, P]),
                              start=True, stop=True)

            def turn(u):
                n = turn_no[u]
                b, t = u
                r = rows(t)
                b0 = 4 + 2 * (n % 2)
                turn_freed(pe, n)
                if b == "cum":
                    pe.wait_ge(logf_made, 1)
                    pe.wait_ge(masks_made, 8)
                    for t in TOKEN_TILES:
                        dst = ps[:, b0, t * H:(t + 1) * H]
                        earlier = [] if t == MT else [MT] + list(range(t))
                        for s in earlier:
                            pe.matmul(dst, ones[0:rows(s), :], logf[0:rows(s), s, :], start=(s == MT), stop=False)
                        ins = pe.matmul(dst, tri[:, :], logf[:, t, :], start=not earlier, stop=True)
                    ins.then_inc(turned, 1)
                    return
                if b == "x":
                    j = TOKEN_TILES.index(t)
                    pe.wait_ge(xs_made, j + 1)
                    for k in range(DK):
                        q, kk = divmod(k, DK // 2)
                        ins = pe.transpose(ps[:, b0 + q, kk * r:(kk + 1) * r], xs[j % 2][0:r, k, :],
                                           ident[0:r, 0:r])
                    ins.then_inc(turned, 1)
                    return
                m = stage_no[u]
                pe.wait_ge(staged_done, m + 1)
                if b in ("k", "q"):
                    for h in range(H):
                        ins = pe.transpose(pair(b0, H * r)[0:FOX_AUG, h * r:(h + 1) * r], st_fox[m % 2][0:r, h, :],
                                           ident[0:r, 0:r])
                else:
                    for k in range(KVRK if b == "ckv" else QRK):
                        ins = pe.transpose(ps[:, b0, k * r:(k + 1) * r], st_lat[m % 2][0:r, k, :],
                                           ident[0:r, 0:r])
                ins.then_inc(turned, 1)

            def project(u):
                n = unit_no[u]
                b, t = u
                c0, w = BLOCKS[b]
                if u == ("ffcq", MT):
                    w = H
                if b == "ffcq":
                    pe.wait_ge(u_lo_made, TOKEN_TILES.index(t) + 1)
                if n >= 4:
                    unit_emptied(pe, n - 4)
                done = 2 * split_order.index(b)
                for p, (ua, wa) in enumerate(((uT_hi, w_hi), (uT_lo, w_hi), (uT_hi, w_lo))):
                    for k in range(DK):
                        if k % (DK // 2) == 0 and t == MT and p != 1:
                            pe.wait_ge(w_lo_made if p else w_hi_made, done + k // (DK // 2) + 1)
                        elif k == 0 and b == "q" and t == 0 and p != 1:
                            pe.wait_ge(w_lo_made if p else w_hi_made, done + 2)
                        ins = pe.matmul(ps[0:rows(t), n % 4, 0:w], ua[:, k, cols(t)], wa[b][:, k, 0:w],
                                        start=(k == 0 and p == 0), stop=(k == DK - 1 and p == 2))
                ins.then_inc(projected, 1)

            for what, u in steps:
                if u == steps[-1][1] and what == "turn":
                    unit_emptied(pe, len(units) - 4)
                    keep_warm((len(units) - 4) % 4, 14)
                turn(u) if what == "turn" else project(u)

            def turn_mix(n):
                pe.wait_ge(mix_made, n + 1)
                if n == 1:
                    pe.wait_ge(mix_out, 1)
                elif n in (3, 5):
                    pe.wait_ge(u2_out, n - 1)
                elif n in (4, 7):
                    pe.wait_ge(pos_made, n // 2 - 1)
                elif n == 2:
                    pe.wait_ge(mix_out, 2)
                elif n == 6:
                    pe.wait_ge(logits_read, 2)
                k0 = n % 2 * DK // 2
                for k in range(DK // 2):
                    ins = pe.transpose(ps[:, MISC, k * P:(k + 1) * P], mixn[:, k0 + k, :], ident[:, :])
                ins.then_inc(mix_turned, 1)

            def out_project(n, q):
                pe.wait_ge(mix_out, n + 1)
                half = n % 2
                if n >= 2 and not half:
                    pe.wait_ge(h_made, n // 2)
                for k in range(half * DK // 2, (half + 1) * DK // 2):
                    ins = pe.matmul(ps[:, ACCUM + q, :], mixT[:, k, :], wo_chunk(k)[:, q * 512:(q + 1) * 512],
                                    start=(k == 0), stop=(k == DK - 1))
                if q == 1:
                    ins.then_inc(wo_done, 1)

            def turn_u2(p, half, bank=MISC):
                pe.wait_ge(u2_made, p + 1)
                if bank == MISC:
                    if half:
                        pe.wait_ge(u2_out, 2 * p + 1)
                    else:
                        pe.wait_ge(mix_out, 2 * p + 3)
                elif p == LAST - 1:
                    pe.wait_ge(o_done, 2 * UNITS - 1)
                k0 = half * DK // 2
                for k in range(DK // 2):
                    ins = pe.transpose(ps[:, bank, k * P:(k + 1) * P], u2n[p % 2][:, k0 + k, :], ident[:, :])
                ins.then_inc(u2_turned, 1)

            def router(p):
                pe.wait_ge(u2_out, 2 * p + 2)
                if p < LAST - 1:
                    pe.wait_ge(mix_out, 2 * p + 4)
                for k in range(DK):
                    ins = pe.matmul(ps[:, router_bank(p), 0:ROUTE], u2T[:, k, :], w_route[:, k, :],
                                    start=(k == 0), stop=(k == DK - 1))
                ins.then_inc(logits_done, 1)

            def ranks(p):
                pe.wait_ge(picks_made, p + 1)
                if p == LAST - 2:
                    pe.wait_ge(mix_out, 2 * LAST + 1)
                elif p == LAST:
                    pe.wait_ge(pos_made, p)
                for s in range(p):
                    pe.matmul(ps[:, MISC, 0:NE], onesb[:, :], picks[:, TILE_ORDER[s], :], start=(s == 0),
                              stop=False)
                pe.matmul(ps[:, MISC, 0:NE], before[:, :], picks[:, TILE_ORDER[p], :], start=(p == 0), stop=True
                          ).then_inc(ranked, 1)

            def between(p, h):
                if p == 0:
                    return
                if h == 0:
                    turn_mix(2 * p - 2)
                if h == 1 and p == 1:
                    pe.wait_ge(wo_in, 48)
                    pe.wait_ge(route_in, 32)
                if h in (1, 2):
                    out_project(2 * p - 2, h - 1)
                    if p >= 2:
                        turn_u2(p - 2, h - 1)
                if h == 3:
                    turn_mix(2 * p - 1)
                if h == 4 and p >= 2:
                    router(p - 2)
                if h in (5, 6):
                    out_project(2 * p - 1, h - 5)
                if h == 6 and p == LAST:
                    turn_mix(2 * p)
                if h == 7:
                    if p == LAST:
                        out_project(2 * p, 0)
                    if p >= 2:
                        ranks(p - 2)

            def attend(ph):
                g0 = ph * UNITS
                depth = FOX_AUG if ph == 0 else MQK

                def score(g):
                    h, i = unit(g)
                    b0, n = score_bank(g), unit_keys(g)
                    q = qT[0:depth, h, i * P:(i + 1) * P]
                    user = bank_user_before(g)
                    if user >= g0:
                        if output_apart(user):
                            pe.wait_ge(pm_copied, user + 1)
                        else:
                            pe.wait_ge(o_done, user + 1)
                    for c0 in range(0, n, 512):
                        c1 = min(n, c0 + 512)
                        m0 = max(c0, n - P)
                        pe.matmul(ps[:, b0 + c0 // 512, 0:c1 - c0], q, kT[0:depth, h, c0:c1], start=True,
                                  stop=False)
                        ins = pe.matmul(ps[:, b0 + c0 // 512, m0 - c0:c1 - c0], identb[:, :],
                                        causal[:, m0 - (n - P):c1 - (n - P)], start=False, stop=True)
                    ins.then_inc(scored, 1)

                def turn_probs(g):
                    pe.wait_ge(exped, g + 1)
                    if g >= 2:
                        pe.wait_ge(p_copied, g - 1)
                        if output_apart(g - 2):
                            pe.wait_ge(o_done, g - 1)
                    pr = probs[g % PROBS]
                    pe.transpose(ps[0:META, score_bank(g), 0:P], pr[:, 0:META], ident[:, :]
                                 ).then_inc(pm_turned, 1)
                    for c in range(unit(g)[1] + 1):
                        ins = pe.transpose(ps[:, 6 + g % 2, c * P:(c + 1) * P],
                                           pr[:, META + c * P:META + (c + 1) * P], ident[:, :])
                    ins.then_inc(p_turned, 1)

                def apply(g):
                    h, i = unit(g)
                    dst = output_place(g)
                    pe.wait_ge(pm_copied, g + 1)
                    if output_apart(g):
                        pe.wait_ge(p_copied, g + 1)
                    pe.matmul(dst, pT[g % 2][0:META, NT, :], vals[0:META, NT, h * HD:(h + 1) * HD],
                              start=True, stop=False)
                    pe.wait_ge(p_copied, g + 1)
                    for c in range(i + 1):
                        ins = pe.matmul(dst, pT[g % 2][:, c, :], vals[:, c, h * HD:(h + 1) * HD],
                                        start=False, stop=(c == i))
                    ins.then_inc(pv_done, 1)

                for g in range(g0, g0 + AHEAD):
                    score(g)
                keep_warm(7, 5)
                for g in range(g0, g0 + UNITS):
                    turn_probs(g)
                    if g == g0:
                        keep_warm(7, 5)
                    if g > g0:
                        apply(g - 1)
                    if ph == 1:
                        between(*divmod(g - g0, H))
                    for u in due(g):
                        score(u)
                apply(g0 + UNITS - 1)

            for n in range(len(units) - 4, len(units)):
                unit_emptied(pe, n)
            pe.wait_ge(v_copied, len(TOKEN_TILES))
            pe.wait_ge(turn_act, sum(by_act(u) for u in turns))
            pe.wait_ge(turn_dve, sum(not by_act(u) for u in turns))
            attend(0)

            pe.wait_ge(wup_in, 32)
            pe.wait_ge(o_done, UNITS)
            pe.wait_ge(p_copied, UNITS)

            def turn_up(n):
                kind, t = up_units[n]
                r = rows(t)
                pe.wait_ge(up_staged, n + 1)
                if n >= 2:
                    pe.wait_ge(up_out, n - 1)
                for h in range(H):
                    ins = pe.transpose(pair(4 + 2 * (n % 2), H * r)[0:MQK, h * r:(h + 1) * r],
                                       st_mla[n % 2][0:r, h, :], ident[0:r, 0:r])
                ins.then_inc(up_turned, 1)

            for n, (kind, t) in enumerate(up_units):
                r = rows(t)
                b0 = 2 * (n % 2)
                if n >= 2:
                    pe.wait_ge(up_staged, n - 1)
                    pe.wait_ge(up_vals, min(n - 1, len(TOKEN_TILES)))
                src, w, kk, nn = (ckvT, w_ukv, KVRK, KVUP // 2) if kind == "kv" else (cqT, w_uq, QRK, QUP // 2)
                for j in range(2):
                    for k in range(kk):
                        ins = pe.matmul(ps[0:r, b0 + j, 0:nn], src[:, k, cols(t)], w[:, k, j * nn:(j + 1) * nn],
                                        start=(k == 0), stop=(k == kk - 1))
                ins.then_inc(up_done, 1)
                if n >= 1:
                    turn_up(n - 1)
            pe.wait_ge(up_out, NU - 2)
            keep_warm(4 + 2 * ((NU - 1) % 2), 14)
            turn_up(NU - 1)
            pe.wait_ge(up_vals, len(TOKEN_TILES))
            pe.wait_ge(up_out, NU)
            attend(1)

            out_project(2 * LAST, 1)
            for half in range(2):
                turn_u2(LAST - 1, half, bank=half)
            turn_mix(2 * NT - 1)
            router(LAST - 1)
            out_project(2 * NT - 1, 0)
            out_project(2 * NT - 1, 1)
            ranks(LAST - 1)
            keep_warm(7, 16)
            for half in range(2):
                turn_u2(LAST, half, bank=half)
            router(LAST)
            ranks(LAST)
            for s in range(NT):
                ins = pe.matmul(ps[:, 0, 0:NE], onesb[:, :], picks[:, s, :], start=(s == 0), stop=(s == NT - 1))
            ins.then_inc(counted, 1)

            def turn_rows(bank, src):
                for k in range(DK):
                    ins = pe.transpose(ps[:, bank, k * slots:(k + 1) * slots], src[:, k, :], ident[0:slots, 0:slots])
                return ins

            def first_products(bank, w, src):
                for j in range(2):
                    for m in range(FK):
                        dst = ps[:, bank, (j * FK + m) * slots:(j * FK + m + 1) * slots]
                        for k in range(DK):
                            ins = pe.matmul(dst, w[:, j, k, m * P:(m + 1) * P], src[:, k, :], start=(k == 0),
                                            stop=(k == DK - 1))
                return ins

            def second_product(bank, parts):
                for n, (src, w) in enumerate(parts):
                    for m in range(FK):
                        for q in range(2):
                            ins = pe.matmul(ps[0:slots, bank + q, :], src[:, m, :], w[:, m, q * 512:(q + 1) * 512],
                                            start=(n == 0 and m == 0), stop=(n == len(parts) - 1 and m == FK - 1))
                return ins

            def turn_gathered(it, s, first):
                e = it * RING + s
                b = s % 2
                pe.wait_ge(xg_in[b], 16 * (RING // 2 * it + s // 2 + 1))
                if not first or s >= 2:
                    pe.wait_ge(xt_out, e - 1)
                pe.sem_inc(waits_ended, 1)
                turn_rows(b, xg[b]).then_inc(xt_done, 1)

            def expand(it, s, first=False):
                e = it * RING + s
                b = s % 2
                pe.wait_ge(xt_out, e + 1)
                pe.wait_ge(w13_in[s], 32 * (it + 1))
                if not first or s >= 2:
                    pe.wait_ge(hT_made, e - 1)
                first_products(2 + b, w13[s], xt[b]).then_inc(h13_done, 1)

            def contract(it, s, first=False):
                e = it * RING + s
                b = s % 2
                pe.wait_ge(hT_made, e + 1)
                pe.wait_ge(w2_lo_made, FK * (e + 1))
                if not first or s >= 2:
                    pe.wait_ge(y_copied, e - 1)
                parts = ((hT_hi[b], w2_hi[b]), (hT_lo[b], w2_hi[b]), (hT_hi[b], w2_lo[s]))
                second_product(4 + 2 * b, parts).then_inc(y_done, 1)

            def pe_expert(it, s, first=False, last=False):
                expand(it, s, first)
                if s < RING - 1:
                    turn_gathered(it, s + 1, first)
                elif not last:
                    turn_gathered(it + 1, 0, False)
                if s >= 1:
                    contract(it, s - 1, first)
                elif not first:
                    contract(it - 1, RING - 1)
                else:
                    keep_warm(7, 5)

            pe.wait_ge(over_made, 1)
            pe.wait_ge(idx_in, 16)
            keep_warm(7, 16)
            turn_gathered(0, 0, True)
            for s in range(RING):
                pe_expert(0, s, first=True)
            with pe.Fori(1, NE // RING - 1) as it:
                for s in range(RING):
                    pe_expert(it, s)
            for s in range(RING):
                pe_expert(NE // RING - 1, s, last=True)
            contract(NE // RING - 1, RING - 1)

            tripped = pe.value_load(over[0:1, 0:1], min_val=0, max_val=1)
            with pe.If(tripped > 0):
                pe.wait_ge(y_copied, NE)
                with pe.Fori(0, NE) as e:
                    with pe.Fori(1, SEQ // slots) as c:
                        n = e * (SEQ // slots - 1) + c
                        pe.wait_ge(fb_xg, n * 16)
                        pe.sem_inc(waits_ended, 1)
                        turn_rows(0, xg[0]).then_inc(fb_xt, 1)
                        pe.wait_ge(fb_xt_out, n)
                        pe.wait_ge(fb_w, n * 48)
                        first_products(2, w13[0], xt[0]).then_inc(fb_h13, 1)
                        pe.wait_ge(fb_hT, n)
                        second_product(4, [(sil[0], w2s[0])]).then_inc(fb_y, 1)


_INS = ['x', 'meta_tokens', 'g_attn', 'w_in', 'b_f', 'g_fox_q', 'g_fox_k', 'g_q_lat', 'w_uq', 'g_kv_lat', 'w_ukv',
        'g_mla_q', 'g_mla_k', 'g_fox_out', 'g_mla_out', 'w_o', 'g_ffn', 'w_group', 'b_group', 'w_expert',
        'b_expert', 'w1', 'w3', 'w2']


def rope_table():
    import numpy as np
    inv = np.exp(-np.float32(np.log(10000.0)) * np.arange(HALF, dtype=np.float32) / np.float32(HALF))
    ang = np.arange(L, dtype=np.float32)[:, None] * inv.astype(np.float32)[None, :]
    by_pos = np.concatenate([np.cos(ang), np.sin(ang)], axis=1).astype(np.float32)
    return np.concatenate([by_pos[META:], by_pos[:META], np.zeros((P - META, ROPE), np.float32)])


def kernel(**inputs):
    import numpy as _np
    import concourse.bacc as _bacc
    from concourse import mybir as _mybir
    from concourse.bass_utils import run_bass_kernel_spmd as _run

    nc = _bacc.Bacc("TRN2", target_bir_lowering=False, num_devices=1)
    arrays, args = {}, {}
    for name in _INS:
        v = _np.ascontiguousarray(inputs[name])
        arrays[f"in_{name}"] = v
        args[name] = nc.dram_tensor(f"in_{name}", v.shape, _mybir.dt.from_np(v.dtype), kind="ExternalInput").ap()
    arrays["in_rope"] = rope_table()
    args["rope"] = nc.dram_tensor("in_rope", arrays["in_rope"].shape, F32, kind="ExternalInput").ap()
    out = nc.dram_tensor("out_0", (1, SEQ, D), F32, kind="ExternalOutput").ap()
    build(nc, args, out)
    r = _run(nc, [arrays], core_ids=[0])
    return r.results[0]["out_0"]
```
